# Optimizing a Trainium2 kernel written in Bass

```python
import math, functools
import jax, jax.numpy as jnp
from jax import lax
import numpy as np

D_MODEL = 1024
BATCH = 1
SEQ = 512
DEPTH = 1
DEC_BATCH = 8
DEC_SEQ = 1
PAST_LEN = 2048
PAGE_SIZE = 128

H_A = 8
N_A = 64
C_A = H_A * N_A
R_W = 64
R_A = 64
R_G = 128
C_SHIFT = 3 * C_A + R_W + R_A + R_G
LNX_EPS = 64e-5
H_Q = 8
H_KV = 2
GQA = H_Q // H_KV
HEAD_DIM = 64
WINDOW = 128
ROT_DIM = HEAD_DIM // 4
ROPE_THETA = 500000.0
N_MEM = 256
MEM_HEADS = 4
MEM_W = MEM_HEADS * HEAD_DIM
Q_W = H_Q * HEAD_DIM
KV_W = H_KV * HEAD_DIM
N_BRANCH = 3
SPLITS = [C_SHIFT, C_SHIFT + Q_W, C_SHIFT + Q_W + KV_W, C_SHIFT + Q_W + 2 * KV_W,
          C_SHIFT + Q_W + 2 * KV_W + MEM_W]
N_PROJ = SPLITS[-1] + N_BRANCH * D_MODEL
N_GROUPS = 4
EXPERTS_PER_GROUP = 8
N_EXPERTS = N_GROUPS * EXPERTS_PER_GROUP
TOP_K = 2
EXPERT_FF = 512
EXPERT_BLOCK = 128
ALPHA = (2.0 * DEPTH) ** 0.25
BETA = (8.0 * DEPTH) ** -0.25
LN_EPS = 1e-5
NEG_INF = -1e30

kernel_name = 'hybrid_rwkv7_swa_sink_memxattn_hmoe_deepnorm_step'

def layer_norm(x, g, b):
    xf = x.astype(jnp.float32)
    mu = jnp.mean(xf, axis=-1, keepdims=True)
    var = jnp.mean(jnp.square(xf - mu), axis=-1, keepdims=True)
    y = (xf - mu) * lax.rsqrt(var + LN_EPS) * g.astype(jnp.float32) + b.astype(jnp.float32)
    return y.astype(x.dtype)

def partial_rope(x, pos):
    half = ROT_DIM // 2
    inv_freq = ROPE_THETA ** (-jnp.arange(half, dtype=jnp.float32) / half)
    ang = pos[:, None] * inv_freq[None, :]
    cos = jnp.cos(ang)[:, None, :]
    sin = jnp.sin(ang)[:, None, :]
    xf = x.astype(jnp.float32)
    x1, x2 = xf[..., :half], xf[..., half:ROT_DIM]
    out = jnp.concatenate([x1 * cos - x2 * sin, x2 * cos + x1 * sin, xf[..., ROT_DIM:]], axis=-1)
    return out.astype(x.dtype)

def wkv_step(S, inp):
    r, w, k, v, a, b = inp
    sa = jnp.einsum('bhvk,bhk->bhv', S, a)
    S = S * w[:, :, None, :] + sa[..., None] * b[:, :, None, :] + v[..., None] * k[:, :, None, :]
    return S, jnp.einsum('bhvk,bhk->bhv', S, r)

def rwkv_time_mix(z, shift_prev, wkv0, p):
    B, T, _ = z.shape
    prev = jnp.concatenate([shift_prev[:, None, :].astype(z.dtype), z[:, :-1]], axis=1)
    zs = z + (prev - z) * p['mu']
    r, k, v, xw, xa, xg = jnp.split(zs, [C_A, 2 * C_A, 3 * C_A, 3 * C_A + R_W, 3 * C_A + R_W + R_A], axis=-1)
    w = -jax.nn.softplus(-(p['w0'] + jnp.tanh(xw) @ p['w_up'])) - 0.5
    decay = jnp.exp(-jnp.exp(w.astype(jnp.float32)))
    a = jax.nn.sigmoid(p['a0'] + xa @ p['a_up'])
    g = jax.nn.sigmoid(xg) @ p['g_up']
    hs = lambda t: t.astype(jnp.float32).reshape(B, T, H_A, N_A)
    kk = hs(k * p['k_k'])
    kk = kk / jnp.maximum(jnp.linalg.norm(kk, axis=-1, keepdims=True), 1e-12)
    k = k * (1.0 + (a - 1.0) * p['k_a'])
    rh, kh, vh, ah = hs(r), hs(k), hs(v), hs(a)
    tm = lambda t: jnp.moveaxis(t, 1, 0)
    xs_scan = (tm(rh), tm(hs(decay)), tm(kh), tm(vh), tm(-kk), tm(kk * ah))
    S_final, y = lax.scan(wkv_step, wkv0.astype(jnp.float32), xs_scan)
    y = jnp.moveaxis(y, 0, 1)
    mu_y = jnp.mean(y, axis=-1, keepdims=True)
    var_y = jnp.mean(jnp.square(y - mu_y), axis=-1, keepdims=True)
    y = ((y - mu_y) * lax.rsqrt(var_y + LNX_EPS)).reshape(B, T, C_A)
    y = y * p['lnx_g'].astype(jnp.float32) + p['lnx_b'].astype(jnp.float32)
    bonus = jnp.sum(rh * kh * p['r_k'].astype(jnp.float32), axis=-1, keepdims=True) * vh
    y = (y + bonus.reshape(B, T, C_A)).astype(z.dtype) * g
    return y, S_final, z[:, -1]

def sink_softmax(s, valid, sink):
    s = jnp.where(valid, s, NEG_INF)
    sink = jnp.broadcast_to(sink.astype(jnp.float32), s.shape[:-1] + (1,))
    return jax.nn.softmax(jnp.concatenate([s, sink], axis=-1), axis=-1)[..., :-1]

def swa_banded(q, k, v, sinks):
    B, T = q.shape[0], q.shape[1]
    nb = T // WINDOW
    qb = q.reshape(B, nb, WINDOW, H_KV, GQA, HEAD_DIM)
    kb = k.reshape(B, nb, WINDOW, H_KV, HEAD_DIM)
    vb = v.reshape(B, nb, WINDOW, H_KV, HEAD_DIM)
    shift = lambda t: jnp.concatenate([jnp.zeros_like(t[:, :1]), t[:, :-1]], axis=1)
    kw = jnp.concatenate([shift(kb), kb], axis=2)
    vw = jnp.concatenate([shift(vb), vb], axis=2)
    s = jnp.einsum('bnqhgd,bnkhd->bnhgqk', qb, kw).astype(jnp.float32) * (HEAD_DIM ** -0.5)
    qi = jnp.arange(WINDOW)[:, None] + WINDOW
    kj = jnp.arange(2 * WINDOW)[None, :]
    band = (kj <= qi) & (qi - kj < WINDOW)
    valid = band[None] & ((jnp.arange(nb) > 0)[:, None, None] | (kj >= WINDOW)[None])
    prob = sink_softmax(s, valid[None, :, None, None], sinks.reshape(H_KV, GQA)[None, None, :, :, None, None])
    o = jnp.einsum('bnhgqk,bnkhd->bnqhgd', prob.astype(v.dtype), vw).reshape(B, T, Q_W)
    return o, k[:, -WINDOW:], v[:, -WINDOW:]

def swa_cached(q, k, v, sinks, ck, cv):
    B, S = q.shape[0], q.shape[1]
    kk = jnp.concatenate([ck, k.astype(ck.dtype)], axis=1)
    vv = jnp.concatenate([cv, v.astype(cv.dtype)], axis=1)
    qb = q.reshape(B, S, H_KV, GQA, HEAD_DIM)
    s = jnp.einsum('bqhgd,bkhd->bhgqk', qb, kk).astype(jnp.float32) * (HEAD_DIM ** -0.5)
    qi = jnp.arange(S)[:, None] + WINDOW
    kj = jnp.arange(WINDOW + S)[None, :]
    valid = (kj <= qi) & (qi - kj < WINDOW)
    prob = sink_softmax(s, valid[None, None, None], sinks.reshape(H_KV, GQA)[None, :, :, None, None])
    o = jnp.einsum('bhgqk,bkhd->bqhgd', prob.astype(vv.dtype), vv).reshape(B, S, Q_W)
    return o, kk[:, -WINDOW:], vv[:, -WINDOW:]

def mem_attention(qm, mk, mv):
    B, T = qm.shape[0], qm.shape[1]
    s = jnp.einsum('bthd,bmhd->bhtm', qm, mk).astype(jnp.float32) * (HEAD_DIM ** -0.5)
    prob = jax.nn.softmax(s, axis=-1)
    return jnp.einsum('bhtm,bmhd->bthd', prob.astype(mv.dtype), mv).reshape(B, T, MEM_W)

def mixing_sublayer(x, pos0, shift_prev, wkv0, swa_fn, mem_k, mem_v, p):
    B, T, _ = x.shape
    z = x @ p['w_in']
    z_rwkv, q, k, v, qm, gates = jnp.split(z, SPLITS, axis=-1)
    o_a, wkv_new, shift_new = rwkv_time_mix(z_rwkv, shift_prev, wkv0, p)
    pos = pos0 + jnp.arange(T, dtype=jnp.float32)
    q = partial_rope(q.reshape(B, T, H_Q, HEAD_DIM), pos)
    k = partial_rope(k.reshape(B, T, H_KV, HEAD_DIM), pos)
    v = v.reshape(B, T, H_KV, HEAD_DIM)
    o_b, k_buf, v_buf = swa_fn(q, k, v, p['sinks'])
    o_m = mem_attention(qm.reshape(B, T, MEM_HEADS, HEAD_DIM), mem_k, mem_v)
    g = jax.nn.sigmoid(gates).reshape(B, T, N_BRANCH, D_MODEL)
    merged = (g[:, :, 0] * (o_a @ p['p_a']) + g[:, :, 1] * (o_b @ p['p_b'])
              + g[:, :, 2] * (o_m @ p['p_m']))
    return merged @ p['w_o'], wkv_new, shift_new, k_buf, v_buf

def routed_experts(xt, experts, gates, e_gate, e_up, e_down):
    n, D = xt.shape
    A = n * TOP_K
    flat_e = experts.reshape(A)
    flat_tok = jnp.arange(A, dtype=jnp.int32) // TOP_K
    flat_g = gates.reshape(A)
    order = jnp.argsort(flat_e)
    se = flat_e[order]
    counts = jnp.bincount(flat_e, length=N_EXPERTS)
    padded = (counts + EXPERT_BLOCK - 1) // EXPERT_BLOCK * EXPERT_BLOCK
    pad_end = jnp.cumsum(padded)
    pad_start = pad_end - padded
    start = jnp.cumsum(counts) - counts
    dest = pad_start[se] + jnp.arange(A, dtype=jnp.int32) - start[se]
    n_blocks = -(-A // EXPERT_BLOCK) + N_EXPERTS
    L = n_blocks * EXPERT_BLOCK
    row_tok = jnp.full((L,), n, jnp.int32).at[dest].set(flat_tok[order])
    row_gate = jnp.zeros((L,), xt.dtype).at[dest].set(flat_g[order])
    xs = jnp.concatenate([xt, jnp.zeros((1, D), xt.dtype)], axis=0)[row_tok]
    xs = xs.reshape(n_blocks, EXPERT_BLOCK, D)
    blk_e = jnp.minimum(jnp.searchsorted(pad_end, jnp.arange(n_blocks) * EXPERT_BLOCK, side='right'),
                        N_EXPERTS - 1)

    def expert_block(args):
        xb, e = args
        h = jax.nn.silu(xb @ e_gate[e]) * (xb @ e_up[e])
        return h @ e_down[e]

    ys = lax.map(expert_block, (xs, blk_e)).reshape(L, D)
    out = jnp.zeros((n + 1, D), xt.dtype).at[row_tok].add(ys * row_gate[:, None])
    return out[:n]

def hier_moe(x, w_group, b_group, w_router, b_router, e_gate, e_up, e_down):
    B, T, D = x.shape
    xt = x.reshape(B * T, D)
    n = B * T
    rows = jnp.arange(n)
    gl = (xt @ w_group).astype(jnp.float32) + b_group.astype(jnp.float32)
    g_idx = jnp.argmax(gl, axis=-1)
    g_w = jax.nn.softmax(gl, axis=-1)[rows, g_idx]
    el = ((xt @ w_router).astype(jnp.float32) + b_router.astype(jnp.float32))
    el = el.reshape(n, N_GROUPS, EXPERTS_PER_GROUP)[rows, g_idx]
    top_v, top_i = lax.top_k(el, TOP_K)
    gates = (g_w[:, None] * jax.nn.softmax(top_v, axis=-1)).astype(x.dtype)
    experts = (g_idx[:, None] * EXPERTS_PER_GROUP + top_i).astype(jnp.int32)
    y = routed_experts(xt, experts, gates, e_gate, e_up, e_down)
    return y.reshape(B, T, D)

def setup_inputs(seed: int = 0) -> dict:
    key = jax.random.key(seed)
    ks = iter(jax.random.split(key, 48))
    nrm = lambda shape, scale: jax.random.normal(next(ks), shape, jnp.float32) * scale
    L = DEPTH
    return {
        'x_prompt': nrm((BATCH, SEQ, D_MODEL), 1.0),
        'x_sample': nrm((DEC_BATCH, DEC_SEQ, D_MODEL), 1.0),
        'mem_prompt': nrm((BATCH, N_MEM, D_MODEL), 1.0),
        'state_wkv': nrm((L, DEC_BATCH, H_A, N_A, N_A), 0.3),
        'state_shift': nrm((L, DEC_BATCH, C_SHIFT), 1.0),
        'cache_win_k': nrm((L, DEC_BATCH, WINDOW, H_KV, HEAD_DIM), 1.0),
        'cache_win_v': nrm((L, DEC_BATCH, WINDOW, H_KV, HEAD_DIM), 1.0),
        'cache_mem_k': nrm((L, DEC_BATCH, N_MEM, MEM_HEADS, HEAD_DIM), 1.0),
        'cache_mem_v': nrm((L, DEC_BATCH, N_MEM, MEM_HEADS, HEAD_DIM), 1.0),
        'ln_in_g': 1.0 + nrm((D_MODEL,), 0.02),
        'ln_in_b': nrm((D_MODEL,), 0.02),
        'w_in': nrm((L, D_MODEL, N_PROJ), D_MODEL ** -0.5),
        'mu': jax.random.uniform(next(ks), (L, C_SHIFT), jnp.float32),
        'w0': jnp.linspace(-6.0, -1.0, C_A, dtype=jnp.float32)[None, :] + nrm((L, C_A), 0.1),
        'w_up': nrm((L, R_W, C_A), 0.1 * R_W ** -0.5),
        'a0': nrm((L, C_A), 0.1),
        'a_up': nrm((L, R_A, C_A), 0.5 * R_A ** -0.5),
        'g_up': nrm((L, R_G, C_A), R_G ** -0.5),
        'k_k': 0.85 + nrm((L, C_A), 0.05),
        'k_a': 1.0 + nrm((L, C_A), 0.05),
        'r_k': nrm((L, H_A, N_A), 0.1),
        'lnx_g': 1.0 + nrm((L, C_A), 0.02),
        'lnx_b': nrm((L, C_A), 0.02),
        'sinks': nrm((L, H_Q), 0.5),
        'w_mem_kv': nrm((L, D_MODEL, 2 * MEM_W), D_MODEL ** -0.5),
        'p_a': nrm((L, C_A, D_MODEL), C_A ** -0.5),
        'p_b': nrm((L, Q_W, D_MODEL), Q_W ** -0.5),
        'p_m': nrm((L, MEM_W, D_MODEL), MEM_W ** -0.5),
        'w_o': nrm((L, D_MODEL, D_MODEL), BETA * D_MODEL ** -0.5),
        'ln1_g': 1.0 + nrm((L, D_MODEL), 0.02),
        'ln1_b': nrm((L, D_MODEL), 0.02),
        'w_group': nrm((L, D_MODEL, N_GROUPS), D_MODEL ** -0.5),
        'b_group': nrm((L, N_GROUPS), 0.01),
        'w_router': nrm((L, D_MODEL, N_EXPERTS), D_MODEL ** -0.5),
        'b_router': nrm((L, N_EXPERTS), 0.01),
        'e_gate': nrm((L, N_EXPERTS, D_MODEL, EXPERT_FF), D_MODEL ** -0.5),
        'e_up': nrm((L, N_EXPERTS, D_MODEL, EXPERT_FF), D_MODEL ** -0.5),
        'e_down': nrm((L, N_EXPERTS, EXPERT_FF, D_MODEL), BETA * EXPERT_FF ** -0.5),
        'ln2_g': 1.0 + nrm((L, D_MODEL), 0.02),
        'ln2_b': nrm((L, D_MODEL), 0.02),
    }

def reference(x_prompt, x_sample, mem_prompt, state_wkv, state_shift, cache_win_k, cache_win_v,
              cache_mem_k, cache_mem_v, ln_in_g, ln_in_b, w_in, mu, w0, w_up, a0, a_up, g_up,
              k_k, k_a, r_k, lnx_g, lnx_b, sinks, w_mem_kv, p_a, p_b, p_m, w_o, ln1_g, ln1_b,
              w_group, b_group, w_router, b_router, e_gate, e_up, e_down, ln2_g, ln2_b):
    B = x_prompt.shape[0]
    xp = layer_norm(x_prompt, ln_in_g, ln_in_b)
    xs = layer_norm(x_sample, ln_in_g, ln_in_b)
    wkv_p_l, wkv_s_l, sh_p_l, sh_s_l = [], [], [], []
    kb_p_l, vb_p_l, kb_s_l, vb_s_l, mk_p_l, mv_p_l = [], [], [], [], [], []
    for l in range(DEPTH):
        p = dict(w_in=w_in[l], mu=mu[l], w0=w0[l], w_up=w_up[l], a0=a0[l], a_up=a_up[l],
                 g_up=g_up[l], k_k=k_k[l], k_a=k_a[l], r_k=r_k[l], lnx_g=lnx_g[l], lnx_b=lnx_b[l],
                 sinks=sinks[l], p_a=p_a[l], p_b=p_b[l], p_m=p_m[l], w_o=w_o[l])
        moe_w = (w_group[l], b_group[l], w_router[l], b_router[l], e_gate[l], e_up[l], e_down[l])
        mkv = mem_prompt @ w_mem_kv[l]
        mk_p = mkv[..., :MEM_W].reshape(B, N_MEM, MEM_HEADS, HEAD_DIM)
        mv_p = mkv[..., MEM_W:].reshape(B, N_MEM, MEM_HEADS, HEAD_DIM)
        hp, wkv_p, sh_p, kb_p, vb_p = mixing_sublayer(
            xp, 0.0, jnp.zeros((B, C_SHIFT), xp.dtype), jnp.zeros((B, H_A, N_A, N_A), jnp.float32),
            swa_banded, mk_p, mv_p, p)
        xp = layer_norm(ALPHA * xp + hp, ln1_g[l], ln1_b[l])
        xp = layer_norm(ALPHA * xp + hier_moe(xp, *moe_w), ln2_g[l], ln2_b[l])
        swa_s = functools.partial(swa_cached, ck=cache_win_k[l], cv=cache_win_v[l])
        hs, wkv_s, sh_s, kb_s, vb_s = mixing_sublayer(
            xs, float(PAST_LEN), state_shift[l], state_wkv[l], swa_s, cache_mem_k[l], cache_mem_v[l], p)
        xs = layer_norm(ALPHA * xs + hs, ln1_g[l], ln1_b[l])
        xs = layer_norm(ALPHA * xs + hier_moe(xs, *moe_w), ln2_g[l], ln2_b[l])
        wkv_p_l.append(wkv_p); wkv_s_l.append(wkv_s); sh_p_l.append(sh_p); sh_s_l.append(sh_s)
        kb_p_l.append(kb_p); vb_p_l.append(vb_p); kb_s_l.append(kb_s); vb_s_l.append(vb_s)
        mk_p_l.append(mk_p); mv_p_l.append(mv_p)
    sd = state_wkv.dtype
    return (xp, xs,
            jnp.stack(wkv_p_l).astype(sd), jnp.stack(wkv_s_l).astype(sd),
            jnp.stack(sh_p_l), jnp.stack(sh_s_l),
            jnp.stack(kb_p_l), jnp.stack(vb_p_l), jnp.stack(kb_s_l), jnp.stack(vb_s_l),
            jnp.stack(mk_p_l), jnp.stack(mv_p_l))


_drawn_inputs = setup_inputs


def setup_inputs(seed=0):
    import zlib

    import numpy as np

    out = dict(_drawn_inputs(seed))
    spreads = {}
    factors = {'w_up': 8.0,
     'lnx_g': 21.109,
     'lnx_b': 31.874,
     'sinks': 100.701,
     'b_group': 64.0,
     'b_router': 8.0,
     'ln2_g': 23.821,
     'ln2_b': 22.568,
     'cache_mem_k': 3.523,
     'cache_mem_v': 2.815,
     'r_k': 3.649,
     'p_b': 3.514}
    for name, (base, spread) in spreads.items():
        noise = np.random.default_rng([zlib.crc32(name.encode()), seed]).standard_normal(out[name].shape)
        drawn = base * np.exp(spread * noise) if base else spread * noise
        out[name] = __import__('jax').numpy.asarray(drawn.astype(out[name].dtype))
    for name, factor in factors.items():
        out[name] = (out[name] * factor).astype(out[name].dtype)
    return out
```

```python
import math
from contextlib import ExitStack

import numpy as np
import concourse.bass as bass
import concourse.mybir as mybir

F32 = mybir.dt.float32
I32 = mybir.dt.int32
U32 = mybir.dt.uint32
ALU = mybir.AluOpType
ACT = mybir.ActivationFunctionType
AX = mybir.AxisListType

P = 128
D = 1024
KD = D // P
T, B = 512, 8
N = T + B
NH = N // 2
NT = T // P
HA, C_A = 8, 512
NJ = C_A // P
CH = 64
C_SHIFT = 1792
SF = C_SHIFT // P
FQ, FK, FV, FM, NF = 14, 18, 19, 20, 22
GATE0 = NF * P
N_PROJ = 5888
WIN, NMEM = 128, 256
ALPHA = 2.0 ** 0.25
LN_EPS, LNX_EPS = 1e-5, 64e-5
DECAY = math.exp(-0.5)
NE, FF, NG, EPG = 32, 512, 4, 8
XB = 8
NB = NE + XB
BIG = 1e30
PAD_ROW = 5000.0


def const_table():
    parts, at, off = [], {}, 0

    def put(name, a):
        nonlocal off
        a = np.asarray(a, np.float32)
        full = np.zeros((P, a.shape[1]), np.float32)
        full[:a.shape[0]] = a
        parts.append(full)
        at[name] = (off, a.shape[1])
        off += a.shape[1]

    r = np.arange(P)[:, None]
    c = np.arange(P)[None, :]
    same = (r // CH) == (c // CH)
    put("ident", np.eye(P))
    put("upper2", np.concatenate([same & (r < c), same & (r <= c)], 1))
    put("low1", (r // 2 == c // 2) & (r > c))
    put("up1", (r // 2 == c // 2) & (r < c))
    for k in range(1, 6):
        b = 2 ** k
        put(f"level{k}", (r // (2 * b) == c // (2 * b)) & (r // b == c // b + 1))
    kj = np.arange(2 * P)[None, :]
    band = (kj <= r + P) & (r + P - kj < WIN)
    put("mask0", np.where(band & (kj >= P), 0.0, -BIG))
    put("mask", np.where(band, 0.0, -BIG))
    half = 8
    inv = 500000.0 ** (-np.arange(half, dtype=np.float32) / half)
    pos = np.concatenate([np.arange(T), np.full(B, 2048)]).astype(np.float32)
    ang = (pos[:, None] * inv[None, :].astype(np.float32)).astype(np.float32)
    cos, sin = np.ones((P, N)), np.zeros((P, N))
    rot = np.zeros((P, P))
    for h in range(2):
        for i in range(half):
            for base, sign, other in ((0, -1.0, half), (half, 1.0, 0)):
                f = h * 64 + base + i
                cos[f] = np.cos(ang[:, i])
                sin[f] = np.sin(ang[:, i])
                rot[h * 64 + other + i, f] = sign
    put("cos", cos)
    put("sin", sin)
    put("rot", rot)
    s8 = np.zeros((P, NJ, HA))
    for j in range(NJ):
        for p in range(P):
            s8[p, j, 2 * j + p // 64] = 1
    put("sel8", s8.reshape(P, -1))
    put("sel8t", np.transpose(s8, (2, 1, 0)).reshape(HA, -1))
    put("bones", (r // 64 == c // 64))
    put("before", r < c)
    put("ones", np.ones((P, P)))
    put("reset", np.tile((np.arange(T) % CH != 0)[None, :], (P, 1)))
    put("iota", np.tile(np.arange(P)[None, :], (P, 1)))
    put("eps", np.tile(np.array([[LN_EPS, LNX_EPS]]), (P, 1)))
    tok = np.arange(NT + 1)[None, :] * P + r
    put("valid", tok < N)
    put("tok1", tok + 1)
    put("asg1", np.stack([2 * tok + 1, 2 * tok + 2], 2).reshape(P, -1))
    return np.concatenate(parts, 1), at


CONST, CAT = const_table()
NCONST = CONST.shape[1]
PR_MU, PR_W0, PR_A0, PR_KK, PR_KA, PR_RK, PR_LG, PR_LB, PR_N = 0, 14, 18, 22, 26, 30, 34, 38, 42


SEMS = """
consts_in params_in x_in mem_in cache_in 
lora_in state_in samp_out samp_in ysamp_in out_in xback_in 
p1w0_in p1w1_in mgw0_in mgw1_in spilled x1_spilled out_done
ln_stats ln_std x_normed x_turned xT_ready mem_turned memT_ready mkv_made mkv_ready mkT_ready
z_made z_ready params_turned params_ready
shift_turned shift_ready v_ready rot_made kT_ready zeros_set kout_turned kout_ready
blk_kv blk_rot blk_q blk_scores blk_max blk_exp blk_prob blk_turned blk_pT_act blk_pT_dve blk_mixed blk_out
sk_turned sk_ready sk_scored sk_cols sk_rows sk_max sk_exp sk_prob sk_pT_made sk_pT_ready sk_mixed sk_done
zs_ready lora_act lora_mm lora_sig kk_sq head_sum head_root head_recip kk_bcast bonus_in bonus_mm prep_done
samp_stack samp_turned samp_rows samp_state ysamp_turned ysamp_ready
exps_made tile_ready tm_turned tm_ready tri_made tri_ready nk_ready lvl_t1 lvl_t1_ready lvl_x lvl_x_ready
nv_made nv_ready xav_made xav_ready gh_made gh_ready ry_made ry_ready chain_mm chain_done y_made y_ready
fstate_turned fstate_ready
gn_mean gn_center gn_sq gn_bcast oa_ready
gate_made gate_sig proj_made proj_used merged
h_made h_used x1_turned x1T_ready logits_made onehot_ready rank_made gexp_in gexp e2_in e2_out
route_ready table_made table_ready
xg_in_a xg_in_b xg_turned xgT_ready gate_mm up_mm gate_act h_ready hT_turned hT_ready y_mm yb_ready
ew0g_in ew0u_in ew0d_in ew1g_in ew1u_in ew1d_in scat_a scat_b
ovf_step pace yk_in 
""".split()


def build(nc, I, O, X):
    with ExitStack() as ctx:
        arena = ctx.enter_context(nc.sbuf_tensor("arena", [P, 53200], F32))
        psum = ctx.enter_context(nc.psum_tensor("psum", [P, 8, 512], F32))
        s = {n: ctx.enter_context(nc.semaphore(n)) for n in SEMS}

        def view(off, *dims):
            n = int(np.prod(dims))
            a = arena[:, off:off + n]
            if len(dims) == 1:
                return a
            names = "abcd"[:len(dims)]
            return a.rearrange("p (%s) -> p %s" % (" ".join(names), " ".join(names)),
                               **dict(zip(names[1:], dims[1:])))

        def bank(b, *dims, off=0):
            n = int(np.prod(dims))
            a = psum[:, :, :].rearrange("p a b -> p (a b)")[:, b * 512 + off:b * 512 + off + n]
            if len(dims) == 1:
                return a
            names = "abcd"[:len(dims)]
            return a.rearrange("p (%s) -> p %s" % (" ".join(names), " ".join(names)),
                               **dict(zip(names[1:], dims[1:])))

        def bc(ap, axis, n):
            a = ap.unsqueeze(axis)
            sh = list(a.shape)
            sh[axis] = n
            return a.to_broadcast(sh)

        off = [0]

        def take(n):
            o = off[0]
            off[0] += n
            return o

        C0 = take(NCONST)
        PRM = take(PR_N + 6)
        GBo = take(2 * D)
        SMo = take(800)
        XTo = take(KD * N)
        Zo = take(NF * N)
        ZSo = take(SF * N)
        KKo = take(NJ * N)
        BVo = take(NJ * N)
        LCo = take(NJ * T)
        YTo = take(NJ * N)
        Fo = off[0]
        FREE = 53200 - Fo
        assert FREE >= 14336, FREE

        def const(name, *dims):
            o, w = CAT[name]
            return view(C0 + o, *(dims or (w,)))

        consts = view(C0, NCONST)
        ident = const("ident")
        prm = view(PRM, PR_N)
        gb = view(GBo, 2, D)
        sm = [SMo]

        def small(*dims):
            o = sm[0]
            sm[0] += int(np.prod(dims))
            assert sm[0] <= SMo + 800
            return view(o, *dims)

        sink_bc = small(HA)
        sink_row = small(1)
        rb = small(NG + NE)
        st6 = small(NT + 1, 2, 6)
        mv = small(NT + 1, 2)
        rstd = small(NT + 1, 1)
        sstT = small(SF, B)
        mx, nmx, den, ske, rden = small(12), small(12), small(12), small(8), small(12)
        smx, snmx, sden, sske, srd = small(2), small(2), small(2), small(2), small(2)
        kTs = small(B)
        qsS = small(6, B)
        pc2 = small(2, NJ)
        wS = small(NJ, B)

        xT = view(XTo, KD, N)
        z = view(Zo, NF, N)
        zs = view(ZSo, SF, N)

        xtok = view(Fo, NT + 1, D)
        memtok = view(Fo + 5120, 2, D)
        memT = view(Fo + 7168, KD, NMEM)
        wmem = view(Fo + 9216, KD, 512)
        p1w = [view(YTo + q * 1024, KD, P) for q in range(2)]
        kT = view(BVo, P + T)
        vtok = view(BVo + 640, NT + 1, P)
        mkT = view(BVo + 1280, 2, NMEM)
        mkv = view(LCo, 2, 512)
        ktl = view(LCo + 1024, P)
        kss = view(LCo + 1152, P)
        vss = view(LCo + 1280, P)
        shb = view(KKo, C_SHIFT)
        prow = view(LCo + 1408, P)
        ssraw = view(ZSo, C_SHIFT)

        S = view(Fo, 12, 256)
        PT = view(Fo + 3072, 24, P)
        qs = view(Fo + 6144, 6, P)
        kst = view(Fo + 6912, 256)
        vst = view(Fo + 7168, 2, P)
        mst = view(Fo + 7424, 256)
        tmpq = view(Fo + 7680, NJ, P)
        kwin = view(Fo, B, P)
        vwin = view(Fo + 1024, B, P)
        kmem = view(Fo + 2048, B, 2, 256)
        vmem = view(Fo + 6144, B, 2, 256)
        kTb = [view(Fo + 10240 + q * 640, 5, P) for q in range(2)]
        sST = view(Fo + 11520, P)
        sW = view(Fo + 11648, P)
        sM = view(Fo + 11776, 2, P)
        sWT = view(Fo + 12032, 64)
        sMT = view(Fo + 12096, 2, 32)

        sg = view(Zo, NJ, N)
        ah = view(Zo + 2080, NJ, N)
        gT = view(Zo + 4160, NJ, N)
        th = view(Zo + 6240, N)
        kk = view(KKo, NJ, N)
        BV = view(BVo, NJ, N)
        Lc = view(LCo, NJ, T)
        YT = view(YTo, NJ, N)
        rT, kTr, vT = zs[:, 0:4, :], zs[:, 4:8, :], zs[:, 8:12, :]
        xwa, xg_ = zs[:, 12, :], zs[:, 13, :]
        wup = view(Fo, C_A)
        gup = view(Fo + 512, C_A)
        sqb = view(Fo + 1024, NJ, N)
        rn = view(Fo + 3104, N)
        sS = view(Fo + 3640, 32, 64)
        sTmp = view(Fo + 5688, 32, 64)
        vec = view(Fo + 7736, 6, 64)
        vvh = view(Fo + 8120, 32)
        sa = view(Fo + 8152, 32)
        sy = view(Fo + 8184, 32)
        sstk = view(Fo + 8216, 6, NJ, B)
        srow = view(Fo + 8408, 6, C_A)
        yrow = view(Fo + 11480, C_A)
        o = [Fo]

        def F(*dims):
            v = view(o[0], *dims)
            o[0] += int(np.prod(dims))
            assert o[0] <= 53200
            return v

        Pexc, Pinc, Pinv = F(NJ, P), F(NJ, P), F(NJ, P)
        AR = F(NJ, 2, P)
        Bt, Kt, Vt = F(NJ, P), F(NJ, P), F(NJ, P)
        Btok, Ktok, Vtok = F(C_A), F(C_A), F(C_A)
        ANV = F(HA, 2, 64)
        MR, NR = F(HA, 2, P), F(HA, 2, P)
        XX = F(HA, 2, P)
        GT, Hm = F(2, NJ, 64), F(2, NJ, 64)
        T1 = view(Fo, HA, P)
        Rh = view(Fo + 1024, NJ, P)
        XAV = view(Fo + 2560, HA, 2, 64)
        Yl = view(Fo + 3584, NJ, P)
        SR = view(ZSo + 12 * N, 3, NJ, 64)
        fst = view(Fo, HA, 64)

        MGW = 34 * P
        mgw = [view(Fo + q * MGW, 34, P) for q in range(2)]
        gsig = [view(ZSo + 4160 + q * N, N) for q in range(2)]
        ptmp = view(ZSo + 4160 + 2 * N, N)
        MG = view(ZSo, KD, N)
        wo = [view(Fo + 2 * MGW, KD, 512), view(KKo, KD, 512)]
        wr = view(Fo + 2 * MGW + 4096, KD, NG + NE)
        x1 = view(Zo, NT + 1, D)
        x1T = xT
        R0 = [ZSo]

        def R(*dims):
            v = view(R0[0], *dims)
            R0[0] += int(np.prod(dims))
            assert R0[0] <= ZSo + SF * N
            return v

        T5 = NT + 1
        LG = R(T5, NG + NE)
        g1 = R(T5, 1)
        eq4, c4, oh4, t4 = R(T5, NG), R(T5, NG), R(T5, NG), R(T5, NG)
        i1 = R(T5, 1)
        gd, gw = R(T5, 1), R(T5, 1)
        el = R(T5, NE)
        eqx, cx = R(T5, NE), R(T5, NE)
        v1, v2 = R(T5, 1), R(T5, 1)
        OH = R(2, T5, NE)
        Osum, rank, qb, blk = R(T5, NE), R(T5, NE), R(T5, NE), R(T5, NE)
        cnt, nx, incl, osx, dov = R(NE), R(NE), R(NE), R(NE), R(NE)
        bk, sk = R(2, T5, 1), R(2, T5, 1)
        SK = R(2, T5, P)
        VB = R(T5, 2, 2, NB)
        tabf = R(2, NB)
        tadd = R(2, NB)
        xe = R(XB, NE)
        xe2 = R(XB, NE)
        pgate = small(2, T5, 1)
        tabi = small(2, NB)
        ovf, ovfi = small(XB + 1), small(XB + 1)
        e2, rden2 = small(T5, 1), small(T5, 1)
        idx = small(2, 2)

        EW = 12288
        E0 = Zo + 5120
        yk = view(E0 + 640, T5, 2, D)
        ewb = [E0 + 1088, E0 + 1088 + EW]
        M0 = [ewb[1] + EW]

        def M(*dims):
            v = view(M0[0], *dims)
            M0[0] += int(np.prod(dims))
            assert M0[0] <= 53200, M0[0]
            return v

        eg = [view(b, KD, FF) for b in ewb]
        eu = [view(b + 4096, KD, FF) for b in ewb]
        ed = [view(b + 8192, FF // P, D) for b in ewb]
        m0 = [XTo]

        def M1(*dims):
            v = view(m0[0], *dims)
            m0[0] += int(np.prod(dims))
            assert m0[0] <= XTo + KD * N
            return v

        xg = [M1(D), M1(D)]
        xgT = M1(KD, P)
        hb, hT = M1(FF), M1(FF // P, P)
        esig = M(FF)
        yb = [M(D), M(D)]

        block = ctx.enter_context(nc.Block())
        Q = NT + 1

        def rows(t):
            return P if t < NT else B

        def extra_blocks(eng, body):
            n = eng.value_load(ovfi.bitcast(I32)[0:1, XB:XB + 1], min_val=0, max_val=XB)
            with eng.If(n > 0):
                with eng.Fori(0, n) as i:
                    body(i)

        @block.sync
        def _(sp):
            sp.dma_start(consts, I["consts"]).then_inc(s["consts_in"], 16)
            sp.dma_start(xtok[:, 0:NT, :], I["x_prompt"].rearrange("(t p) d -> p t d", p=P)).then_inc(s["x_in"], 16)
            sp.dma_start(xtok[0:B, NT, :], I["x_sample"]).then_inc(s["x_in"], 16)
            sp.dma_start(gb[:, 0, :], I["ln_in_g"].partition_broadcast(P)).then_inc(s["x_in"], 16)
            sp.dma_start(gb[:, 1, :], I["ln_in_b"].partition_broadcast(P)).then_inc(s["x_in"], 16)
            sp.dma_start(memtok, I["mem_prompt"].rearrange("(t p) d -> p t d", p=P)).then_inc(s["mem_in"], 16)
            sp.dma_start(wmem, I["w_mem_kv"].rearrange("(p c) n -> p c n", c=KD)).then_inc(s["mem_in"], 16)
            sp.dma_start(prow[0:PR_N, :], I["params"]).then_inc(s["params_in"], 16)
            sp.dma_start(ssraw[0:B, :], I["state_shift"]).then_inc(s["params_in"], 16)
            sp.dma_start(sink_bc, I["sinks_bc"]).then_inc(s["params_in"], 16)
            sp.dma_start(sink_row[0:64, :], I["sinks_row"]).then_inc(s["params_in"], 16)
            sp.dma_start(rb, I["router_b"]).then_inc(s["params_in"], 16)

            w_in = I["w_in"].rearrange("(p c) n -> p c n", c=KD)

            def p1_load(q, need, src_a, src_b, dst_a, dst_b):
                sp.wait_ge(s["z_made"], need)
                sp.dma_start(dst_a, src_a).then_inc(s[f"p1w{q}_in"], 16)
                sp.dma_start(dst_b, src_b).then_inc(s[f"p1w{q}_in"], 16)

            def p1_tile(f, q, need):
                cols = bass.ds(f * P, P)
                p1_load(q, need, w_in[:, 0:4, cols], w_in[:, 4:8, cols], p1w[q][:, 0:4, :], p1w[q][:, 4:8, :])

            with sp.Fori(0, FQ // 2) as i:
                for q in range(2):
                    p1_tile(i * 2 + q, q, i * 2 + q + 1)
            for j in range(4):
                c0 = FQ * P + j * 64
                p1_load(j % 2, FQ + j + 1, w_in[:, :, c0:c0 + 64], w_in[:, :, c0 + 256:c0 + 320],
                        p1w[j % 2][:, :, 0:64], p1w[j % 2][:, :, 64:128])
            for f in range(FK, NF):
                p1_tile(f, f % 2, f + 1)

            for t in range(Q):
                sp.wait_ge(s["x_normed"], t + 1)
                sp.dma_start(X["x0"][t * P:t * P + rows(t), :], xtok[0:rows(t), t, :]).then_inc(s["spilled"], 16)
            for t in range(2):
                sp.wait_ge(s["mkv_ready"], t + 1)
                sp.dma_start(O["mem_k_prompt"][t * P:(t + 1) * P, :], mkv[:, t, 0:256]).then_inc(s["out_done"], 16)
                sp.dma_start(O["mem_v_prompt"][t * P:(t + 1) * P, :], mkv[:, t, 256:512]).then_inc(s["out_done"], 16)
            sp.wait_ge(s["shift_ready"], 1)
            sp.dma_start(O["shift_prompt"], shb[0:1, :]).then_inc(s["out_done"], 16)
            sp.dma_start(O["shift_sample"], shb[1:1 + B, :]).then_inc(s["out_done"], 16)
            sp.wait_ge(s["kout_ready"], 1)
            sp.wait_ge(s["v_ready"], 1)
            sp.dma_start(O["win_k_prompt"], ktl).then_inc(s["out_done"], 16)
            sp.dma_start(O["win_v_prompt"], vtok[:, NT, :]).then_inc(s["out_done"], 16)

            sp.wait_ge(s["blk_out"], NT + 1)
            sp.wait_ge(s["blk_kv"], NT + 1)
            sp.dma_start(kwin[0:P - 1, :, :], I["cache_win_k"][:, 1:, :].rearrange("b w f -> w b f")).then_inc(s["cache_in"], 16)
            sp.dma_start(vwin[0:P - 1, :, :], I["cache_win_v"][:, 1:, :].rearrange("b w f -> w b f")).then_inc(s["cache_in"], 16)
            sp.dma_start(kwin[P - 1:P, :, :], kss[0:B, :]).then_inc(s["cache_in"], 16)
            sp.dma_start(vwin[P - 1:P, :, :], vss[0:B, :]).then_inc(s["cache_in"], 16)
            sp.dma_start(kmem, I["cache_mem_k"].rearrange("b (t p) f -> p b t f", p=P)).then_inc(s["cache_in"], 16)
            sp.dma_start(vmem, I["cache_mem_v"].rearrange("b (t p) f -> p b t f", p=P)).then_inc(s["cache_in"], 16)
            sp.wait_ge(s["cache_in"], 96)
            sp.dma_start(O["win_k_sample"].rearrange("b w f -> w b f"), kwin).then_inc(s["out_done"], 16)
            sp.dma_start(O["win_v_sample"].rearrange("b w f -> w b f"), vwin).then_inc(s["out_done"], 16)

            sp.wait_ge(s["sk_done"], 1)
            sp.wait_ge(s["out_done"], 16 * 10)
            sp.dma_start(wup[0:64, :], I["w_up"]).then_inc(s["lora_in"], 16)
            sp.dma_start(wup[64:128, :], I["a_up"]).then_inc(s["lora_in"], 16)
            sp.dma_start(gup, I["g_up"]).then_inc(s["lora_in"], 16)
            for h in range(2):
                sp.dma_start(sS[h * 64:h * 64 + 64, :, :],
                             I["state_wkv"][:, h * 32:h * 32 + 32, :]).then_inc(s["state_in"], 16)
            sp.wait_ge(s["samp_rows"], 1)
            sp.dma_start(X["sv"].rearrange("q b f -> b q f"), srow[0:B, :, :]).then_inc(s["samp_out"], 16)
            sp.wait_ge(s["samp_out"], 16)
            svv = X["sv"].rearrange("q b (h k) -> (b h) q k", k=64)
            for h in range(2):
                sp.dma_start(vec[h * 64:h * 64 + 64, :, :], svv).then_inc(s["samp_in"], 16)
                sp.dma_start(vvh[h * 64:h * 64 + 64, :], svv[:, 3, h * 32:h * 32 + 32]).then_inc(s["samp_in"], 16)
            sp.wait_ge(s["samp_state"], 1)
            for h in range(2):
                sp.dma_start(O["wkv_sample"][:, h * 32:h * 32 + 32, :], sS[h * 64:h * 64 + 64, :, :]).then_inc(s["out_done"], 16)
                sp.dma_start(X["sy"][:, h * 32:h * 32 + 32], sy[h * 64:h * 64 + 64, :]).then_inc(s["samp_out"], 16)
            sp.wait_ge(s["samp_out"], 48)
            sp.dma_start(yrow[0:B, :], X["sy"].rearrange("(b h) v -> b (h v)", b=B)).then_inc(s["ysamp_in"], 16)
            sp.wait_ge(s["fstate_ready"], 1)
            sp.dma_start(O["wkv_prompt"].rearrange("h v k -> v h k"), fst[0:64, :, :]).then_inc(s["out_done"], 16)

            sp.wait_ge(s["oa_ready"], 1)
            sp.wait_ge(s["out_done"], 16 * 13)
            pa = I["p_a"].rearrange("(c p) n -> p c n", p=P)
            pm = I["p_m"].rearrange("(c p) n -> p c n", p=P)
            pbv = I["p_b"].rearrange("(e j p) n -> e p j n", e=2, p=64)
            with sp.Fori(0, KD // 2) as i:
                for q in range(2):
                    sp.wait_ge(s["merged"], i * 2 + q + 1)
                    for g in range(3):
                        sp.dma_start(mgw[q][:, g * KD:(g + 1) * KD, :],
                                     w_in[:, :, bass.ds(i * (2 * P) + (GATE0 + g * D + q * P), P)]).then_inc(s[f"mgw{q}_in"], 16)
                    cols = bass.ds(i * (2 * P) + q * P, P)
                    sp.dma_start(mgw[q][:, 24:28, :], pa[:, :, cols]).then_inc(s[f"mgw{q}_in"], 16)
                    for e in range(2):
                        sp.dma_start(mgw[q][e * 64:e * 64 + 64, 28:32, :], pbv[e, :, :, cols]).then_inc(s[f"mgw{q}_in"], 16)
                    sp.dma_start(mgw[q][:, 32:34, :], pm[:, :, cols]).then_inc(s[f"mgw{q}_in"], 16)
            wov = I["w_o"].rearrange("(c p) n -> p c n", p=P)
            for h in range(2):
                sp.dma_start(wo[h], wov[:, :, h * 512:h * 512 + 512]).then_inc(s["out_in"], 16)
            sp.dma_start(wr, I["router_w"].rearrange("(p c) n -> p c n", c=KD)).then_inc(s["out_in"], 16)
            sp.dma_start(gb[:, 0, :], I["ln1_g"].partition_broadcast(P)).then_inc(s["out_in"], 16)
            sp.dma_start(gb[:, 1, :], I["ln1_b"].partition_broadcast(P)).then_inc(s["out_in"], 16)
            sp.wait_ge(s["merged"], KD + 2)
            sp.wait_ge(s["spilled"], 16 * Q)
            sp.dma_start(x1[:, 0:NT, :], X["x0"][0:T, :].rearrange("(t p) d -> p t d", p=P)).then_inc(s["xback_in"], 16)
            sp.dma_start(x1[0:B, NT, :], X["x0"][T:N, :]).then_inc(s["xback_in"], 16)
            for t in range(Q):
                sp.wait_ge(s["x_normed"], Q + t + 1)
                sp.dma_start(X["x1"][t * P:t * P + rows(t), :], x1[0:rows(t), t, :]).then_inc(s["x1_spilled"], 16)
            sp.wait_ge(s["x_normed"], 2 * Q)
            sp.dma_start(gb[:, 0, :], I["ln2_g"].partition_broadcast(P)).then_inc(s["yk_in"], 16)
            sp.dma_start(gb[:, 1, :], I["ln2_b"].partition_broadcast(P)).then_inc(s["yk_in"], 16)

            sp.wait_ge(s["table_ready"], 1)
            wg = I["e_gate"].rearrange("e (p c) n -> e p c n", c=KD)
            wu = I["e_up"].rearrange("e (p c) n -> e p c n", c=KD)
            wd = I["e_down"].rearrange("e (p c) n -> e p c n", c=FF // P)
            def expert_load(e):
                return [w[bass.ds(e, 1)].rearrange("e p c n -> (e p) c n") for w in (wg, wu, wd)]

            def extra_load(i):
                e = sp.value_load(ovfi.bitcast(I32)[0:1, bass.ds(i, 1)], min_val=0, max_val=NE - 1)
                sp.wait_ge(s["y_mm"], i + (NE + 2))
                for w, dst, what in zip(expert_load(e), (eg[0], eu[0], ed[0]), "gud"):
                    sp.dma_start(dst, w).then_inc(s[f"ew0{what}_in"], 16)

            with sp.Fori(0, NE // 2) as i:
                for q in range(2):
                    e = i * 2 + q
                    sp.wait_ge(s["gate_mm"], e + 1)
                    sp.dma_start(eg[q], wg[bass.ds(e, 1)].rearrange("e p c n -> (e p) c n")).then_inc(s[f"ew{q}g_in"], 16)
                    sp.wait_ge(s["up_mm"], e + 1)
                    sp.dma_start(eu[q], wu[bass.ds(e, 1)].rearrange("e p c n -> (e p) c n")).then_inc(s[f"ew{q}u_in"], 16)
                    sp.wait_ge(s["y_mm"], e + 1)
                    sp.dma_start(ed[q], wd[bass.ds(e, 1)].rearrange("e p c n -> (e p) c n")).then_inc(s[f"ew{q}d_in"], 16)
            extra_blocks(sp, extra_load)
            sp.wait_ge(s["ovf_step"], 1)
            ya = X["ya"].rearrange("(t k) d -> t k d", k=2)
            for t in range(Q):
                sp.dma_start(yk[0:rows(t), t, :, :], ya[t * P:t * P + rows(t), :, :]).then_inc(s["yk_in"], 16)
            sp.wait_ge(s["x_normed"], 3 * Q)
            sp.dma_start(O["y_prompt"].rearrange("(t p) d -> p t d", p=P), x1[:, 0:NT, :]).then_inc(s["out_done"], 16)
            sp.dma_start(O["y_sample"], x1[0:B, NT, :]).then_inc(s["out_done"], 16)
            sp.wait_ge(s["out_done"], 16 * 15)
            sp.wait_ge(s["x1_spilled"], 16 * Q)

        @block.tensor
        def _(pe):
            def mm(out, a, b, start=True, stop=True):
                return pe.matmul(out, a, b, start=start, stop=stop)

            def turn(out, a):
                n = a.shape[0]
                b = a.start_partition() if n < P else 0
                return pe.transpose(out, a, ident[b:b + n, b:b + n])

            pe.wait_ge(s["consts_in"], 16)
            for t in range(Q):
                n = rows(t)
                pe.wait_ge(s["x_normed"], t + 1)
                if t >= 2:
                    pe.wait_ge(s["xT_ready"], t - 1)
                for c in range(KD):
                    last = turn(bank(2 * (t % 2), KD, P)[:, c, 0:n], xtok[0:n, t, c::KD])
                last.then_inc(s["x_turned"], 1)
            pe.wait_ge(s["mem_in"], 32)
            for t in range(2):
                for c in range(KD):
                    last = turn(bank(4 + 2 * t, KD, P)[:, c, :], memtok[:, t, c::KD])
                last.then_inc(s["mem_turned"], 1)
            pe.wait_ge(s["memT_ready"], 2)
            for t in range(2):
                for c in range(KD):
                    last = mm(bank(4 + t, 512), memT[:, c, t * P:(t + 1) * P], wmem[:, c, :], c == 0, c == KD - 1)
                last.then_inc(s["mkv_made"], 1)
            pe.wait_ge(s["mkv_ready"], 2)
            for f in range(2):
                for t in range(2):
                    last = turn(bank(6, 2, NMEM)[:, f, t * P:(t + 1) * P], mkv[:, t, f * P:(f + 1) * P])
            last.then_inc(s["mkv_made"], 1)
            pe.sem_inc(s["z_made"], 2)
            pe.wait_ge(s["xT_ready"], Q)
            with pe.Fori(0, NF // 2) as i:
                for q in range(2):
                    pe.wait_ge(s[f"p1w{q}_in"], i * 32 + 32)
                    pe.wait_ge(s["z_ready"], i * 2 + q + 1)
                    for h in range(2):
                        for c in range(KD):
                            last = mm(bank(2 * q + h, NH), p1w[q][:, c, :], xT[:, c, h * NH:(h + 1) * NH], c == 0, c == KD - 1)
                    last.then_inc(s["z_made"], 1)
            pe.wait_ge(s["z_ready"], NF + 2)
            pe.wait_ge(s["mkT_ready"], 1)
            pe.wait_ge(s["params_in"], 80)
            turn(bank(7, PR_N), prow[0:PR_N, :]).then_inc(s["params_turned"], 1)
            for f in range(SF):
                last = turn(bank(0, C_SHIFT)[0:9, f * P:(f + 1) * P], z[:, f, T - 1:N])
            for f in range(SF):
                last = turn(bank(4, SF, B)[:, f, :], ssraw[0:B, f * P:(f + 1) * P])
            for t in range(NT):
                last = turn(bank(5, NT, P)[:, t, :], z[:, FV, t * P:(t + 1) * P])
            last = turn(bank(6, P)[0:B, :], z[:, FV, T:N])
            last.then_inc(s["shift_turned"], 1)
            pe.wait_ge(s["params_ready"], 1)
            pe.wait_ge(s["shift_ready"], 1)
            mm(bank(7, T), const("rot"), z[:, FK, 0:T])
            mm(bank(0, B), const("rot"), z[:, FK, T:N])
            mm(bank(1, NJ, B), const("rot"), z[:, FQ:FQ + NJ, T:N]).then_inc(s["rot_made"], 1)
            pe.wait_ge(s["kT_ready"], 1)
            turn(bank(2, P), kT[:, T:T + P])
            turn(bank(3, P)[0:B, :], kTs).then_inc(s["kout_turned"], 1)
            pe.wait_ge(s["kout_ready"], 1)
            pe.wait_ge(s["v_ready"], 1)

            with pe.Fori(0, NT) as i:
                pe.wait_ge(s["blk_out"], i + 1)
                mm(bank(6, NJ, P), const("rot"), z[:, FQ:FQ + NJ, bass.ds(i * P, P)]).then_inc(s["blk_rot"], 1)
                pe.wait_ge(s["blk_q"], i + 1)
                pe.wait_ge(s["blk_kv"], i + 1)
                for kv in range(2):
                    r = slice(kv * 64, kv * 64 + 64)
                    for j in range(NJ):
                        mm(bank(0, 12, 256)[:, kv * 4 + j, :], qs[r, j, :], kst[r, :])
                    for m in range(2):
                        last = mm(bank(0, 12, 256)[:, 8 + kv * 2 + m, :], qs[r, 4 + m, :], mkT[r, m, :])
                last.then_inc(s["blk_scores"], 1)
                pe.wait_ge(s["blk_prob"], i + 1)
                for g in range(24):
                    last = turn(bank(0, 24, P)[:, g, :], S[:, g // 2, (g % 2) * P:(g % 2) * P + P])
                last.then_inc(s["blk_turned"], 1)
                pe.wait_ge(s["blk_pT_act"], i + 1)
                pe.wait_ge(s["blk_pT_dve"], i + 1)
                for kv in range(2):
                    r = slice(kv * 64, kv * 64 + 64)
                    for j in range(NJ):
                        for k in range(2):
                            mm(bank(6, NJ, P)[r, j, :], vst[:, k, r], PT[:, (kv * 4 + j) * 2 + k, :], k == 0, k == 1)
                    for m in range(2):
                        for k in range(2):
                            last = mm(bank(7, 2, P)[r, m, :], mkv[:, k, 256 + (2 * m + kv) * 64:320 + (2 * m + kv) * 64],
                                      PT[:, (8 + kv * 2 + m) * 2 + k, :], k == 0, k == 1)
                last.then_inc(s["blk_mixed"], 1)
            pe.wait_ge(s["blk_out"], NT + 1)

            pe.wait_ge(s["cache_in"], 96)
            for b in range(B):
                if b >= 2:
                    pe.wait_ge(s["sk_ready"], b - 1)
                kp = bank(2 * (b % 2), 5, P)
                turn(kp[:, 0, :], kwin[:, b, :])
                for f in range(2):
                    for t in range(2):
                        last = turn(kp[:, 1 + 2 * f + t, :], kmem[:, b, t, f * P:(f + 1) * P])
                last.then_inc(s["sk_turned"], 1)
                pe.wait_ge(s["sk_ready"], b + 1)
                kt = kTb[b % 2]
                for kv in range(2):
                    r = slice(kv * 64, kv * 64 + 64)
                    mm(bank(4 + kv, B, NJ)[:, b, :], kt[r, 0, :], qsS[r, 0:4, b])
                    for f in range(2):
                        for t in range(2):
                            last = mm(bank(6 + kv, 2, B, 2)[:, t, b, f:f + 1], kt[r, 1 + 2 * f + t, :], qsS[r, 4 + f, b:b + 1])
                last.then_inc(s["sk_scored"], 1)
            pe.wait_ge(s["sk_cols"], 1)
            turn(bank(0, P)[0:64, :], sST[:, 0:64])
            for t in range(2):
                last = turn(bank(1, 2, P)[0:32, t, :], sST[:, 64 + 32 * t:96 + 32 * t])
            last.then_inc(s["sk_rows"], 1)
            pe.wait_ge(s["sk_prob"], 1)
            turn(bank(2, 64), sW[0:64, :])
            for t in range(2):
                last = turn(bank(3, 2, 32)[:, t, :], sM[0:32, t, :])
            last.then_inc(s["sk_pT_made"], 1)
            pe.wait_ge(s["sk_pT_ready"], 1)
            for b in range(B):
                for kv in range(2):
                    r = slice(kv * 64, kv * 64 + 64)
                    mm(bank(4, B, NJ)[r, b, :], vwin[:, b, r], sWT[:, kv * 32 + b * 4:kv * 32 + b * 4 + 4])
                    for f in range(2):
                        for t in range(2):
                            last = mm(bank(5, B, 2)[r, b, f:f + 1], vmem[:, b, t, (2 * f + kv) * 64:(2 * f + kv) * 64 + 64],
                                      sMT[:, t, kv * 16 + b * 2 + f:kv * 16 + b * 2 + f + 1], t == 0, t == 1)
            last.then_inc(s["sk_mixed"], 1)

            pe.wait_ge(s["sk_done"], 1)
            pe.wait_ge(s["lora_in"], 48)
            pe.wait_ge(s["lora_act"], 1)
            n = 0
            for what in range(3):
                for j in range(NJ):
                    if n >= 2:
                        pe.wait_ge(s["lora_sig"], n - 1)
                    for h in range(2):
                        cols = slice(h * NH, (h + 1) * NH)
                        a, b_ = [(wup[0:64, j * P:(j + 1) * P], th[0:64, cols]),
                                 (wup[64:128, j * P:(j + 1) * P], xwa[64:128, cols]),
                                 (gup[:, j * P:(j + 1) * P], xg_[:, cols])][what]
                        last = mm(bank(2 * (n % 2) + h, NH), a, b_)
                    last.then_inc(s["lora_mm"], 1)
                    n += 1
            pe.wait_ge(s["kk_sq"], 1)
            for h in range(2):
                for j in range(NJ):
                    last = mm(bank(4 + h, NH)[0:HA, :], const("sel8", NJ, HA)[:, j, :], sqb[:, j, h * NH:(h + 1) * NH], j == 0, j == 3)
            last.then_inc(s["head_sum"], 1)
            pe.wait_ge(s["head_recip"], 1)
            for j in range(NJ):
                if j >= 1:
                    pe.wait_ge(s["prep_done"], j)
                for h in range(2):
                    last = mm(bank(4 + h, NH), const("sel8t", NJ, P)[0:HA, j, :], rn[0:HA, h * NH:(h + 1) * NH])
                last.then_inc(s["kk_bcast"], 1)
            pe.wait_ge(s["bonus_in"], 1)
            for j in range(NJ):
                if j >= 1:
                    pe.wait_ge(s["prep_done"], NJ + j)
                for h in range(2):
                    last = mm(bank(6 + h, NH), const("bones"), sqb[:, j, h * NH:(h + 1) * NH])
                last.then_inc(s["bonus_mm"], 1)
            pe.wait_ge(s["samp_stack"], 2)
            pe.wait_ge(s["prep_done"], 2 * NJ)
            pe.wait_ge(s["lora_sig"], 12)
            for q in range(6):
                for j in range(NJ):
                    last = turn(bank(0, 6, C_A)[0:B, q, j * P:(j + 1) * P], sstk[:, q, j, :])
            last.then_inc(s["samp_turned"], 1)
            pe.wait_ge(s["ysamp_in"], 16)
            pe.wait_ge(s["samp_rows"], 1)
            for j in range(NJ):
                last = turn(bank(6, NJ, B)[:, j, :], yrow[0:B, j * P:(j + 1) * P])
            last.then_inc(s["ysamp_turned"], 1)
            pe.wait_ge(s["ysamp_ready"], 1)

            with pe.Fori(0, NT) as i:
                pe.wait_ge(s["tile_ready"], i + 1)
                pe.wait_ge(s["y_ready"], i + 1)
                for q, src in enumerate((AR[:, :, 0, :], Bt, Kt, Vt)):
                    for j in range(NJ):
                        last = turn(bank(q, NJ, P)[:, j, :], src[:, j, :])
                last.then_inc(s["tm_turned"], 1)
                for par in range(2):
                    r = slice(par * 64, par * 64 + 64)
                    for j in range(NJ):
                        last = mm(bank(4 + 2 * par, NJ, 2, P)[:, j, :, :], Bt[r, j, :], AR[r, j, :, :])
                last.then_inc(s["tri_made"], 1)
                pe.wait_ge(s["tm_ready"], i + 1)
                for par in range(2):
                    r = slice(par * 64, par * 64 + 64)
                    for j in range(NJ):
                        last = mm(bank(2 * par, NJ, 2, P)[:, j, :, :], Kt[r, j, :], AR[r, j, :, :])
                last.then_inc(s["tri_made"], 1)
                pe.wait_ge(s["tri_ready"], i * 2 + 1)
                for par in range(2):
                    r = slice(par * 64, par * 64 + 64)
                    for j in range(NJ):
                        last = mm(bank(4 + 2 * par, NJ, P)[:, j, :], AR[r, j, 0, :], Bt[r, j, :])
                last.then_inc(s["tri_made"], 1)
                pe.wait_ge(s["nk_ready"], i + 1)
                pe.wait_ge(s["tri_ready"], i * 2 + 2)
                for k in range(5):
                    for g in range(2):
                        if k:
                            pe.wait_ge(s["lvl_x_ready"], i * 10 + 2 * (k - 1) + g + 1)
                        for j in range(NJ):
                            last = mm(bank(g, NJ, P)[:, j, :], MR[:, g * 4 + j, 0, :], XX[:, g * 4 + j, 0, :])
                        last.then_inc(s["lvl_t1"], 1)
                    for g in range(2):
                        pe.wait_ge(s["lvl_t1_ready"], i * 10 + 2 * k + g + 1)
                        for j in range(NJ):
                            h = g * 4 + j
                            mm(bank(2 + g, NJ, P)[:, j, :], XX[:, h, 1, :], T1[:, h, :])
                            last = mm(bank(4 + g, NJ, P)[:, j, :], T1[:, h, :], XX[:, h, 1, :])
                        last.then_inc(s["lvl_x"], 1)
                pe.wait_ge(s["lvl_x_ready"], i * 10 + 10)
                for h in range(HA):
                    hd = (h % 4) * 2 + h // 4
                    last = mm(bank(6, HA, 64)[:, h, :], NR[:, h, 0, :], Vtok[:, hd * 64:hd * 64 + 64])
                last.then_inc(s["nv_made"], 1)
                pe.wait_ge(s["nv_ready"], i + 1)
                for h in range(HA):
                    last = mm(bank(0, HA, P)[:, h, :], XX[:, h, 1, :], ANV[:, h, :, :])
                last.then_inc(s["xav_made"], 1)
                pe.wait_ge(s["xav_ready"], i + 1)
                pe.sem_inc(s["pace"], 1)
                for c in range(2):
                    t_ = slice(c * 64, c * 64 + 64)
                    for h in range(HA):
                        j, par = h % 4, h // 4
                        hd = j * 2 + par
                        r = slice(par * 64, par * 64 + 64)
                        f = slice(hd * 64, hd * 64 + 64)
                        o_ = bank(4 + c, NJ, 2, 64)
                        mm(o_[r, j, 0, :], XAV[t_, h, 0, :], Btok[t_, f])
                        mm(o_[r, j, 1, :], Btok[t_, f], XAV[t_, h, 1, :], True, False)
                        last = mm(o_[r, j, 1, :], Ktok[t_, f], Vtok[t_, f], False, True)
                last.then_inc(s["gh_made"], 1)
                for h in range(HA):
                    j, par = h % 4, h // 4
                    hd = j * 2 + par
                    r = slice(par * 64, par * 64 + 64)
                    mm(bank(2, NJ, P)[r, j, :], XAV[:, h, 0, :], MR[:, h, 1, :])
                    mm(bank(3, NJ, P)[r, j, :], XAV[:, h, 1, :], MR[:, h, 1, :], True, False)
                    last = mm(bank(3, NJ, P)[r, j, :], Vtok[:, hd * 64:hd * 64 + 64], NR[:, h, 1, :], False, True)
                last.then_inc(s["ry_made"], 1)
                pe.wait_ge(s["gh_ready"], i + 1)
                for c in range(2):
                    pe.wait_ge(s["chain_done"], i * 2 + c + 1)
                    pe.sem_inc(s["pace"], 1)
                    for par in range(2):
                        r = slice(par * 64, par * 64 + 64)
                        for j in range(NJ):
                            last = mm(bank(6 + par, NJ, 64)[r, j, :], GT[r, c, j, :], SR[r, c, j, :])
                    last.then_inc(s["chain_mm"], 1)
                pe.wait_ge(s["ry_ready"], i + 1)
                pe.sem_inc(s["pace"], 1)
                for par in range(2):
                    r = slice(par * 64, par * 64 + 64)
                    for j in range(NJ):
                        for c in range(2):
                            last = mm(bank(par, NJ, P)[r, j, c * 64:c * 64 + 64], SR[r, c, j, :], Rh[r, j, c * 64:c * 64 + 64])
                last.then_inc(s["y_made"], 1)
            pe.wait_ge(s["y_ready"], NT + 1)
            pe.wait_ge(s["chain_done"], 2 * NT + 1)
            for j in range(NJ):
                last = turn(bank(2, NJ, P)[0:64, j, :], SR[:, 0, j, :])
            last.then_inc(s["fstate_turned"], 1)
            for j in range(NJ):
                if j >= 2:
                    pe.wait_ge(s["gn_center"], j - 1)
                for h in range(2):
                    last = mm(bank(4 + 2 * (j % 2) + h, NH), const("bones"), YT[:, j, h * NH:(h + 1) * NH])
                last.then_inc(s["gn_mean"], 1)
            pe.wait_ge(s["gn_sq"], 1)
            for h in range(2):
                for j in range(NJ):
                    last = mm(bank(h, NH)[0:HA, :], const("sel8", NJ, HA)[:, j, :], sqb[:, j, h * NH:(h + 1) * NH], j == 0, j == 3)
            last.then_inc(s["head_sum"], 1)
            pe.wait_ge(s["head_recip"], 2)
            for j in range(NJ):
                if j >= 1:
                    pe.wait_ge(s["gn_bcast"], NT + j)
                for h in range(2):
                    last = mm(bank(4 + h, NH), const("sel8t", NJ, P)[0:HA, j, :], rn[0:HA, h * NH:(h + 1) * NH])
                last.then_inc(s["gn_mean"], 1)
            pe.wait_ge(s["oa_ready"], 1)

            branch = [(24, 4, lambda c: YT[:, c, :]), (28, 4, lambda c: z[:, FQ + c, :]), (32, 2, lambda c: z[:, FM + c, :])]
            with pe.Fori(0, KD // 2) as i:
                for q in range(2):
                    pe.wait_ge(s[f"mgw{q}_in"], i * 112 + 112)
                    for g in range(3):
                        par = (q * 3 + g) % 2
                        step = q * 3 + g
                        pe.wait_ge(s["gate_sig"], i * 6 + step + 1)
                        for h in range(2):
                            for c in range(KD):
                                last = mm(bank(2 * par + h, NH), mgw[q][:, g * KD + c, :], xT[:, c, h * NH:(h + 1) * NH], c == 0, c == KD - 1)
                        last.then_inc(s["gate_made"], 1)
                        pe.wait_ge(s["proj_used"], i * 6 + step + 1)
                        w0, nk, act = branch[g]
                        for h in range(2):
                            for c in range(nk):
                                last = mm(bank(4 + 2 * par + h, NH), mgw[q][:, w0 + c, :], act(c)[:, h * NH:(h + 1) * NH], c == 0, c == nk - 1)
                        last.then_inc(s["proj_made"], 1)
            pe.wait_ge(s["merged"], KD + 2)
            pe.wait_ge(s["out_in"], 80)
            for t in range(Q):
                n = rows(t)
                if t >= 2:
                    pe.wait_ge(s["h_used"], t - 1)
                for h in range(2):
                    for c in range(KD):
                        last = mm(bank(2 * (t % 2) + h, 512)[0:n, :], MG[:, c, t * P:t * P + n], wo[h][:, c, :], c == 0, c == KD - 1)
                last.then_inc(s["h_made"], 1)
            pe.wait_ge(s["h_used"], Q)
            for t in range(Q):
                n = rows(t)
                pe.wait_ge(s["x_normed"], Q + t + 1)
                if t >= 2:
                    pe.wait_ge(s["x1T_ready"], t - 1)
                for c in range(KD):
                    last = turn(bank(4 + 2 * (t % 2), KD, P)[:, c, 0:n], x1[0:n, t, c::KD])
                last.then_inc(s["x1_turned"], 1)
            pe.wait_ge(s["x1T_ready"], Q)
            for t in range(Q):
                n = rows(t)
                for c in range(KD):
                    last = mm(bank(0, Q, NG + NE)[0:n, t, :], x1T[:, c, t * P:t * P + n], wr[:, c, :], c == 0, c == KD - 1)
            last.then_inc(s["logits_made"], 1)
            pe.wait_ge(s["onehot_ready"], 1)
            for t in range(Q):
                for u in range(t):
                    mm(bank(1, Q, NE)[:, t, :], const("ones"), Osum[:, u, :], u == 0, False)
                mm(bank(1, Q, NE)[:, t, :], const("before"), Osum[:, t, :], t == 0, True)
            for t in range(Q):
                last = mm(bank(2, NE), const("ones"), Osum[:, t, :], t == 0, t == Q - 1)
            last.then_inc(s["rank_made"], 1)
            pe.wait_ge(s["route_ready"], 1)
            for t in range(Q):
                for k in range(2):
                    last = mm(bank(3, 2, NB), SK[:, k, t, :], VB[:, t, k, :, :], t == 0 and k == 0, t == Q - 1 and k == 1)
            last.then_inc(s["table_made"], 1)
            pe.wait_ge(s["table_ready"], 1)
            pe.sem_inc(s["gate_mm"], 2)
            pe.sem_inc(s["up_mm"], 2)
            pe.sem_inc(s["y_mm"], 2)

            def turn_rows(q):
                for c in range(KD):
                    last = turn(bank(0, KD, P)[:, c, :], xg[q][:, c::KD])
                last.then_inc(s["xg_turned"], 1)

            def gate(q):
                for c in range(KD):
                    last = mm(bank(2, FF), xgT[:, c, :], eg[q][:, c, :], c == 0, c == KD - 1)
                last.then_inc(s["gate_mm"], 1)

            def up(q):
                for c in range(KD):
                    last = mm(bank(3, FF), xgT[:, c, :], eu[q][:, c, :], c == 0, c == KD - 1)
                last.then_inc(s["up_mm"], 1)

            def turn_h():
                for c in range(FF // P):
                    last = turn(bank(4, 4, P)[:, c, :], hb[:, c::4])
                last.then_inc(s["hT_turned"], 1)

            def down(q):
                for h in range(2):
                    for c in range(FF // P):
                        last = mm(bank(5 + h, 512), hT[:, c, :], ed[q][:, c, h * 512:h * 512 + 512], c == 0, c == 3)
                last.then_inc(s["y_mm"], 1)

            def block_rows(q, e, i):
                pe.wait_ge(s[f"xg_in_{'ab'[q]}"], i * 16 + 16)
                turn_rows(q)
                pe.wait_ge(s["xgT_ready"], e + 1)
                pe.wait_ge(s[f"ew{q}g_in"], i * 16 + 16)
                gate(q)
                pe.wait_ge(s[f"ew{q}u_in"], i * 16 + 16)
                up(q)
                pe.wait_ge(s["h_ready"], e + 1)
                turn_h()
                pe.wait_ge(s["hT_ready"], e + 1)
                pe.wait_ge(s[f"ew{q}d_in"], i * 16 + 16)
                pe.wait_ge(s["yb_ready"], e + 1)
                down(q)

            with pe.Fori(0, NE // 2) as i:
                for q in range(2):
                    block_rows(q, i * 2 + q, i)
            extra_blocks(pe, lambda i: block_rows(0, i + NE, i + NE // 2))

        @block.scalar
        def _(act):
            def copy(out, a):
                return act.activation(out, a, ACT.Copy)

            def root(count, out, a, bias, scale=1.0):
                return act.activation(out, a, ACT.Sqrt, bias=bias, scale=scale)

            eps = const("eps")
            act.wait_ge(s["consts_in"], 16)
            act.wait_ge(s["ln_stats"], 1)
            act.activation(rstd, mv[:, :, 1:2], ACT.Sqrt, bias=eps[:, 0:1]).then_inc(s["ln_std"], 1)
            for t in range(Q):
                n = rows(t)
                act.wait_ge(s["x_turned"], t + 1)
                copy(xT[:, :, t * P:t * P + n], bank(2 * (t % 2), KD, P)[:, :, 0:n]).then_inc(s["xT_ready"], 1)
            for t in range(2):
                act.wait_ge(s["mem_turned"], t + 1)
                copy(memT[:, :, t * P:(t + 1) * P], bank(4 + 2 * t, KD, P)).then_inc(s["memT_ready"], 1)
            for t in range(2):
                act.wait_ge(s["mkv_made"], t + 1)
                copy(mkv[:, t, :], bank(4 + t, 512)).then_inc(s["mkv_ready"], 1)
            act.wait_ge(s["mkv_made"], 3)
            copy(mkT, bank(6, 2, NMEM)).then_inc(s["mkT_ready"], 1)
            act.sem_inc(s["z_ready"], 2)
            with act.Fori(0, NF // 2) as i:
                for q in range(2):
                    act.wait_ge(s["z_made"], i * 2 + q + 3)
                    copy(z[:, bass.ds(i * 2 + q, 1), :].rearrange("p a (h n) -> p (a h) n", h=2),
                         psum[:, 2 * q:2 * q + 2, 0:NH]).then_inc(s["z_ready"], 1)
            act.wait_ge(s["params_turned"], 1)
            copy(prm, bank(7, PR_N)).then_inc(s["params_ready"], 1)
            act.wait_ge(s["shift_turned"], 1)
            copy(shb[0:9, :], bank(0, C_SHIFT)[0:9, :])
            copy(sstT, bank(4, SF, B)).then_inc(s["shift_ready"], 1)
            copy(vtok[:, 1:, :], bank(5, NT, P))
            copy(vss[0:B, :], bank(6, P)[0:B, :]).then_inc(s["v_ready"], 1)
            act.wait_ge(s["kout_turned"], 1)
            copy(ktl, bank(2, P))
            copy(kss[0:B, :], bank(3, P)[0:B, :]).then_inc(s["kout_ready"], 1)

            act.sem_inc(s["blk_out"], 1)
            with act.Fori(0, NT) as i:
                act.wait_ge(s["blk_max"], i + 1)
                for h in range(8):
                    act.activation(S[:, h, :], S[:, h, :], ACT.Exp, bias=nmx[:, h:h + 1], accum_out=den[:, h:h + 1])
                for h in range(8, 12):
                    act.activation(S[:, h, :], bank(0, 12, 256)[:, h, :], ACT.Exp, bias=nmx[:, h:h + 1], scale=0.125,
                                   accum_out=den[:, h:h + 1])
                act.activation(ske, ske, ACT.Exp).then_inc(s["blk_exp"], 1)
                act.wait_ge(s["blk_turned"], i + 1)
                copy(PT[:, 0:12, :], bank(0, 12, P)).then_inc(s["blk_pT_act"], 1)
                act.wait_ge(s["blk_mixed"], i + 1)
                cols = bass.ds(i * P, P)
                copy(z[:, FQ:FQ + NJ, cols], bank(6, NJ, P))
                copy(z[:, FM:FM + 2, cols], bank(7, 2, P)).then_inc(s["blk_out"], 1)

            for b in range(B):
                act.wait_ge(s["sk_turned"], b + 1)
                if b >= 2:
                    act.wait_ge(s["sk_scored"], b - 1)
                copy(kTb[b % 2], bank(2 * (b % 2), 5, P)).then_inc(s["sk_ready"], 1)
            act.wait_ge(s["sk_scored"], B)
            for kv in range(2):
                copy(sST[:, kv * 32:kv * 32 + 32], bank(4 + kv, 32))
                last = copy(sST[:, 64:128].rearrange("p (t k c) -> p t k c", t=2, k=2)[:, :, kv, :], bank(6 + kv, 2, 16))
            last.then_inc(s["sk_cols"], 1)
            act.wait_ge(s["sk_max"], 1)
            act.activation(sW[0:64, :], bank(0, P)[0:64, :], ACT.Exp, bias=snmx[0:64, 0:1], scale=0.125, accum_out=sden[0:64, 0:1])
            act.activation(sM[0:32, :, :], bank(1, 2, P)[0:32, :, :], ACT.Exp, bias=snmx[0:32, 1:2], scale=0.125,
                           accum_out=sden[0:32, 1:2])
            act.activation(sske[0:64, 0:1], sske[0:64, 0:1], ACT.Exp).then_inc(s["sk_exp"], 1)
            act.wait_ge(s["sk_pT_made"], 1)
            copy(sWT, bank(2, 64))
            copy(sMT, bank(3, 2, 32)).then_inc(s["sk_pT_ready"], 1)
            act.wait_ge(s["sk_mixed"], 1)
            copy(z[:, FQ:FQ + NJ, T:N], bank(4, B, NJ).rearrange("p b j -> p j b"))
            copy(z[:, FM:FM + 2, T:N], bank(5, B, 2).rearrange("p b j -> p j b")).then_inc(s["sk_done"], 1)

            act.wait_ge(s["zs_ready"], 1)
            act.activation(th[0:64, :], xwa[0:64, :], ACT.Tanh)
            act.activation(xg_, xg_, ACT.Sigmoid).then_inc(s["lora_act"], 1)
            n = 0
            for what in range(3):
                for j in range(NJ):
                    act.wait_ge(s["lora_mm"], n + 1)
                    src = psum[:, 2 * (n % 2):2 * (n % 2) + 2, 0:NH]
                    dst = (sg, ah, gT)[what][:, j, :].rearrange("p (h n) -> p h n", h=2)
                    if what < 2:
                        r0 = (PR_W0, PR_A0)[what] + j
                        last = act.activation(dst, src, ACT.Sigmoid, bias=prm[:, r0:r0 + 1])
                    else:
                        last = copy(dst, src)
                    last.then_inc(s["lora_sig"], 1)
                    n += 1
            for j in range(NJ):
                last = act.activation(sqb[:, j, :], kTr[:, j, :], ACT.Square, scale=prm[:, PR_KK + j:PR_KK + j + 1])
            last.then_inc(s["kk_sq"], 1)
            act.wait_ge(s["head_sum"], 1)
            act.activation(rn[0:HA, :].rearrange("p (h n) -> p h n", h=2), psum[0:HA, 4:6, 0:NH], ACT.Sqrt).then_inc(s["head_root"], 1)
            act.drain()
            act.activation(wS, sg[:, :, T:N], ACT.Exp, scale=-DECAY).then_inc(s["samp_stack"], 1)
            act.wait_ge(s["samp_turned"], 1)
            copy(srow[0:B, :, :], bank(0, 6, C_A)[0:B, :, :]).then_inc(s["samp_rows"], 1)
            act.wait_ge(s["ysamp_turned"], 1)
            copy(YT[:, :, T:N], bank(6, NJ, B)).then_inc(s["ysamp_ready"], 1)

            act.wait_ge(s["prep_done"], 2 * NJ + 1)
            with act.Fori(0, NT) as i:
                cols = bass.ds(i * P, P)
                act.wait_ge(s["y_ready"], i + 1)
                act.wait_ge(s["gn_bcast"], i + 1)
                act.activation(Pinc, Lc[:, :, cols], ACT.Exp, scale=-DECAY)
                act.activation(Pinv, Lc[:, :, cols], ACT.Exp, scale=DECAY)
                act.activation(Pexc, Pexc, ACT.Exp, scale=-DECAY).then_inc(s["exps_made"], 1)
                act.wait_ge(s["tm_turned"], i + 1)
                copy(ANV[:, :, 0, :].rearrange("p (e j) k -> p e j k", e=2),
                     bank(0, NJ, 2, 64).rearrange("p j e k -> p e j k"))
                copy(Btok, bank(1, 512))
                copy(Ktok, bank(2, 512))
                copy(Vtok, bank(3, 512)).then_inc(s["tm_ready"], 1)
                act.wait_ge(s["nv_made"], i + 1)
                copy(ANV[:, :, 1, :], bank(6, HA, 64)).then_inc(s["nv_ready"], 1)
                act.wait_ge(s["xav_made"], i + 1)
                copy(XAV, bank(0, HA, 2, 64)).then_inc(s["xav_ready"], 1)
                act.wait_ge(s["ry_made"], i + 1)
                copy(Yl, bank(3, NJ, P)).then_inc(s["ry_ready"], 1)
            act.wait_ge(s["fstate_turned"], 1)
            copy(fst[0:64, :, :], bank(2, HA, 64)[0:64, :, :]).then_inc(s["fstate_ready"], 1)
            act.wait_ge(s["gn_sq"], 1)
            act.wait_ge(s["head_sum"], 2)
            act.activation(rn[0:HA, :].rearrange("p (h n) -> p h n", h=2), psum[0:HA, 0:2, 0:NH], ACT.Sqrt,
                           scale=1.0 / 64, bias=eps[0:HA, 1:2]).then_inc(s["head_root"], 1)

            act.wait_ge(s["oa_ready"], 1)
            act.sem_inc(s["gate_sig"], 2)
            with act.Fori(0, KD // 2) as i:
                for step in range(6):
                    act.wait_ge(s["gate_made"], i * 6 + step + 1)
                    act.wait_ge(s["proj_used"], i * 6 + step + 1)
                    act.activation(gsig[step % 2].rearrange("p (h n) -> p h n", h=2),
                                   psum[:, 2 * (step % 2):2 * (step % 2) + 2, 0:NH], ACT.Sigmoid).then_inc(s["gate_sig"], 1)
            act.wait_ge(s["ln_stats"], 2)
            act.activation(rstd, mv[:, :, 1:2], ACT.Sqrt, bias=eps[:, 0:1]).then_inc(s["ln_std"], 1)
            for t in range(Q):
                n = rows(t)
                act.wait_ge(s["x1_turned"], t + 1)
                copy(x1T[:, :, t * P:t * P + n], bank(4 + 2 * (t % 2), KD, P)[:, :, 0:n]).then_inc(s["x1T_ready"], 1)
            act.wait_ge(s["gexp_in"], 1)
            act.activation(t4, t4, ACT.Exp).then_inc(s["gexp"], 1)
            act.wait_ge(s["e2_in"], 1)
            act.activation(e2, e2, ACT.Exp).then_inc(s["e2_out"], 1)

            act.wait_ge(s["table_ready"], 1)
            def block_act(e):
                act.wait_ge(s["xg_turned"], e + 1)
                copy(xgT, bank(0, KD, P)).then_inc(s["xgT_ready"], 1)
                act.wait_ge(s["gate_mm"], e + 3)
                act.activation(esig, bank(2, FF), ACT.Sigmoid).then_inc(s["gate_act"], 1)

            with act.Fori(0, NE) as e:
                block_act(e)
            extra_blocks(act, lambda i: block_act(i + NE))
            act.wait_ge(s["ln_stats"], 3)
            act.activation(rstd, mv[:, :, 1:2], ACT.Sqrt, bias=eps[:, 0:1]).then_inc(s["ln_std"], 1)

        @block.vector
        def _(v):
            def tt(out, a, b, op):
                return v.tensor_tensor(out, a, b, op)

            def stt(out, a, sc, b, op0, op1):
                return v.scalar_tensor_tensor(out, a, sc, b, op0, op1)

            def ts(out, a, s1, op0, s2=None, op1=None):
                if op1 is None:
                    return v.tensor_scalar(out, a, s1, None, op0)
                return v.tensor_scalar(out, a, s1, s2, op0, op1)

            def layer_norm(x, pas, first_wait):
                for t in range(Q):
                    n = rows(t)
                    first_wait(t)
                    for h in range(2):
                        v.bn_stats(st6[0:n, t, h, :], x[0:n, t, h * 512:(h + 1) * 512])
                v.drain()
                for t in range(Q):
                    last = v.bn_aggr(mv[0:rows(t), t, :], st6[0:rows(t), t, :, :])
                last.then_inc(s["ln_stats"], 1)
                v.wait_ge(s["ln_std"], pas)
                v.reciprocal(rstd, rstd)
                v.drain()
                for t in range(Q):
                    n = rows(t)
                    xt = x[0:n, t, :]
                    ts(xt, xt, mv[0:n, t, 0:1], ALU.subtract, rstd[0:n, t, :], ALU.mult)
                    v.drain()
                    tt(xt, xt, gb[0:n, 0, :], ALU.mult)
                    v.drain()
                    tt(xt, xt, gb[0:n, 1, :], ALU.add).then_inc(s["x_normed"], 1)

            v.memset(mv, 1.0)
            v.drain()
            v.wait_ge(s["x_in"], 64)
            layer_norm(xtok, 1, lambda t: None)

            v.wait_ge(s["mkT_ready"], 1)
            v.memset(kT[:, 0:P], 0.0)
            v.memset(vtok[:, 0, :], 0.0).then_inc(s["zeros_set"], 1)
            v.wait_ge(s["z_ready"], NF + 2)
            cos, sin = const("cos"), const("sin")
            v.wait_ge(s["rot_made"], 1)
            v.wait_ge(s["spilled"], 16 * Q)
            tt(kT[:, P:], z[:, FK, 0:T], cos[:, 0:T], ALU.mult)
            tt(view(Fo, T), bank(7, T), sin[:, 0:T], ALU.mult)
            tt(kTs, z[:, FK, T:N], cos[:, T:N], ALU.mult)
            tt(view(Fo + 512, B), bank(0, B), sin[:, T:N], ALU.mult)
            tt(qsS[:, 0:4, :], z[:, FQ:FQ + NJ, T:N], bc(cos[:, T:N], 1, NJ), ALU.mult)
            tt(view(Fo + 520, NJ, B), bank(1, NJ, B), bc(sin[:, T:N], 1, NJ), ALU.mult)
            v.tensor_copy(qsS[:, 4:6, :], z[:, FM:FM + 2, T:N])
            v.drain()
            tt(kT[:, P:], kT[:, P:], view(Fo, T), ALU.add)
            tt(qsS[:, 0:4, :], qsS[:, 0:4, :], view(Fo + 520, NJ, B), ALU.add)
            tt(kTs, kTs, view(Fo + 512, B), ALU.add).then_inc(s["kT_ready"], 1)

            v.wait_ge(s["shift_ready"], 1)
            tt(zs[:, :, 1:T], z[:, 0:SF, 0:T - 1], z[:, 0:SF, 1:T], ALU.subtract)
            ts(zs[:, :, 0:1], z[:, 0:SF, 0:1], -1.0, ALU.mult)
            tt(zs[:, :, T:N], sstT, z[:, 0:SF, T:N], ALU.subtract)
            v.drain()
            for f in range(SF):
                last = stt(zs[:, f, :], zs[:, f, :], prm[:, PR_MU + f:PR_MU + f + 1], z[:, f, :], ALU.mult, ALU.add)
            last.then_inc(s["zs_ready"], 1)

            v.wait_ge(s["params_in"], 80)
            v.wait_ge(s["mkv_made"], 2)
            with v.Fori(0, NT) as i:
                cols = bass.ds(i * P, P)
                v.wait_ge(s["blk_rot"], i + 1)
                tt(qs[:, 0:4, :], z[:, FQ:FQ + NJ, cols], bc(cos[:, cols], 1, NJ), ALU.mult)
                tt(tmpq, bank(6, NJ, P), bc(sin[:, cols], 1, NJ), ALU.mult)
                v.tensor_copy(qs[:, 4:6, :], z[:, FM:FM + 2, cols])
                v.drain()
                tt(qs[:, 0:4, :], qs[:, 0:4, :], tmpq, ALU.add).then_inc(s["blk_q"], 1)
                v.wait_ge(s["blk_scores"], i + 1)
                v.wait_ge(s["blk_kv"], i + 1)
                stt(S[:, 0:8, :], bank(0, 8, 256), 0.125, bc(mst, 1, 8), ALU.mult, ALU.add)
                v.tensor_reduce(mx[:, 8:12], bank(4, 4, 256), AX.X, ALU.max)
                v.drain()
                v.tensor_reduce(mx[:, 0:8], S[:, 0:8, :], AX.X, ALU.max)
                ts(nmx[:, 8:12], mx[:, 8:12], -0.125, ALU.mult)
                v.drain()
                tt(mx[:, 0:8], mx[:, 0:8], sink_bc, ALU.max)
                v.drain()
                ts(nmx[:, 0:8], mx[:, 0:8], -1.0, ALU.mult)
                v.drain()
                tt(ske, sink_bc, nmx[:, 0:8], ALU.add).then_inc(s["blk_max"], 1)
                v.wait_ge(s["blk_exp"], i + 1)
                tt(den[:, 0:8], den[:, 0:8], ske, ALU.add)
                v.drain()
                v.reciprocal(rden, den)
                v.drain()
                tt(S, S, bc(rden, 2, 256), ALU.mult).then_inc(s["blk_prob"], 1)
                v.wait_ge(s["blk_turned"], i + 1)
                v.tensor_copy(PT[:, 12:24, :], bank(3, 12, P)).then_inc(s["blk_pT_dve"], 1)

            v.wait_ge(s["sk_rows"], 1)
            v.tensor_reduce(smx[0:64, 0:1], bank(0, P)[0:64, :], AX.X, ALU.max)
            v.tensor_reduce(smx[0:32, 1:2], bank(1, 2 * P)[0:32, :], AX.X, ALU.max)
            v.drain()
            ts(smx[0:64, 0:1], smx[0:64, 0:1], 0.125, ALU.mult)
            ts(snmx[0:32, 1:2], smx[0:32, 1:2], -0.125, ALU.mult)
            v.drain()
            tt(smx[0:64, 0:1], smx[0:64, 0:1], sink_row[0:64, :], ALU.max)
            v.drain()
            ts(snmx[0:64, 0:1], smx[0:64, 0:1], -1.0, ALU.mult)
            v.drain()
            tt(sske[0:64, 0:1], sink_row[0:64, :], snmx[0:64, 0:1], ALU.add).then_inc(s["sk_max"], 1)
            v.wait_ge(s["sk_exp"], 1)
            tt(sden[0:64, 0:1], sden[0:64, 0:1], sske[0:64, 0:1], ALU.add)
            v.drain()
            v.reciprocal(srd[0:64, 0:1], sden[0:64, 0:1])
            v.reciprocal(srd[0:32, 1:2], sden[0:32, 1:2])
            v.drain()
            ts(sW[0:64, :], sW[0:64, :], srd[0:64, 0:1], ALU.mult)
            ts(sM[0:32, :, :], sM[0:32, :, :], srd[0:32, 1:2], ALU.mult).then_inc(s["sk_prob"], 1)

            def pcol(r0, j):
                return prm[:, r0 + j:r0 + j + 1]

            def halves(ap):
                return ap.rearrange("p (h n) -> p h n", h=2)

            v.wait_ge(s["head_root"], 1)
            ts(rn[0:HA, :], rn[0:HA, :], 1e-12, ALU.max)
            v.drain()
            v.reciprocal(rn[0:HA, :], rn[0:HA, :]).then_inc(s["head_recip"], 1)
            for j in range(NJ):
                v.wait_ge(s["kk_bcast"], j + 1)
                stt(halves(kk[:, j, :]), halves(kTr[:, j, :]), pcol(PR_KK, j), psum[:, 4:6, 0:NH], ALU.mult, ALU.mult).then_inc(s["prep_done"], 1)
            v.wait_ge(s["lora_sig"], 8)
            for j in range(NJ):
                ts(sqb[:, j, :], ah[:, j, :], 1.0, ALU.subtract, pcol(PR_KA, j), ALU.mult)
            v.drain()
            tt(ah, kk, ah, ALU.mult)
            stt(kTr, sqb, 1.0, kTr, ALU.add, ALU.mult)
            v.drain()
            for j in range(NJ):
                last = stt(sqb[:, j, :], rT[:, j, :], pcol(PR_RK, j), kTr[:, j, :], ALU.mult, ALU.mult)
            last.then_inc(s["bonus_in"], 1)
            for j in range(NJ):
                v.wait_ge(s["bonus_mm"], j + 1)
                tt(halves(BV[:, j, :]), halves(vT[:, j, :]), psum[:, 6:8, 0:NH], ALU.mult).then_inc(s["prep_done"], 1)
            v.wait_ge(s["samp_stack"], 1)
            ts(sstk[:, 0, :, :], kk[:, :, T:N], -1.0, ALU.mult)
            v.tensor_copy(sstk[:, 1, :, :], wS)
            v.tensor_copy(sstk[:, 2, :, :], kTr[:, :, T:N])
            v.tensor_copy(sstk[:, 3, :, :], vT[:, :, T:N])
            v.tensor_copy(sstk[:, 4, :, :], ah[:, :, T:N])
            v.tensor_copy(sstk[:, 5, :, :], rT[:, :, T:N]).then_inc(s["samp_stack"], 1)
            for j in range(NJ):
                v.tensor_tensor_scan(Lc[:, j, :], const("reset"), sg[:, j, 0:T], 0.0, ALU.mult, ALU.add)
            v.memset(SR[:, 0, :, :], 0.0)
            v.drain()
            v.sem_inc(s["prep_done"], 1)
            v.wait_ge(s["samp_in"], 64)
            v.wait_ge(s["state_in"], 32)

            def key(q):
                return bc(vec[:, q, :], 1, 32)

            tt(sTmp, sS, key(0), ALU.mult)
            v.drain()
            v.tensor_reduce(sa, sTmp, AX.X, ALU.add)
            tt(sS, sS, key(1), ALU.mult)
            v.drain()
            tt(sTmp, key(4), bc(sa, 2, 64), ALU.mult)
            v.drain()
            tt(sS, sS, sTmp, ALU.add)
            v.drain()
            tt(sTmp, key(2), bc(vvh, 2, 64), ALU.mult)
            v.drain()
            tt(sS, sS, sTmp, ALU.add)
            v.drain()
            tt(sTmp, sS, key(5), ALU.mult)
            v.drain()
            v.tensor_reduce(sy, sTmp, AX.X, ALU.add).then_inc(s["samp_state"], 1)
            v.wait_ge(s["ysamp_turned"], 1)
            v.wait_ge(s["out_done"], 16 * 12)

            v.sem_inc(s["y_ready"], 1)
            v.sem_inc(s["chain_done"], 1)
            up2, lows = const("upper2", 2, P), [const(f"level{k}") for k in range(1, 6)]
            with v.Fori(0, NT) as i:
                cols = bass.ds(i * P, P)
                tt(Pexc, Lc[:, :, cols], sg[:, :, cols], ALU.subtract).then_inc(s["gn_bcast"], 1)
                v.wait_ge(s["exps_made"], i + 1)
                stt(AR[:, :, 0, :], kk[:, :, cols], -1.0, Pexc, ALU.mult, ALU.mult)
                tt(AR[:, :, 1, :], rT[:, :, cols], Pinc, ALU.mult)
                tt(Bt, ah[:, :, cols], Pinv, ALU.mult)
                tt(Kt, kTr[:, :, cols], Pinv, ALU.mult)
                v.tensor_copy(pc2, Pinc.rearrange("p j (c n) -> p c j n", c=2)[:, :, :, CH - 1])
                v.tensor_copy(Vt, vT[:, :, cols]).then_inc(s["tile_ready"], 1)
                v.wait_ge(s["tri_made"], i * 3 + 1)
                tt(MR, bank(4, HA, 2, P), bc(up2, 1, HA), ALU.mult).then_inc(s["tri_ready"], 1)
                v.wait_ge(s["tri_made"], i * 3 + 2)
                tt(NR, bank(0, HA, 2, P), bc(up2, 1, HA), ALU.mult).then_inc(s["nk_ready"], 1)
                v.wait_ge(s["tri_made"], i * 3 + 3)
                for par in range(2):
                    tt(XX[:, par * 4:par * 4 + 4, 0, :], bank(4 + 2 * par, NJ, P), bc(const("low1"), 1, NJ), ALU.mult)
                tt(XX[:, :, 1, :], MR[:, :, 0, :], bc(const("up1"), 1, HA), ALU.mult)
                v.drain()
                tt(XX, XX, bc(bc(ident, 1, 2), 1, HA), ALU.add).then_inc(s["tri_ready"], 1)
                for k in range(5):
                    for g in range(2):
                        v.wait_ge(s["lvl_t1"], i * 10 + 2 * k + g + 1)
                        tt(T1[:, g * 4:g * 4 + 4, :], bank(g, NJ, P), bc(lows[k], 1, NJ), ALU.mult).then_inc(s["lvl_t1_ready"], 1)
                    for g in range(2):
                        v.wait_ge(s["lvl_x"], i * 10 + 2 * k + g + 1)
                        h = slice(g * 4, g * 4 + 4)
                        tt(XX[:, h, 0, :], XX[:, h, 0, :], bank(2 + g, NJ, P), ALU.add)
                        tt(XX[:, h, 1, :], XX[:, h, 1, :], bank(4 + g, NJ, P), ALU.add).then_inc(s["lvl_x_ready"], 1)
                v.wait_ge(s["gh_made"], i + 1)
                for c in range(2):
                    for r in (slice(0, 64), slice(64, 128)):
                        tt(GT[r, c, :, :], bank(4 + c, NJ, 2, 64)[r, :, 0, :], bc(ident[r, r], 1, NJ), ALU.add)
                    last = v.tensor_copy(Hm[:, c, :, :], bank(4 + c, NJ, 2, 64)[:, :, 1, :])
                last.then_inc(s["gh_ready"], 1)
                v.wait_ge(s["ry_made"], i + 1)
                tt(Rh, bank(2, NJ, P), AR[:, :, 1, :], ALU.add)
                for c in range(2):
                    v.wait_ge(s["chain_mm"], i * 2 + c + 1)
                    for par in range(2):
                        r = slice(par * 64, par * 64 + 64)
                        tt(SR[r, c + 1, :, :], bank(6 + par, NJ, 64)[r, :, :], Hm[r, c, :, :], ALU.add)
                    v.drain()
                    last = tt(SR[:, c + 1, :, :], SR[:, c + 1, :, :], bc(pc2[:, c, :], 2, 64), ALU.mult)
                    if c == 0:
                        last.then_inc(s["chain_done"], 1)
                v.wait_ge(s["y_made"], i + 1)
                v.wait_ge(s["ry_ready"], i + 1)
                for par in range(2):
                    r = slice(par * 64, par * 64 + 64)
                    tt(YT[r, :, cols], bank(par, NJ, P)[r, :, :], Yl[r, :, :], ALU.add)
                v.drain()
                v.sem_inc(s["y_ready"], 1)
                v.tensor_copy(SR[:, 0, :, :], SR[:, 2, :, :]).then_inc(s["chain_done"], 1)

            v.wait_ge(s["ysamp_ready"], 1)
            v.wait_ge(s["fstate_turned"], 1)
            v.drain()
            for j in range(NJ):
                v.wait_ge(s["gn_mean"], j + 1)
                stt(halves(YT[:, j, :]), psum[:, 4 + 2 * (j % 2):6 + 2 * (j % 2), 0:NH], -1.0 / 64, halves(YT[:, j, :]),
                    ALU.mult, ALU.add).then_inc(s["gn_center"], 1)
            v.drain()
            tt(sqb, YT, YT, ALU.mult).then_inc(s["gn_sq"], 1)
            v.wait_ge(s["head_root"], 2)
            v.reciprocal(rn[0:HA, :], rn[0:HA, :]).then_inc(s["head_recip"], 1)
            for j in range(NJ):
                v.wait_ge(s["gn_mean"], NJ + j + 1)
                tt(halves(YT[:, j, :]), halves(YT[:, j, :]), psum[:, 4:6, 0:NH], ALU.mult).then_inc(s["gn_bcast"], 1)
                v.drain()
                ts(YT[:, j, :], YT[:, j, :], pcol(PR_LG, j), ALU.mult, pcol(PR_LB, j), ALU.add)
            v.drain()
            tt(YT, YT, BV, ALU.add)
            v.drain()
            tt(YT, YT, gT, ALU.mult).then_inc(s["oa_ready"], 1)

            v.drain()
            v.sem_inc(s["merged"], 2)
            v.sem_inc(s["proj_used"], 2)
            with v.Fori(0, KD // 2) as i:
                for q in range(2):
                    dst = MG[:, bass.ds(i * 2 + q, 1), :].rearrange("p a (h n) -> p (a h) n", h=2)
                    for g in range(3):
                        step = q * 3 + g
                        v.wait_ge(s["gate_sig"], i * 6 + step + 3)
                        v.wait_ge(s["proj_made"], i * 6 + step + 1)
                        pj = psum[:, 4 + 2 * (step % 2):6 + 2 * (step % 2), 0:NH]
                        if g == 0:
                            tt(dst, halves(gsig[step % 2]), pj, ALU.mult).then_inc(s["proj_used"], 1)
                        else:
                            tt(halves(ptmp), halves(gsig[step % 2]), pj, ALU.mult).then_inc(s["proj_used"], 1)
                            v.drain()
                            last = tt(dst, dst, halves(ptmp), ALU.add)
                            v.drain()
                    v.sem_inc(s["merged"], 1)

            v.wait_ge(s["xback_in"], 32)
            v.wait_ge(s["out_in"], 80)

            def residual(t):
                n = rows(t)
                v.wait_ge(s["h_made"], t + 1)
                stt(x1[0:n, t, :], x1[0:n, t, :], ALPHA, bank(2 * (t % 2), D)[0:n, :], ALU.mult, ALU.add).then_inc(s["h_used"], 1)
                v.drain()

            layer_norm(x1, 2, residual)

            v.memset(LG, 0.0)
            v.drain()
            v.wait_ge(s["logits_made"], 1)
            lgp = bank(0, Q, NG + NE)
            tt(LG[:, 0:NT, :], lgp[:, 0:NT, :], bc(rb, 1, NT), ALU.add)
            tt(LG[0:B, NT, :], lgp[0:B, NT, :], rb[0:B, :], ALU.add)
            v.drain()
            iota = const("iota")

            def last1(ap, n):
                return ap.to_broadcast(list(ap.shape[:-1]) + [n])

            def first_max(vals, top, eq, cand, pos, onehot, n):
                v.tensor_reduce(top, vals, AX.X, ALU.max)
                v.drain()
                tt(eq, vals, last1(top, n), ALU.is_equal)
                v.drain()
                stt(cand, eq, -1000.0, bc(iota[:, 0:n], 1, Q), ALU.mult, ALU.add)
                v.drain()
                v.tensor_reduce(pos, cand, AX.X, ALU.min)
                v.drain()
                tt(onehot, cand, last1(pos, n), ALU.is_equal)
                v.drain()

            gl, er = LG[:, :, 0:NG], LG[:, :, NG:]
            first_max(gl, g1, eq4, c4, i1, oh4, NG)
            tt(t4, gl, last1(g1, NG), ALU.subtract).then_inc(s["gexp_in"], 1)
            ts(c4, oh4, 1.0, ALU.subtract, BIG, ALU.mult)
            tt(el.rearrange("p t (g e) -> p t g e", g=NG), er.rearrange("p t (g e) -> p t g e", g=NG), bc(oh4, 3, EPG), ALU.mult)
            v.drain()
            tt(el.rearrange("p t (g e) -> p t g e", g=NG), el.rearrange("p t (g e) -> p t g e", g=NG), bc(c4, 3, EPG), ALU.add)
            v.drain()
            first_max(el, v1, eqx, cx, i1, OH[:, 0, :, :], NE)
            stt(el, OH[:, 0, :, :], -2.0 * BIG, el, ALU.mult, ALU.add)
            v.drain()
            first_max(el, v2, eqx, cx, i1, OH[:, 1, :, :], NE)
            tt(e2, v2, v1, ALU.subtract).then_inc(s["e2_in"], 1)
            tt(OH, OH, bc(last1(const("valid", Q, 1), NE), 1, 2), ALU.mult)
            v.drain()
            tt(Osum, OH[:, 0, :, :], OH[:, 1, :, :], ALU.add).then_inc(s["onehot_ready"], 1)
            v.wait_ge(s["gexp"], 1)
            v.tensor_reduce(gd, t4, AX.X, ALU.add)
            v.wait_ge(s["e2_out"], 1)
            ts(rden2, e2, 1.0, ALU.add)
            v.drain()
            tt(gd, gd, rden2, ALU.mult)
            v.drain()
            v.reciprocal(pgate[:, 0, :, :], gd)
            v.drain()
            tt(pgate[:, 1, :, :], pgate[:, 0, :, :], e2, ALU.mult)
            v.wait_ge(s["rank_made"], 1)
            v.tensor_copy(rank, bank(1, Q, NE))
            v.tensor_copy(cnt, bank(2, NE))
            v.drain()
            ts(qb, rank, float(P), ALU.is_ge)
            ts(nx, cnt, float(P), ALU.is_gt)
            v.drain()
            for q in range(2, 5):
                stt(qb, rank, float(P * q), qb, ALU.is_ge, ALU.add)
                stt(nx, cnt, float(P * q), nx, ALU.is_gt, ALU.add)
                v.drain()
            v.tensor_tensor_scan(incl, const("ones")[:, 0:NE], nx, 0.0, ALU.mult, ALU.add)
            stt(rank, qb, -float(P), rank, ALU.mult, ALU.add)
            ts(blk, qb, 0.0, ALU.is_gt)
            v.drain()
            tt(osx, incl, nx, ALU.subtract)
            v.drain()
            stt(dov, osx, float(NE - 1), iota[:, 0:NE], ALU.add, ALU.subtract)
            v.drain()
            tt(blk, blk, bc(dov, 1, Q), ALU.mult)
            v.drain()
            tt(blk, blk, qb, ALU.add)
            v.drain()
            tt(blk, blk, bc(iota[:, 0:NE], 1, Q), ALU.add)
            v.drain()
            for k in range(2):
                tt(el, OH[:, k, :, :], blk, ALU.mult)
                tt(cx, OH[:, k, :, :], rank, ALU.mult)
                v.drain()
                v.tensor_reduce(bk[:, k, :, :], el, AX.X, ALU.add)
                v.tensor_reduce(sk[:, k, :, :], cx, AX.X, ALU.add)
                v.drain()
            asg = const("asg1", Q, 2)
            for k in range(2):
                tt(SK[:, k, :, :], bc(iota, 1, Q), last1(sk[:, k, :, :], P), ALU.is_equal)
                tt(VB[:, :, k, 1, :], bc(iota[:, 0:NB], 1, Q), last1(bk[:, k, :, :], NB), ALU.is_equal)
                v.drain()
                tt(VB[:, :, k, 1, :], VB[:, :, k, 1, :], last1(const("valid", Q, 1), NB), ALU.mult)
                v.drain()
                tt(VB[:, :, k, 0, :], VB[:, :, k, 1, :], last1(asg[:, :, k:k + 1], NB), ALU.mult)
                v.drain()
                tt(VB[:, :, k, 1, :], VB[:, :, k, 1, :], last1(const("tok1", Q, 1), NB), ALU.mult)
                v.drain()
            v.sem_inc(s["route_ready"], 1)
            tt(xe, bc(iota[:, 0:XB], 2, NE), bc(osx, 1, XB), ALU.is_ge)
            tt(xe2, bc(iota[:, 0:XB], 2, NE), bc(incl, 1, XB), ALU.is_lt)
            v.drain()
            tt(xe, xe, xe2, ALU.mult)
            v.drain()
            tt(xe, xe, bc(iota[:, 0:NE], 1, XB), ALU.mult)
            v.drain()
            v.tensor_reduce(ovf[:, 0:XB], xe, AX.X, ALU.add)
            v.tensor_copy(ovf[:, XB:XB + 1], incl[:, NE - 1:NE])
            v.drain()
            v.tensor_copy(ovfi.bitcast(I32), ovf)
            v.wait_ge(s["table_made"], 1)
            ts(tadd, bank(3, 2, NB), 0.0, ALU.is_equal, PAD_ROW, ALU.mult)
            v.drain()
            stt(tabf, bank(3, 2, NB), -1.0, tadd, ALU.add, ALU.add)
            v.drain()
            v.tensor_copy(tabi.bitcast(U32), tabf)
            v.memset(xg[0], 0.0)
            v.memset(xg[1], 0.0)
            v.drain()
            v.sem_inc(s["table_ready"], 1)

            v.sem_inc(s["yb_ready"], 1)
            def block_vec(q, e, i):
                v.wait_ge(s["gate_act"], e + 1)
                tt(esig, esig, bank(2, FF), ALU.mult)
                v.drain()
                v.wait_ge(s["up_mm"], e + 3)
                tt(hb, esig, bank(3, FF), ALU.mult).then_inc(s["h_ready"], 1)
                v.wait_ge(s["hT_turned"], e + 1)
                v.tensor_copy(hT, bank(4, 4, P)).then_inc(s["hT_ready"], 1)
                v.wait_ge(s["y_mm"], e + 3)
                v.wait_ge(s[f"scat_{'ab'[q]}"], i * 16 + 16)
                v.tensor_copy(yb[q], bank(5, D)).then_inc(s["yb_ready"], 1)

            with v.Fori(0, NE // 2) as i:
                for q in range(2):
                    block_vec(q, i * 2 + q, i)
            extra_blocks(v, lambda i: block_vec(0, i + NE, i + NE // 2))

            v.wait_ge(s["yk_in"], 16 * (Q + 2))

            def expert_sum(t):
                n = rows(t)
                xt = x1[0:n, t, :]
                ts(xt, xt, ALPHA, ALU.mult)
                v.drain()
                for k in range(2):
                    stt(xt, yk[0:n, t, k, :], pgate[0:n, k, t, :], xt, ALU.mult, ALU.add)
                    v.drain()

            layer_norm(x1, 3, expert_sum)

        @block.gpsimd
        def _(g):
            g.wait_ge(s["zeros_set"], 1)
            g.wait_ge(s["kT_ready"], 1)
            g.wait_ge(s["v_ready"], 1)
            g.wait_ge(s["consts_in"], 16)
            g.wait_ge(s["mkv_made"], 2)
            g.wait_ge(s["spilled"], 16 * Q)
            g.tensor_copy(mst, const("mask0"))
            with g.Fori(0, NT) as i:
                g.wait_ge(s["blk_out"], i + 1)
                g.sem_inc(s["pace"], 1)
                g.tensor_copy(kst, kT[:, bass.ds(i * P, 2 * P)])
                g.tensor_copy(vst, vtok[:, bass.ds(i, 2), :])
                g.drain()
                g.sem_inc(s["blk_kv"], 1)
                g.wait_ge(s["blk_max"], i + 1)
                g.sem_inc(s["pace"], 1)
                g.tensor_copy(mst, const("mask"))
            g.drain()
            g.sem_inc(s["blk_kv"], 1)

            g.wait_ge(s["table_ready"], 1)
            g.wait_ge(s["x1_spilled"], 16 * Q)
            tab = tabi.bitcast(U32)
            ix = idx.bitcast(U32)

            def gather(q, b, sem):
                g.tensor_copy(ix[:, q, :], tab[:, :, b])
                g.drain()
                g.indirect_dma_start(xg[q], None, X["x1"], bass.IndirectOffsetOnAxis(ap=ix[:, q, 1:2], axis=0),
                                     bounds_check=N - 1, oob_is_err=False).then_inc(sem, 16)

            def scatter(q, sem):
                g.indirect_dma_start(X["ya"], bass.IndirectOffsetOnAxis(ap=ix[:, q, 0:1], axis=0), yb[q], None,
                                     bounds_check=2 * N - 1, oob_is_err=False).then_inc(sem, 16)

            g.dma_start(X["prime"][0:1, :], const("iota")[0:1, 0:16]).then_inc(s["scat_a"], 16)
            g.dma_start(X["prime"][1:2, :], const("iota")[0:1, 0:16]).then_inc(s["scat_b"], 16)
            with g.Fori(0, NE // 2) as i:
                for q in range(2):
                    e = i * 2 + q
                    g.wait_ge(s[f"scat_{'ab'[q]}"], i * 16 + 16)
                    g.sem_inc(s["pace"], 1)
                    gather(q, bass.ds(e, 1), s[f"xg_in_{'ab'[q]}"])
                for q in range(2):
                    e = i * 2 + q
                    g.wait_ge(s["yb_ready"], e + 2)
                    g.sem_inc(s["pace"], 1)
                    scatter(q, s[f"scat_{'ab'[q]}"])
            g.wait_ge(s["scat_a"], 16 * (NE // 2 + 1))
            g.wait_ge(s["scat_b"], 16 * (NE // 2 + 1))

            def extra_rows(i):
                g.wait_ge(s["scat_a"], i * 16 + 16 * (NE // 2 + 1))
                g.sem_inc(s["pace"], 1)
                gather(0, bass.ds(i + NE, 1), s["xg_in_a"])
                g.wait_ge(s["yb_ready"], i + (NE + 2))
                g.sem_inc(s["pace"], 1)
                scatter(0, s["scat_a"])
                g.wait_ge(s["scat_a"], i * 16 + 16 * (NE // 2 + 2))
                g.sem_inc(s["pace"], 1)

            extra_blocks(g, extra_rows)
            g.sem_inc(s["ovf_step"], 1)


OUTS = [("y_prompt", (T, D), (1, T, D)), ("y_sample", (B, D), (B, 1, D)),
        ("wkv_prompt", (HA, 64, 64), (1, 1, HA, 64, 64)), ("wkv_sample", (B * HA, 64, 64), (1, B, HA, 64, 64)),
        ("shift_prompt", (1, C_SHIFT), (1, 1, C_SHIFT)), ("shift_sample", (B, C_SHIFT), (1, B, C_SHIFT)),
        ("win_k_prompt", (P, P), (1, 1, P, 2, 64)), ("win_v_prompt", (P, P), (1, 1, P, 2, 64)),
        ("win_k_sample", (B, P, P), (1, B, P, 2, 64)), ("win_v_sample", (B, P, P), (1, B, P, 2, 64)),
        ("mem_k_prompt", (NMEM, 256), (1, 1, NMEM, 4, 64)), ("mem_v_prompt", (NMEM, 256), (1, 1, NMEM, 4, 64))]


def kernel(**a):
    import concourse.bacc as bacc
    from concourse.bass_utils import run_bass_kernel_spmd

    nc = bacc.Bacc("TRN2", target_bir_lowering=False, num_devices=1)
    arrays, I, O, X = {}, {}, {}, {}

    def give(name, x):
        x = np.ascontiguousarray(x)
        arrays["in_" + name] = x
        I[name] = nc.dram_tensor("in_" + name, x.shape, F32, kind="ExternalInput").ap()

    give("consts", CONST)
    give("x_prompt", np.reshape(a["x_prompt"], (T, D)))
    give("x_sample", np.reshape(a["x_sample"], (B, D)))
    give("mem_prompt", np.reshape(a["mem_prompt"], (NMEM, D)))
    give("state_wkv", np.reshape(a["state_wkv"], (B * HA, 64, 64)))
    give("state_shift", np.reshape(a["state_shift"], (B, C_SHIFT)))
    for n in ("cache_win_k", "cache_win_v"):
        give(n, np.reshape(a[n], (B, WIN, P)))
    for n in ("cache_mem_k", "cache_mem_v"):
        give(n, np.reshape(a[n], (B, NMEM, 256)))
    for n in ("ln_in_g", "ln_in_b"):
        give(n, a[n])
    for n in ("ln1_g", "ln1_b", "ln2_g", "ln2_b", "w_in", "w_up", "a_up", "g_up", "w_mem_kv", "p_a", "p_b", "p_m", "w_o",
              "e_gate", "e_up", "e_down"):
        give(n, a[n][0])
    vecs = ("mu", "w0", "a0", "k_k", "k_a", "r_k", "lnx_g", "lnx_b")
    give("params", np.concatenate([np.reshape(a[n], (-1, P)) for n in vecs]))
    give("sinks_bc", np.tile(np.reshape(a["sinks"], (1, HA)), (P, 1)))
    give("sinks_row", np.reshape(np.tile(np.reshape(a["sinks"], (2, 1, 4)), (1, B, 1)), (64, 1)))
    give("router_b", np.tile(np.concatenate([a["b_group"], a["b_router"]], 1), (P, 1)))
    give("router_w", np.concatenate([a["w_group"][0], a["w_router"][0]], 1))
    for n, shape in (("x0", (N, D)), ("x1", (N, D)), ("ya", (2 * N, D)), ("sv", (6, B, C_A)), ("sy", (B * HA, 64)), ("prime", (2, 16))):
        X[n] = nc.dram_tensor("scratch_" + n, shape, F32).ap()
    for n, shape, _ in OUTS:
        O[n] = nc.dram_tensor("out_" + n, shape, F32, kind="ExternalOutput").ap()
    build(nc, I, O, X)
    got = run_bass_kernel_spmd(nc, [arrays], core_ids=[0]).results[0]
    return tuple(np.reshape(got["out_" + n], shape) for n, _, shape in OUTS)
```

```python
import math
from contextlib import ExitStack

import numpy as np
import concourse.bass as bass
import concourse.mybir as mybir

F32 = mybir.dt.float32
I32 = mybir.dt.int32
U32 = mybir.dt.uint32
ALU = mybir.AluOpType
ACT = mybir.ActivationFunctionType
AX = mybir.AxisListType

P = 128
D = 1024
KD = D // P
T, B = 512, 8
N = T + B
NH = N // 2
NT = T // P
HA, C_A = 8, 512
NJ = C_A // P
CH = 64
C_SHIFT = 1792
SF = C_SHIFT // P
FQ, FK, FV, FM, NF = 14, 18, 19, 20, 22
GATE0 = NF * P
N_GATE = 3 * KD
G_CACHE, G_BONUS, G_SAMP, G_TILE = 8, 10, 11, 16
N_PROJ = 5888
WIN, NMEM = 128, 256
ALPHA = 2.0 ** 0.25
LN_EPS, LNX_EPS = 1e-5, 64e-5
DECAY = math.exp(-0.5)
NE, FF, NG, EPG = 32, 512, 4, 8
XB = 8
NB = NE + XB
BIG = 1e30
PAD_ROW = 5000.0


def const_table():
    parts, at, off = [], {}, 0

    def put(name, a):
        nonlocal off
        a = np.asarray(a, np.float32)
        full = np.zeros((P, a.shape[1]), np.float32)
        full[:a.shape[0]] = a
        parts.append(full)
        at[name] = (off, a.shape[1])
        off += a.shape[1]

    r = np.arange(P)[:, None]
    c = np.arange(P)[None, :]
    same = (r // CH) == (c // CH)
    put("ident", np.eye(P))
    put("upper2", np.concatenate([same & (r < c), same & (r <= c)], 1))
    put("low1", (r // 2 == c // 2) & (r > c))
    put("up1", (r // 2 == c // 2) & (r < c))
    for k in range(1, 6):
        b = 2 ** k
        put(f"level{k}", (r // (2 * b) == c // (2 * b)) & (r // b == c // b + 1))
    kj = np.arange(2 * P)[None, :]
    band = (kj <= r + P) & (r + P - kj < WIN)
    put("mask0", np.where(band & (kj >= P), 0.0, -BIG))
    put("mask", np.where(band, 0.0, -BIG))
    half = 8
    inv = 500000.0 ** (-np.arange(half, dtype=np.float32) / half)
    pos = np.concatenate([np.arange(T), np.full(B, 2048)]).astype(np.float32)
    ang = (pos[:, None] * inv[None, :].astype(np.float32)).astype(np.float32)
    cos, sin = np.ones((P, N)), np.zeros((P, N))
    rot = np.zeros((P, P))
    for h in range(2):
        for i in range(half):
            for base, sign, other in ((0, -1.0, half), (half, 1.0, 0)):
                f = h * 64 + base + i
                cos[f] = np.cos(ang[:, i])
                sin[f] = np.sin(ang[:, i])
                rot[h * 64 + other + i, f] = sign
    put("cos", cos)
    put("sin", sin)
    put("rot", rot)
    s8 = np.zeros((P, NJ, HA))
    for j in range(NJ):
        for p in range(P):
            s8[p, j, 2 * j + p // 64] = 1
    put("sel8", s8.reshape(P, -1))
    put("sel8t", np.transpose(s8, (2, 1, 0)).reshape(HA, -1))
    put("bones", (r // 64 == c // 64))
    put("before", r < c)
    put("ones", np.ones((P, P)))
    put("reset", np.tile((np.arange(T) % CH != 0)[None, :], (P, 1)))
    put("iota", np.tile(np.arange(P)[None, :], (P, 1)))
    put("eps", np.tile(np.array([[LN_EPS, LNX_EPS]]), (P, 1)))
    tok = np.arange(NT + 1)[None, :] * P + r
    put("valid", tok < N)
    put("tok1", tok + 1)
    put("asg1", np.stack([2 * tok + 1, 2 * tok + 2], 2).reshape(P, -1))
    return np.concatenate(parts, 1), at


CONST, CAT = const_table()
NCONST = CONST.shape[1]
PR_MU, PR_W0, PR_A0, PR_KK, PR_KA, PR_RK, PR_LG, PR_LB, PR_N = 0, 14, 18, 22, 26, 30, 34, 38, 42


SEMS = """
consts_in params_in x_in mem_in cache_in 
lora_in state_in samp_in out_in xback_in 
p1w0_in p1w1_in mgw0_in mgw1_in spilled x1_spilled out_done
ln_stats ln_std ln_rs ln_scaled ln_gained x_normed x_turned xT_ready mem_turned memT_ready mkv_made mkv_ready mkT_ready
z_made z_ready side_turned side_ready
v_ready rot_made kT_ready kout_turned kout_ready
blk_kv blk_rot blk_q blk_scores blk_max blk_exp blk_prob blk_turned blk_pT_act blk_pT_dve blk_mixed blk_out
sk_turned sk_ready sk_scored sk_cols sk_rows sk_max sk_exp sk_prob sk_pT_made sk_pT_ready sk_mixed sk_done
zs_ready lora_act lora_mm lora_sig kk_sq head_sum head_root head_recip kk_bcast bonus_in bonus_mm prep_done
samp_stack samp_state
exps_made tile_ready tm_turned tm_ready tri_made tri_ready nk_ready lvl_t1 lvl_t1_ready lvl_x lvl_x_ready
nv_made nv_ready xav_made xav_ready gh_made gh_ready ry_made ry_ready chain_mm chain_done y_made y_ready
fstate_ready
gn_mean gn_center gn_sq gn_bcast oa_ready
gate_made gate_out gate_spill0 gate_spill1 gate_sig proj_made proj_used merged
h_made h_used x1_turned x1T_ready logits_made onehot_ready rank_made gexp_in gexp e2_in e2_out
route_ready table_made table_ready
xg_in_a xg_in_b xg_turned xgT_ready gate_mm up_mm gate_act h_ready hT_turned hT_ready y_mm yb_ready
ew0g_in ew0u_in ew0d_in ew1g_in ew1u_in ew1d_in scat_a scat_b
ovf_step pace gidx_ready ln2_in yk0_in yk1_in yk2_in yk3_in yk4_in 
""".split()


SIDE_PARAMS, SIDE_SHIFT, SIDE_SAMP, SIDE_YSAMP, SIDE_STATE = 1, 2, 3, 4, 5


def build(nc, I, O, X):
    with ExitStack() as ctx:
        arena = ctx.enter_context(nc.sbuf_tensor("arena", [P, 53200], F32))
        psum = ctx.enter_context(nc.psum_tensor("psum", [P, 8, 512], F32))
        s = {n: ctx.enter_context(nc.semaphore(n)) for n in SEMS}

        def view(off, *dims):
            n = int(np.prod(dims))
            a = arena[:, off:off + n]
            if len(dims) == 1:
                return a
            names = "abcd"[:len(dims)]
            return a.rearrange("p (%s) -> p %s" % (" ".join(names), " ".join(names)),
                               **dict(zip(names[1:], dims[1:])))

        def bank(b, *dims, off=0):
            n = int(np.prod(dims))
            a = psum[:, :, :].rearrange("p a b -> p (a b)")[:, b * 512 + off:b * 512 + off + n]
            if len(dims) == 1:
                return a
            names = "abcd"[:len(dims)]
            return a.rearrange("p (%s) -> p %s" % (" ".join(names), " ".join(names)),
                               **dict(zip(names[1:], dims[1:])))

        def bc(ap, axis, n):
            a = ap.unsqueeze(axis)
            sh = list(a.shape)
            sh[axis] = n
            return a.to_broadcast(sh)

        off = [0]

        def take(n):
            o = off[0]
            off[0] += n
            return o

        C0 = take(NCONST)
        PRM = take(PR_N + 6)
        GBo = take(2 * D)
        SMo = take(800)
        XTo = take(KD * N)
        Zo = take(NF * N)
        ZSo = take(SF * N)
        KKo = take(NJ * N)
        BVo = take(NJ * N)
        LCo = take(NJ * T)
        YTo = take(NJ * N)
        Fo = off[0]
        FREE = 53200 - Fo
        assert FREE >= 14336, FREE

        def const(name, *dims):
            o, w = CAT[name]
            return view(C0 + o, *(dims or (w,)))

        consts = view(C0, NCONST)
        ident = const("ident")
        prm = view(PRM, PR_N)
        gb = view(GBo, 2, D)
        sm = [SMo]

        def small(*dims):
            o = sm[0]
            sm[0] += int(np.prod(dims))
            assert sm[0] <= SMo + 800
            return view(o, *dims)

        sink_bc = small(HA)
        sink_row = small(1)
        rb = small(NG + NE)
        st6 = small(NT + 1, 2, 6)
        mv = small(NT + 1, 2)
        rstd, nmr = small(NT + 1, 1), small(NT + 1, 1)
        sstT = small(SF, B)
        mx, nmx, den, ske, rden = small(12), small(12), small(12), small(8), small(12)
        smx, snmx, sden, sske, srd = small(2), small(2), small(2), small(2), small(2)
        kTs = small(B)
        qsS = small(6, B)
        pc2 = small(2, NJ)
        wS = small(NJ, B)

        xT = view(XTo, KD, N)
        z = view(Zo, NF, N)
        zs = view(ZSo, SF, N)

        xtok = view(Fo, NT + 1, D)
        memtok = view(Fo + 5120, 2, D)
        memT = view(Fo + 7168, KD, NMEM)
        wmem = view(Fo + 9216, KD, 512)
        p1w = [view(YTo + q * 1024, KD, P) for q in range(2)]
        kT = view(BVo, P + T)
        vtok = view(BVo + 640, NT + 1, P)
        mkT = view(BVo + 1280, 2, NMEM)
        mkv = view(LCo, 2, 512)
        ktl = view(LCo + 1024, P)
        kss = view(LCo + 1152, P)
        vss = view(LCo + 1280, P)
        shb = view(KKo, C_SHIFT)
        prow = view(LCo + 1408, P)
        ssraw = view(ZSo, C_SHIFT)

        S = view(Fo, 12, 256)
        PT = view(Fo + 3072, 24, P)
        qs = view(Fo + 6144, 6, P)
        kst = view(Fo + 6912, 256)
        vst = view(Fo + 7168, 2, P)
        mst = view(Fo + 7424, 256)
        tmpq = view(Fo + 7680, NJ, P)
        kwin = view(Fo, B, P)
        vwin = view(Fo + 1024, B, P)
        kmem = view(Fo + 2048, B, 2, 256)
        vmem = view(Fo + 6144, B, 2, 256)
        kTb = [view(Fo + 10240 + q * 640, 5, P) for q in range(2)]
        sST = view(Fo + 11520, P)
        sW = view(Fo + 11648, P)
        sM = view(Fo + 11776, 2, P)
        sWT = view(Fo + 12032, 64)
        sMT = view(Fo + 12096, 2, 32)

        sg = view(Zo, NJ, N)
        ah = view(Zo + 2080, NJ, N)
        gT = view(Zo + 4160, NJ, N)
        th = view(Zo + 6240, N)
        kk = view(KKo, NJ, N)
        BV = view(BVo, NJ, N)
        Lc = view(LCo, NJ, T)
        YT = view(YTo, NJ, N)
        rT, kTr, vT = zs[:, 0:4, :], zs[:, 4:8, :], zs[:, 8:12, :]
        xwa, xg_ = zs[:, 12, :], zs[:, 13, :]
        wup = view(Fo, C_A)
        gup = view(Fo + 512, C_A)
        sqb = view(Fo + 1024, NJ, N)
        rn = view(Fo + 3104, N)
        sS = view(Fo + 3640, 32, 64)
        sTmp = view(Fo + 5688, 32, 64)
        vec = view(Fo + 7736, 6, 64)
        vvh = view(Fo + 8120, 32)
        sa = view(Fo + 8152, 32)
        sy = view(Fo + 8184, 32)
        sstk = view(Fo + 8216, 6, NJ, B)
        srow = view(Fo + 8408, 6, C_A)
        yrow = view(Fo + 11480, C_A)
        o = [Fo]

        def F(*dims):
            v = view(o[0], *dims)
            o[0] += int(np.prod(dims))
            assert o[0] <= 53200
            return v

        Pexc, Pinc, Pinv = F(NJ, P), F(NJ, P), F(NJ, P)
        AR = F(NJ, 2, P)
        Bt, Kt, Vt = F(NJ, P), F(NJ, P), F(NJ, P)
        Btok, Ktok, Vtok = F(C_A), F(C_A), F(C_A)
        ANV = F(HA, 2, 64)
        MR, NR = F(HA, 2, P), F(HA, 2, P)
        XX = F(HA, 2, P)
        GT, Hm = F(2, NJ, 64), F(2, NJ, 64)
        T1 = view(Fo, HA, P)
        Rh = view(Fo + 1024, NJ, P)
        XAV = view(Fo + 2560, HA, 2, 64)
        Yl = view(Fo + 3584, NJ, P)
        SR = view(ZSo + 12 * N, 3, NJ, 64)
        fst = view(Fo, HA, 64)

        MGo = Fo + 3640
        MGW = 10 * P + 3 * N
        mgw = [view(MGo + q * MGW, 10, P) for q in range(2)]
        mgg = [view(MGo + q * MGW + 10 * P, 3, N) for q in range(2)]
        ptmp = view(ZSo + 4160, N)
        MG = view(ZSo, KD, N)
        wo = [view(MGo + 2 * MGW, KD, 512), view(KKo, KD, 512)]
        wr = view(MGo + 2 * MGW + 4096, KD, NG + NE)
        assert MGo + 2 * MGW + 4096 + KD * (NG + NE) <= 53200
        gcol = [view(GBo + q * 1024, KD, P) for q in range(2)]
        gout = [z[:, FK + q, :] for q in range(2)]
        x1 = view(Zo, NT + 1, D)
        x1T = xT
        R0 = [ZSo]

        def R(*dims):
            v = view(R0[0], *dims)
            R0[0] += int(np.prod(dims))
            assert R0[0] <= ZSo + SF * N
            return v

        T5 = NT + 1
        LG = R(T5, NG + NE)
        g1 = R(T5, 1)
        eq4, c4, oh4, t4 = R(T5, NG), R(T5, NG), R(T5, NG), R(T5, NG)
        i1 = R(T5, 1)
        gd, gw = R(T5, 1), R(T5, 1)
        el = R(T5, NE)
        eqx, cx = R(T5, NE), R(T5, NE)
        v1, v2 = R(T5, 1), R(T5, 1)
        OH = R(2, T5, NE)
        Osum, rank, qb, blk = R(T5, NE), R(T5, NE), R(T5, NE), R(T5, NE)
        cnt, nx, incl, osx, dov = R(NE), R(NE), R(NE), R(NE), R(NE)
        bk, sk = R(2, T5, 1), R(2, T5, 1)
        SK = R(2, T5, P)
        VB = R(T5, 2, 2, NB)
        tabf = R(2, NB)
        tadd = R(2, NB)
        xe = R(XB, NE)
        xe2 = R(XB, NE)
        pgate = small(2, T5, 1)
        tabi = small(2, NB + 1)
        ovf, ovfi = small(XB + 1), small(XB + 1)
        e2, rden2 = small(T5, 1), small(T5, 1)
        idx = small(4, 1)

        EW = KD * FF
        eg = [view(Fo, KD, FF), view(Fo + EW, KD, FF)]
        eu = [view(Zo + 5120, KD, FF), view(KKo, KD, FF)]
        ed = [view(LCo, FF // P, D), view(Fo + 2 * EW, FF // P, D)]
        yb = [view(Fo + 3 * EW + q * D, D) for q in range(2)]
        esig = view(Zo + 5120 + EW, FF)
        yk = view(Fo, T5, 2, D)
        assert MGo + 2 * MGW >= Fo + 2 * EW and Fo + 3 * EW + 2 * D <= 53200
        m0 = [XTo]

        def M1(*dims):
            v = view(m0[0], *dims)
            m0[0] += int(np.prod(dims))
            assert m0[0] <= XTo + KD * N
            return v

        xg = [M1(D), M1(D)]
        xgT = M1(KD, P)
        hb, hT = M1(FF), M1(FF // P, P)

        block = ctx.enter_context(nc.Block())
        Q = NT + 1

        def rows(t):
            return P if t < NT else B

        def extra_blocks(eng, body):
            n = eng.value_load(ovfi.bitcast(I32)[0:1, XB:XB + 1], min_val=0, max_val=XB)
            with eng.If(n > 0):
                with eng.Fori(0, n) as i:
                    body(i)

        @block.sync
        def _(sp):
            sp.dma_start(xtok[:, 0:NT, :], I["x_prompt"].rearrange("(t p) d -> p t d", p=P)).then_inc(s["x_in"], 16)
            sp.dma_start(xtok[0:B, NT, :], I["x_sample"]).then_inc(s["x_in"], 16)
            sp.dma_start(consts, I["consts"]).then_inc(s["consts_in"], 16)
            sp.dma_start(gb[:, 0, :], I["ln_in_g"].partition_broadcast(P)).then_inc(s["x_in"], 16)
            sp.dma_start(gb[:, 1, :], I["ln_in_b"].partition_broadcast(P)).then_inc(s["x_in"], 16)
            sp.dma_start(memtok, I["mem_prompt"].rearrange("(t p) d -> p t d", p=P)).then_inc(s["mem_in"], 16)
            sp.dma_start(wmem, I["w_mem_kv"].rearrange("(p c) n -> p c n", c=KD)).then_inc(s["mem_in"], 16)
            sp.dma_start(prow[0:PR_N, :], I["params"]).then_inc(s["params_in"], 16)
            sp.dma_start(ssraw[0:B, :], I["state_shift"]).then_inc(s["params_in"], 16)
            sp.dma_start(sink_bc, I["sinks_bc"]).then_inc(s["params_in"], 16)
            sp.dma_start(sink_row[0:64, :], I["sinks_row"]).then_inc(s["params_in"], 16)
            sp.dma_start(rb, I["router_b"]).then_inc(s["params_in"], 16)

            w_in = I["w_in"].rearrange("(p c) n -> p c n", c=KD)

            def p1_load(q, need, src_a, src_b, dst_a, dst_b):
                sp.wait_ge(s["z_made"], need)
                sp.dma_start(dst_a, src_a).then_inc(s[f"p1w{q}_in"], 16)
                sp.dma_start(dst_b, src_b).then_inc(s[f"p1w{q}_in"], 16)

            def p1_tile(f, q, need):
                cols = bass.ds(f * P, P)
                p1_load(q, need, w_in[:, 0:4, cols], w_in[:, 4:8, cols], p1w[q][:, 0:4, :], p1w[q][:, 4:8, :])

            with sp.Fori(0, FQ // 2) as i:
                for q in range(2):
                    p1_tile(i * 2 + q, q, i * 2 + q + 1)
            for j in range(4):
                c0 = FQ * P + j * 64
                p1_load(j % 2, FQ + j + 1, w_in[:, :, c0:c0 + 64], w_in[:, :, c0 + 256:c0 + 320],
                        p1w[j % 2][:, :, 0:64], p1w[j % 2][:, :, 64:128])
            for f in range(FK, NF):
                p1_tile(f, f % 2, f + 1)

            for t in range(Q):
                sp.wait_ge(s["x_normed"], t + 1)
                sp.dma_start(X["x0"][t * P:t * P + rows(t), :], xtok[0:rows(t), t, :]).then_inc(s["spilled"], 16)

            def gate_load(k, q):
                sp.dma_start(gcol[q], w_in[:, :, bass.ds(k * P + GATE0, P)]).then_inc(s[f"p1w{q}_in"], 16)

            def gate_step(k, q, ahead=True):
                if ahead:
                    sp.wait_ge(s["gate_made"], k + 1)
                    gate_load(k + 2, q)
                sp.wait_ge(s["gate_out"], k + 1)
                sp.dma_start(X["gates"][bass.ds(k, 1)].rearrange("a p n -> (a p) n"), gout[q]).then_inc(s[f"gate_spill{q}"], 16)

            sp.wait_ge(s["z_ready"], NF + 2)
            for q in range(2):
                gate_load(q, q)
            for t in range(2):
                sp.wait_ge(s["mkv_ready"], t + 1)
                sp.dma_start(O["mem_k_prompt"][t * P:(t + 1) * P, :], mkv[:, t, 0:256]).then_inc(s["out_done"], 16)
                sp.dma_start(O["mem_v_prompt"][t * P:(t + 1) * P, :], mkv[:, t, 256:512]).then_inc(s["out_done"], 16)
            sp.wait_ge(s["side_ready"], SIDE_SHIFT)
            sp.dma_start(O["shift_prompt"], shb[0:1, :]).then_inc(s["out_done"], 16)
            sp.dma_start(O["shift_sample"], shb[1:1 + B, :]).then_inc(s["out_done"], 16)
            sp.wait_ge(s["kout_ready"], 1)
            sp.wait_ge(s["v_ready"], 1)
            sp.dma_start(O["win_k_prompt"], ktl).then_inc(s["out_done"], 16)
            sp.dma_start(O["win_v_prompt"], vtok[:, NT, :]).then_inc(s["out_done"], 16)

            with sp.Fori(0, NT) as i:
                for q in range(2):
                    gate_step(i * 2 + q, q)

            sp.wait_ge(s["blk_out"], NT + 1)
            sp.wait_ge(s["blk_kv"], NT + 1)
            sp.dma_start(kwin[0:P - 1, :, :], I["cache_win_k"][:, 1:, :].rearrange("b w f -> w b f")).then_inc(s["cache_in"], 16)
            sp.dma_start(vwin[0:P - 1, :, :], I["cache_win_v"][:, 1:, :].rearrange("b w f -> w b f")).then_inc(s["cache_in"], 16)
            sp.dma_start(kwin[P - 1:P, :, :], kss[0:B, :]).then_inc(s["cache_in"], 16)
            sp.dma_start(vwin[P - 1:P, :, :], vss[0:B, :]).then_inc(s["cache_in"], 16)
            sp.dma_start(kmem, I["cache_mem_k"].rearrange("b (t p) f -> p b t f", p=P)).then_inc(s["cache_in"], 16)
            sp.dma_start(vmem, I["cache_mem_v"].rearrange("b (t p) f -> p b t f", p=P)).then_inc(s["cache_in"], 16)
            for k in range(G_CACHE, G_BONUS):
                gate_step(k, k % 2)
            sp.wait_ge(s["cache_in"], 96)
            sp.dma_start(O["win_k_sample"].rearrange("b w f -> w b f"), kwin).then_inc(s["out_done"], 16)
            sp.dma_start(O["win_v_sample"].rearrange("b w f -> w b f"), vwin).then_inc(s["out_done"], 16)

            sp.wait_ge(s["sk_done"], 1)
            sp.wait_ge(s["out_done"], 16 * 10)
            sp.dma_start(wup[0:64, :], I["w_up"]).then_inc(s["lora_in"], 16)
            sp.dma_start(wup[64:128, :], I["a_up"]).then_inc(s["lora_in"], 16)
            sp.dma_start(gup, I["g_up"]).then_inc(s["lora_in"], 16)
            for h in range(2):
                sp.dma_start(sS[h * 64:h * 64 + 64, :, :],
                             I["state_wkv"][:, h * 32:h * 32 + 32, :]).then_inc(s["state_in"], 16)
            gate_step(G_BONUS, G_BONUS % 2)
            sp.wait_ge(s["side_ready"], SIDE_SAMP)
            sp.dma_start(X["sv"].rearrange("q b f -> b q f"), srow[0:B, :, :]).then_inc(s["spilled"], 16)
            sp.wait_ge(s["spilled"], 16 * (Q + 1))
            svv = X["sv"].rearrange("q b (h k) -> (b h) q k", k=64)
            for h in range(2):
                sp.dma_start(vec[h * 64:h * 64 + 64, :, :], svv).then_inc(s["samp_in"], 16)
                sp.dma_start(vvh[h * 64:h * 64 + 64, :], svv[:, 3, h * 32:h * 32 + 32]).then_inc(s["samp_in"], 16)
            for k in range(G_SAMP, G_TILE - 1):
                gate_step(k, k % 2)
            sp.wait_ge(s["samp_state"], 1)
            for h in range(2):
                sp.dma_start(O["wkv_sample"][:, h * 32:h * 32 + 32, :], sS[h * 64:h * 64 + 64, :, :]).then_inc(s["out_done"], 16)
                sp.dma_start(X["sy"][:, h * 32:h * 32 + 32], sy[h * 64:h * 64 + 64, :]).then_inc(s["spilled"], 16)
            sp.wait_ge(s["spilled"], 16 * (Q + 3))
            sp.dma_start(yrow[0:B, :], X["sy"].rearrange("(b h) v -> b (h v)", b=B)).then_inc(s["samp_in"], 16)
            gate_step(G_TILE - 1, (G_TILE - 1) % 2)
            with sp.Fori(0, NT - 1) as i:
                for q in range(2):
                    gate_step(i * 2 + (G_TILE + q), q)
            for k in range(N_GATE - 2, N_GATE):
                gate_step(k, k % 2, ahead=False)
            sp.wait_ge(s["fstate_ready"], 1)
            sp.dma_start(O["wkv_prompt"].rearrange("h v k -> v h k"), fst[0:64, :, :]).then_inc(s["out_done"], 16)

            for q in range(2):
                sp.wait_ge(s[f"gate_spill{q}"], 16 * (N_GATE // 2 + 1))
            gates = X["gates"].rearrange("(g c) p n -> c p g n", g=3)
            pa = I["p_a"].rearrange("(c p) n -> p c n", p=P)
            pm = I["p_m"].rearrange("(c p) n -> p c n", p=P)
            pbv = I["p_b"].rearrange("(e j p) n -> e p j n", e=2, p=64)
            with sp.Fori(0, KD // 2) as i:
                for q in range(2):
                    sp.wait_ge(s["merged"], i * 2 + q + 1)
                    sp.dma_start(mgg[q], gates[bass.ds(i * 2 + q, 1)].rearrange("c p g n -> (c p) g n")).then_inc(s[f"mgw{q}_in"], 16)
                    cols = bass.ds(i * (2 * P) + q * P, P)
                    sp.dma_start(mgw[q][:, 0:4, :], pa[:, :, cols]).then_inc(s[f"mgw{q}_in"], 16)
                    for e in range(2):
                        sp.dma_start(mgw[q][e * 64:e * 64 + 64, 4:8, :], pbv[e, :, :, cols]).then_inc(s[f"mgw{q}_in"], 16)
                    sp.dma_start(mgw[q][:, 8:10, :], pm[:, :, cols]).then_inc(s[f"mgw{q}_in"], 16)
            wov = I["w_o"].rearrange("(c p) n -> p c n", p=P)
            for h in range(2):
                sp.dma_start(wo[h], wov[:, :, h * 512:h * 512 + 512]).then_inc(s["out_in"], 16)
            sp.dma_start(wr, I["router_w"].rearrange("(p c) n -> p c n", c=KD)).then_inc(s["out_in"], 16)
            sp.dma_start(gb[:, 0, :], I["ln1_g"].partition_broadcast(P)).then_inc(s["out_in"], 16)
            sp.dma_start(gb[:, 1, :], I["ln1_b"].partition_broadcast(P)).then_inc(s["out_in"], 16)
            sp.wait_ge(s["merged"], KD + 2)
            sp.wait_ge(s["spilled"], 16 * Q)
            sp.dma_start(x1[:, 0:NT, :], X["x0"][0:T, :].rearrange("(t p) d -> p t d", p=P)).then_inc(s["xback_in"], 16)
            sp.dma_start(x1[0:B, NT, :], X["x0"][T:N, :]).then_inc(s["xback_in"], 16)
            wg = I["e_gate"].rearrange("e (p c) n -> e p c n", c=KD)
            wu = I["e_up"].rearrange("e (p c) n -> e p c n", c=KD)
            wd = I["e_down"].rearrange("e (p c) n -> e p c n", c=FF // P)
            sp.dma_start(eg[0], wg[0]).then_inc(s["ew0g_in"], 16)
            sp.dma_start(eu[0], wu[0]).then_inc(s["ew0u_in"], 16)
            sp.dma_start(ed[0], wd[0]).then_inc(s["ew0d_in"], 16)
            sp.dma_start(eg[1], wg[1]).then_inc(s["ew1g_in"], 16)
            for t in range(Q):
                sp.wait_ge(s["x_normed"], Q + t + 1)
                sp.dma_start(X["x1"][t * P:t * P + rows(t), :], x1[0:rows(t), t, :]).then_inc(s["x1_spilled"], 16)
            sp.wait_ge(s["x_normed"], 2 * Q)
            sp.dma_start(gb[:, 0, :], I["ln2_g"].partition_broadcast(P)).then_inc(s["ln2_in"], 16)
            sp.dma_start(gb[:, 1, :], I["ln2_b"].partition_broadcast(P)).then_inc(s["ln2_in"], 16)

            sp.wait_ge(s["h_made"], Q)
            sp.dma_start(eu[1], wu[1]).then_inc(s["ew1u_in"], 16)
            sp.dma_start(ed[1], wd[1]).then_inc(s["ew1d_in"], 16)

            def expert_load(e):
                return [w[bass.ds(e, 1)].rearrange("e p c n -> (e p) c n") for w in (wg, wu, wd)]

            def extra_load(i):
                e = sp.value_load(ovfi.bitcast(I32)[0:1, bass.ds(i, 1)], min_val=0, max_val=NE - 1)
                sp.wait_ge(s["y_mm"], i + (NE + 2))
                for w, dst, what in zip(expert_load(e), (eg[0], eu[0], ed[0]), "gud"):
                    sp.dma_start(dst, w).then_inc(s[f"ew0{what}_in"], 16)

            with sp.Fori(0, NE // 2 - 1) as i:
                for q in range(2):
                    e = i * 2 + (q + 2)
                    sp.wait_ge(s["gate_mm"], e + 1)
                    sp.dma_start(eg[q], wg[bass.ds(e, 1)].rearrange("e p c n -> (e p) c n")).then_inc(s[f"ew{q}g_in"], 16)
                    sp.wait_ge(s["up_mm"], e + 1)
                    sp.dma_start(eu[q], wu[bass.ds(e, 1)].rearrange("e p c n -> (e p) c n")).then_inc(s[f"ew{q}u_in"], 16)
                    sp.wait_ge(s["y_mm"], e + 1)
                    sp.dma_start(ed[q], wd[bass.ds(e, 1)].rearrange("e p c n -> (e p) c n")).then_inc(s[f"ew{q}d_in"], 16)
            extra_blocks(sp, extra_load)
            sp.wait_ge(s["ovf_step"], 1)
            ya = X["ya"].rearrange("(t k) d -> t k d", k=2)
            for t in range(Q):
                sp.dma_start(yk[0:rows(t), t, :, :], ya[t * P:t * P + rows(t), :, :]).then_inc(s[f"yk{t}_in"], 16)
            for t in range(Q):
                sp.wait_ge(s["x_normed"], 2 * Q + t + 1)
                dst = O["y_prompt"][t * P:(t + 1) * P, :] if t < NT else O["y_sample"]
                sp.dma_start(dst, x1[0:rows(t), t, :]).then_inc(s["out_done"], 16)
            sp.wait_ge(s["out_done"], 16 * (13 + Q))
            sp.wait_ge(s["x1_spilled"], 16 * Q)

        @block.tensor
        def _(pe):
            def mm(out, a, b, start=True, stop=True):
                return pe.matmul(out, a, b, start=start, stop=stop)

            def turn(out, a):
                n = a.shape[0]
                b = a.start_partition() if n < P else 0
                return pe.transpose(out, a, ident[b:b + n, b:b + n])

            def gate_tile(k, q, n, b):
                pe.wait_ge(s[f"p1w{q}_in"], n * 16 + (16 * NF + 16))
                for h in range(2):
                    for c in range(KD):
                        last = mm(bank(b + h, NH), gcol[q][:, c, :], xT[:, c, h * NH:(h + 1) * NH], c == 0, c == KD - 1)
                last.then_inc(s["gate_made"], 1)

            pe.sem_inc(s["z_made"], 2)
            pe.wait_ge(s["consts_in"], 16)
            def turn_x(t):
                n = rows(t)
                pe.wait_ge(s["x_normed"], t + 1)
                if t >= 2:
                    pe.wait_ge(s["xT_ready"], t - 1)
                for c in range(KD):
                    last = turn(bank(2 * (t % 2), KD, P)[:, c, 0:n], xtok[0:n, t, c::KD])
                last.then_inc(s["x_turned"], 1)

            pe.wait_ge(s["mem_in"], 32)
            for t in range(2):
                for c in range(KD):
                    last = turn(bank(4 + 2 * t, KD, P)[:, c, :], memtok[:, t, c::KD])
                last.then_inc(s["mem_turned"], 1)
            pe.wait_ge(s["memT_ready"], 2)
            for t in range(2):
                for c in range(KD):
                    last = mm(bank(4 + t, 512), memT[:, c, t * P:(t + 1) * P], wmem[:, c, :], c == 0, c == KD - 1)
                last.then_inc(s["mkv_made"], 1)
                for u in ((0, 1), (2, 3, 4))[t]:
                    turn_x(u)
            pe.wait_ge(s["mkv_ready"], 2)
            for f in range(2):
                for t in range(2):
                    last = turn(bank(6, 2, NMEM)[:, f, t * P:(t + 1) * P], mkv[:, t, f * P:(f + 1) * P])
            last.then_inc(s["mkv_made"], 1)
            pe.wait_ge(s["xT_ready"], Q)
            with pe.Fori(0, NF // 2) as i:
                for q in range(2):
                    pe.wait_ge(s[f"p1w{q}_in"], i * 32 + 32)
                    pe.wait_ge(s["z_ready"], i * 2 + q + 1)
                    for h in range(2):
                        for c in range(KD):
                            last = mm(bank(2 * q + h, NH), p1w[q][:, c, :], xT[:, c, h * NH:(h + 1) * NH], c == 0, c == KD - 1)
                    last.then_inc(s["z_made"], 1)
            pe.wait_ge(s["z_ready"], NF + 2)
            pe.wait_ge(s["mkT_ready"], 1)
            pe.wait_ge(s["params_in"], 80)
            turn(bank(7, PR_N), prow[0:PR_N, :]).then_inc(s["side_turned"], 1)
            for f in range(SF):
                last = turn(bank(0, C_SHIFT)[0:9, f * P:(f + 1) * P], z[:, f, T - 1:N])
            for f in range(SF):
                last = turn(bank(4, SF, B)[:, f, :], ssraw[0:B, f * P:(f + 1) * P])
            for t in range(NT):
                last = turn(bank(5, NT, P)[:, t, :], z[:, FV, t * P:(t + 1) * P])
            last = turn(bank(6, P)[0:B, :], z[:, FV, T:N])
            last.then_inc(s["side_turned"], 1)
            pe.wait_ge(s["side_ready"], SIDE_PARAMS)
            pe.wait_ge(s["side_ready"], SIDE_SHIFT)
            mm(bank(7, T), const("rot"), z[:, FK, 0:T])
            mm(bank(0, B), const("rot"), z[:, FK, T:N])
            mm(bank(1, NJ, B), const("rot"), z[:, FQ:FQ + NJ, T:N]).then_inc(s["rot_made"], 1)
            pe.wait_ge(s["kT_ready"], 1)
            turn(bank(2, P), kT[:, T:T + P])
            turn(bank(3, P)[0:B, :], kTs).then_inc(s["kout_turned"], 1)
            pe.wait_ge(s["kout_ready"], 1)
            pe.wait_ge(s["v_ready"], 1)

            with pe.Fori(0, NT) as i:
                pe.wait_ge(s["blk_out"], i + 1)
                mm(bank(6, NJ, P), const("rot"), z[:, FQ:FQ + NJ, bass.ds(i * P, P)]).then_inc(s["blk_rot"], 1)
                pe.wait_ge(s["blk_q"], i + 1)
                pe.wait_ge(s["blk_kv"], i + 1)
                for kv in range(2):
                    r = slice(kv * 64, kv * 64 + 64)
                    for j in range(NJ):
                        mm(bank(0, 12, 256)[:, kv * 4 + j, :], qs[r, j, :], kst[r, :])
                    for m in range(2):
                        last = mm(bank(0, 12, 256)[:, 8 + kv * 2 + m, :], qs[r, 4 + m, :], mkT[r, m, :])
                last.then_inc(s["blk_scores"], 1)
                gate_tile(i * 2, 0, i, 6)
                pe.wait_ge(s["gate_out"], i * 2 + 1)
                gate_tile(i * 2 + 1, 1, i, 6)
                pe.wait_ge(s["blk_prob"], i + 1)
                for g in range(24):
                    last = turn(bank(0, 24, P)[:, g, :], S[:, g // 2, (g % 2) * P:(g % 2) * P + P])
                last.then_inc(s["blk_turned"], 1)
                pe.wait_ge(s["blk_pT_act"], i + 1)
                pe.wait_ge(s["blk_pT_dve"], i + 1)
                pe.wait_ge(s["gate_out"], i * 2 + 2)
                for kv in range(2):
                    r = slice(kv * 64, kv * 64 + 64)
                    for j in range(NJ):
                        for k in range(2):
                            mm(bank(6, NJ, P)[r, j, :], vst[:, k, r], PT[:, (kv * 4 + j) * 2 + k, :], k == 0, k == 1)
                    for m in range(2):
                        for k in range(2):
                            last = mm(bank(7, 2, P)[r, m, :], mkv[:, k, 256 + (2 * m + kv) * 64:320 + (2 * m + kv) * 64],
                                      PT[:, (8 + kv * 2 + m) * 2 + k, :], k == 0, k == 1)
                last.then_inc(s["blk_mixed"], 1)
            pe.wait_ge(s["blk_out"], NT + 1)

            for k in range(G_CACHE, G_BONUS):
                gate_tile(k, k % 2, k // 2, 2 * (k % 2))
            pe.wait_ge(s["gate_out"], G_BONUS)
            pe.wait_ge(s["cache_in"], 96)
            def turn_keys(b):
                if b >= 2:
                    pe.wait_ge(s["sk_ready"], b - 1)
                kp = bank(2 * (b % 2), 5, P)
                turn(kp[:, 0, :], kwin[:, b, :])
                for f in range(2):
                    for t in range(2):
                        last = turn(kp[:, 1 + 2 * f + t, :], kmem[:, b, t, f * P:(f + 1) * P])
                last.then_inc(s["sk_turned"], 1)

            turn_keys(0)
            for b in range(B):
                if b + 1 < B:
                    turn_keys(b + 1)
                pe.wait_ge(s["sk_ready"], b + 1)
                kt = kTb[b % 2]
                for kv in range(2):
                    r = slice(kv * 64, kv * 64 + 64)
                    mm(bank(4 + kv, B, NJ)[:, b, :], kt[r, 0, :], qsS[r, 0:4, b])
                    for f in range(2):
                        for t in range(2):
                            last = mm(bank(6 + kv, 2, B, 2)[:, t, b, f:f + 1], kt[r, 1 + 2 * f + t, :], qsS[r, 4 + f, b:b + 1])
                last.then_inc(s["sk_scored"], 1)
            pe.wait_ge(s["sk_cols"], 1)
            turn(bank(0, P)[0:64, :], sST[:, 0:64])
            for t in range(2):
                last = turn(bank(1, 2, P)[0:32, t, :], sST[:, 64 + 32 * t:96 + 32 * t])
            last.then_inc(s["sk_rows"], 1)
            pe.wait_ge(s["sk_prob"], 1)
            turn(bank(2, 64), sW[0:64, :])
            for t in range(2):
                last = turn(bank(3, 2, 32)[:, t, :], sM[0:32, t, :])
            last.then_inc(s["sk_pT_made"], 1)
            pe.wait_ge(s["sk_pT_ready"], 1)
            for b in range(B):
                for kv in range(2):
                    r = slice(kv * 64, kv * 64 + 64)
                    mm(bank(4, B, NJ)[r, b, :], vwin[:, b, r], sWT[:, kv * 32 + b * 4:kv * 32 + b * 4 + 4])
                    for f in range(2):
                        for t in range(2):
                            last = mm(bank(5, B, 2)[r, b, f:f + 1], vmem[:, b, t, (2 * f + kv) * 64:(2 * f + kv) * 64 + 64],
                                      sMT[:, t, kv * 16 + b * 2 + f:kv * 16 + b * 2 + f + 1], t == 0, t == 1)
            last.then_inc(s["sk_mixed"], 1)

            pe.wait_ge(s["sk_done"], 1)
            pe.wait_ge(s["lora_in"], 48)
            pe.wait_ge(s["lora_act"], 1)
            n = 0
            for what in range(3):
                for j in range(NJ):
                    if n >= 2:
                        pe.wait_ge(s["lora_sig"], n - 1)
                    for h in range(2):
                        cols = slice(h * NH, (h + 1) * NH)
                        a, b_ = [(wup[0:64, j * P:(j + 1) * P], th[0:64, cols]),
                                 (wup[64:128, j * P:(j + 1) * P], xwa[64:128, cols]),
                                 (gup[:, j * P:(j + 1) * P], xg_[:, cols])][what]
                        last = mm(bank(2 * (n % 2) + h, NH), a, b_)
                    last.then_inc(s["lora_mm"], 1)
                    n += 1
            pe.wait_ge(s["kk_sq"], 1)
            for h in range(2):
                for j in range(NJ):
                    last = mm(bank(4 + h, NH)[0:HA, :], const("sel8", NJ, HA)[:, j, :], sqb[:, j, h * NH:(h + 1) * NH], j == 0, j == 3)
            last.then_inc(s["head_sum"], 1)
            pe.wait_ge(s["head_recip"], 1)
            for j in range(NJ):
                if j >= 1:
                    pe.wait_ge(s["prep_done"], j)
                for h in range(2):
                    last = mm(bank(4 + h, NH), const("sel8t", NJ, P)[0:HA, j, :], rn[0:HA, h * NH:(h + 1) * NH])
                last.then_inc(s["kk_bcast"], 1)
            pe.wait_ge(s["lora_sig"], 12)
            gate_tile(G_BONUS, G_BONUS % 2, G_BONUS // 2, 0)
            pe.wait_ge(s["bonus_in"], 1)
            for j in range(NJ):
                if j >= 1:
                    pe.wait_ge(s["prep_done"], NJ + j)
                for h in range(2):
                    last = mm(bank(6 + h, NH), const("bones"), sqb[:, j, h * NH:(h + 1) * NH])
                last.then_inc(s["bonus_mm"], 1)
            pe.wait_ge(s["samp_stack"], 2)
            pe.wait_ge(s["prep_done"], 2 * NJ)
            pe.wait_ge(s["gate_out"], G_SAMP)
            for q in range(6):
                for j in range(NJ):
                    last = turn(bank(0, 6, C_A)[0:B, q, j * P:(j + 1) * P], sstk[:, q, j, :])
            last.then_inc(s["side_turned"], 1)
            pe.wait_ge(s["side_ready"], SIDE_SAMP)
            for k in range(G_SAMP, G_TILE):
                if k >= G_SAMP + 2:
                    pe.wait_ge(s["gate_out"], k - 1)
                gate_tile(k, k % 2, k // 2, 2 * (k % 2))
            pe.wait_ge(s["gate_out"], G_TILE)
            pe.wait_ge(s["samp_in"], 80)
            for j in range(NJ):
                last = turn(bank(6, NJ, B)[:, j, :], yrow[0:B, j * P:(j + 1) * P])
            last.then_inc(s["side_turned"], 1)
            pe.wait_ge(s["side_ready"], SIDE_YSAMP)

            with pe.Fori(0, NT) as i:
                gate_tile(i * 2 + G_TILE, 0, i + G_TILE // 2, 4)
                pe.wait_ge(s["tile_ready"], i + 1)
                pe.wait_ge(s["y_ready"], i + 1)
                for q, src in enumerate((AR[:, :, 0, :], Bt, Kt, Vt)):
                    for j in range(NJ):
                        last = turn(bank(q, NJ, P)[:, j, :], src[:, j, :])
                last.then_inc(s["tm_turned"], 1)
                pe.wait_ge(s["gate_out"], i * 2 + (G_TILE + 1))
                pe.sem_inc(s["pace"], 1)
                for par in range(2):
                    r = slice(par * 64, par * 64 + 64)
                    for j in range(NJ):
                        last = mm(bank(4 + 2 * par, NJ, 2, P)[:, j, :, :], Bt[r, j, :], AR[r, j, :, :])
                last.then_inc(s["tri_made"], 1)
                pe.wait_ge(s["tm_ready"], i + 1)
                for par in range(2):
                    r = slice(par * 64, par * 64 + 64)
                    for j in range(NJ):
                        last = mm(bank(2 * par, NJ, 2, P)[:, j, :, :], Kt[r, j, :], AR[r, j, :, :])
                last.then_inc(s["tri_made"], 1)
                pe.wait_ge(s["tri_ready"], i * 2 + 1)
                for par in range(2):
                    r = slice(par * 64, par * 64 + 64)
                    for j in range(NJ):
                        last = mm(bank(4 + par, NJ, P)[:, j, :], AR[r, j, 0, :], Bt[r, j, :])
                last.then_inc(s["tri_made"], 1)
                gate_tile(i * 2 + (G_TILE + 1), 1, i + G_TILE // 2, 6)
                pe.wait_ge(s["nk_ready"], i + 1)
                pe.wait_ge(s["tri_ready"], i * 2 + 2)
                for k in range(5):
                    for g in range(2):
                        if k:
                            pe.wait_ge(s["lvl_x_ready"], i * 10 + 2 * (k - 1) + g + 1)
                        for j in range(NJ):
                            last = mm(bank(g, NJ, P)[:, j, :], MR[:, g * 4 + j, 0, :], XX[:, g * 4 + j, 0, :])
                        last.then_inc(s["lvl_t1"], 1)
                    for g in range(2):
                        pe.wait_ge(s["lvl_t1_ready"], i * 10 + 2 * k + g + 1)
                        for j in range(NJ):
                            h = g * 4 + j
                            if k < 4:
                                mm(bank(2 + g, NJ, P)[:, j, :], XX[:, h, 1, :], T1[:, h, :])
                            last = mm(bank(4 + g, NJ, P)[:, j, :], T1[:, h, :], XX[:, h, 1, :])
                        last.then_inc(s["lvl_x"], 1)
                pe.wait_ge(s["lvl_x_ready"], i * 10 + 10)
                pe.wait_ge(s["gate_out"], i * 2 + (G_TILE + 2))
                for h in range(HA):
                    hd = (h % 4) * 2 + h // 4
                    last = mm(bank(6, HA, 64)[:, h, :], NR[:, h, 0, :], Vtok[:, hd * 64:hd * 64 + 64])
                last.then_inc(s["nv_made"], 1)
                pe.wait_ge(s["nv_ready"], i + 1)
                for h in range(HA):
                    last = mm(bank(0, HA, P)[:, h, :], XX[:, h, 1, :], ANV[:, h, :, :])
                last.then_inc(s["xav_made"], 1)
                pe.wait_ge(s["xav_ready"], i + 1)
                pe.sem_inc(s["pace"], 1)
                for c in range(2):
                    t_ = slice(c * 64, c * 64 + 64)
                    for h in range(HA):
                        j, par = h % 4, h // 4
                        hd = j * 2 + par
                        r = slice(par * 64, par * 64 + 64)
                        f = slice(hd * 64, hd * 64 + 64)
                        o_ = bank(4 + c, NJ, 2, 64)
                        mm(o_[r, j, 0, :], XAV[t_, h, 0, :], Btok[t_, f])
                        mm(o_[r, j, 1, :], Btok[t_, f], XAV[t_, h, 1, :], True, False)
                        last = mm(o_[r, j, 1, :], Ktok[t_, f], Vtok[t_, f], False, True)
                last.then_inc(s["gh_made"], 1)
                for h in range(HA):
                    j, par = h % 4, h // 4
                    hd = j * 2 + par
                    r = slice(par * 64, par * 64 + 64)
                    mm(bank(2, NJ, P)[r, j, :], XAV[:, h, 0, :], MR[:, h, 1, :])
                    mm(bank(3, NJ, P)[r, j, :], XAV[:, h, 1, :], MR[:, h, 1, :], True, False)
                    last = mm(bank(3, NJ, P)[r, j, :], Vtok[:, hd * 64:hd * 64 + 64], NR[:, h, 1, :], False, True)
                last.then_inc(s["ry_made"], 1)
                pe.wait_ge(s["gh_ready"], i + 1)
                for c in range(2):
                    pe.wait_ge(s["chain_done"], i * 2 + c + 1)
                    pe.sem_inc(s["pace"], 1)
                    for par in range(2):
                        r = slice(par * 64, par * 64 + 64)
                        for j in range(NJ):
                            last = mm(bank(6 + par, NJ, 64)[r, j, :], GT[r, c, j, :], SR[r, c, j, :])
                    last.then_inc(s["chain_mm"], 1)
                pe.wait_ge(s["ry_ready"], i + 1)
                pe.sem_inc(s["pace"], 1)
                for par in range(2):
                    r = slice(par * 64, par * 64 + 64)
                    for j in range(NJ):
                        for c in range(2):
                            last = mm(bank(par, NJ, P)[r, j, c * 64:c * 64 + 64], SR[r, c, j, :], Rh[r, j, c * 64:c * 64 + 64])
                last.then_inc(s["y_made"], 1)
            pe.wait_ge(s["y_ready"], NT + 1)
            pe.wait_ge(s["chain_done"], 2 * NT + 1)
            for j in range(NJ):
                last = turn(bank(2, NJ, P)[0:64, j, :], SR[:, 0, j, :])
            last.then_inc(s["side_turned"], 1)
            for j in range(NJ):
                if j >= 2:
                    pe.wait_ge(s["gn_center"], j - 1)
                for h in range(2):
                    last = mm(bank(4 + 2 * (j % 2) + h, NH), const("bones"), YT[:, j, h * NH:(h + 1) * NH])
                last.then_inc(s["gn_mean"], 1)
            pe.wait_ge(s["gn_sq"], 1)
            for h in range(2):
                for j in range(NJ):
                    last = mm(bank(h, NH)[0:HA, :], const("sel8", NJ, HA)[:, j, :], sqb[:, j, h * NH:(h + 1) * NH], j == 0, j == 3)
            last.then_inc(s["head_sum"], 1)
            pe.wait_ge(s["head_recip"], 2)
            for j in range(NJ):
                if j >= 1:
                    pe.wait_ge(s["gn_bcast"], NT + j)
                for h in range(2):
                    last = mm(bank(4 + h, NH), const("sel8t", NJ, P)[0:HA, j, :], rn[0:HA, h * NH:(h + 1) * NH])
                last.then_inc(s["gn_mean"], 1)
            pe.wait_ge(s["oa_ready"], 1)

            branch = [(0, 4, lambda c: YT[:, c, :]), (4, 4, lambda c: z[:, FQ + c, :]), (8, 2, lambda c: z[:, FM + c, :])]
            with pe.Fori(0, KD // 2) as i:
                for q in range(2):
                    pe.wait_ge(s[f"mgw{q}_in"], i * 80 + 80)
                    for g in range(3):
                        par = (q * 3 + g) % 2
                        step = q * 3 + g
                        pe.wait_ge(s["proj_used"], i * 6 + step + 1)
                        w0, nk, act = branch[g]
                        for h in range(2):
                            for c in range(nk):
                                last = mm(bank(4 + 2 * par + h, NH), mgw[q][:, w0 + c, :], act(c)[:, h * NH:(h + 1) * NH], c == 0, c == nk - 1)
                        last.then_inc(s["proj_made"], 1)
            pe.wait_ge(s["merged"], KD + 2)
            pe.wait_ge(s["out_in"], 80)
            for t in range(Q + 2):
                if t < Q:
                    n = rows(t)
                    if t >= 2:
                        pe.wait_ge(s["h_used"], t - 1)
                    for h in range(2):
                        for c in range(KD):
                            last = mm(bank(2 * (t % 2) + h, 512)[0:n, :], MG[:, c, t * P:t * P + n], wo[h][:, c, :], c == 0, c == KD - 1)
                    last.then_inc(s["h_made"], 1)
                if t >= 2:
                    u = t - 2
                    n = rows(u)
                    pe.wait_ge(s["x_normed"], Q + u + 1)
                    for c in range(KD):
                        last = turn(bank(4, KD, P)[:, c, 0:n], x1[0:n, u, c::KD])
                    last.then_inc(s["x1_turned"], 1)
                    pe.wait_ge(s["x1T_ready"], u + 1)
                    for c in range(KD):
                        last = mm(bank(6, Q, NG + NE)[0:n, u, :], x1T[:, c, u * P:u * P + n], wr[:, c, :], c == 0, c == KD - 1)
            last.then_inc(s["logits_made"], 1)
            pe.wait_ge(s["onehot_ready"], 1)
            for t in range(Q):
                for u in range(t):
                    mm(bank(1, Q, NE)[:, t, :], const("ones"), Osum[:, u, :], u == 0, False)
                mm(bank(1, Q, NE)[:, t, :], const("before"), Osum[:, t, :], t == 0, True)
            for t in range(Q):
                last = mm(bank(2, NE), const("ones"), Osum[:, t, :], t == 0, t == Q - 1)
            last.then_inc(s["rank_made"], 1)
            pe.wait_ge(s["route_ready"], 1)
            for t in range(Q):
                for k in range(2):
                    last = mm(bank(3, 2, NB), SK[:, k, t, :], VB[:, t, k, :, :], t == 0 and k == 0, t == Q - 1 and k == 1)
            last.then_inc(s["table_made"], 1)
            pe.wait_ge(s["table_ready"], 1)
            pe.sem_inc(s["gate_mm"], 2)
            pe.sem_inc(s["up_mm"], 2)
            pe.sem_inc(s["y_mm"], 2)

            def turn_rows(q):
                for c in range(KD):
                    last = turn(bank(0, KD, P)[:, c, :], xg[q][:, c::KD])
                last.then_inc(s["xg_turned"], 1)

            def gate(q):
                for c in range(KD):
                    last = mm(bank(2, FF), xgT[:, c, :], eg[q][:, c, :], c == 0, c == KD - 1)
                last.then_inc(s["gate_mm"], 1)

            def up(q):
                for c in range(KD):
                    last = mm(bank(3, FF), xgT[:, c, :], eu[q][:, c, :], c == 0, c == KD - 1)
                last.then_inc(s["up_mm"], 1)

            def turn_h():
                for c in range(FF // P):
                    last = turn(bank(4, 4, P)[:, c, :], hb[:, c::4])
                last.then_inc(s["hT_turned"], 1)

            def down(q):
                for h in range(2):
                    for c in range(FF // P):
                        last = mm(bank(5 + h, 512), hT[:, c, :], ed[q][:, c, h * 512:h * 512 + 512], c == 0, c == 3)
                last.then_inc(s["y_mm"], 1)

            def rows_step(e, q, n):
                pe.wait_ge(s[f"xg_in_{'ab'[q]}"], n * 16 + 16)
                turn_rows(q)

            def gate_step(e, q, n, first=False):
                pe.wait_ge(s["xgT_ready"], e + 1)
                if not first:
                    pe.wait_ge(s["h_ready"], e)
                pe.wait_ge(s[f"ew{q}g_in"], n * 16 + 16)
                gate(q)

            def up_step(e, q, n):
                pe.wait_ge(s[f"ew{q}u_in"], n * 16 + 16)
                up(q)

            def turn_h_step(e, q, n):
                pe.wait_ge(s["h_ready"], e + 1)
                turn_h()

            def down_step(e, q, n):
                pe.wait_ge(s["hT_ready"], e + 1)
                pe.wait_ge(s[f"ew{q}d_in"], n * 16 + 16)
                pe.wait_ge(s["yb_ready"], e + 1)
                down(q)

            def steady(e, q, n, before, after):
                gate_step(e, q, n)
                turn_h_step(*before)
                up_step(e, q, n)
                if after:
                    rows_step(*after)
                down_step(*before)

            rows_step(0, 0, 0)
            gate_step(0, 0, 0, first=True)
            up_step(0, 0, 0)
            rows_step(1, 1, 0)
            with pe.Fori(0, NE // 2 - 1) as i:
                e = i * 2
                steady(e + 1, 1, i, (e, 0, i), (e + 2, 0, i + 1))
                steady(e + 2, 0, i + 1, (e + 1, 1, i), (e + 3, 1, i + 1))
            last_n = NE // 2 - 1
            steady(NE - 1, 1, last_n, (NE - 2, 0, last_n), None)
            turn_h_step(NE - 1, 1, last_n)
            down_step(NE - 1, 1, last_n)

            def extra(i):
                b = (i + NE, 0, i + NE // 2)
                rows_step(*b)
                gate_step(*b)
                up_step(*b)
                turn_h_step(*b)
                down_step(*b)

            extra_blocks(pe, extra)

        @block.scalar
        def _(act):
            def copy(out, a):
                return act.activation(out, a, ACT.Copy)

            def root(count, out, a, bias, scale=1.0):
                return act.activation(out, a, ACT.Sqrt, bias=bias, scale=scale)

            eps = const("eps")

            def layer_norm(x, pas, turned=None, between=None):
                for t in range(Q + 1):
                    if t < Q:
                        n = rows(t)
                        act.wait_ge(s["ln_stats"], pas * Q + t + 1)
                        act.activation(rstd[0:n, t, :], mv[0:n, t, 1:2], ACT.Sqrt, bias=eps[0:n, 0:1]).then_inc(s["ln_std"], 1)
                    if t >= 1:
                        u, n = t - 1, rows(t - 1)
                        act.wait_ge(s["ln_rs"], pas * Q + u + 1)
                        act.activation(x[0:n, u, :], x[0:n, u, :], ACT.Identity, bias=nmr[0:n, u, :],
                                       scale=rstd[0:n, u, :]).then_inc(s["ln_scaled"], 1)
                    if between and t == 2:
                        between()
                    if turned and t >= 2:
                        turned(t - 2)
                if turned:
                    turned(Q - 1)

            act.wait_ge(s["consts_in"], 16)

            def x_turned(t):
                n = rows(t)
                act.wait_ge(s["x_turned"], t + 1)
                copy(xT[:, :, t * P:t * P + n], bank(2 * (t % 2), KD, P)[:, :, 0:n]).then_inc(s["xT_ready"], 1)

            def mem_turned():
                for t in range(2):
                    act.wait_ge(s["mem_turned"], t + 1)
                    copy(memT[:, :, t * P:(t + 1) * P], bank(4 + 2 * t, KD, P)).then_inc(s["memT_ready"], 1)

            layer_norm(xtok, 0, between=mem_turned)
            for t in range(2):
                act.wait_ge(s["mkv_made"], t + 1)
                copy(mkv[:, t, :], bank(4 + t, 512)).then_inc(s["mkv_ready"], 1)
                for u in ((0, 1), (2, 3, 4))[t]:
                    x_turned(u)
            act.wait_ge(s["mkv_made"], 3)
            copy(mkT, bank(6, 2, NMEM)).then_inc(s["mkT_ready"], 1)
            act.sem_inc(s["z_ready"], 2)
            with act.Fori(0, NF // 2) as i:
                for q in range(2):
                    act.wait_ge(s["z_made"], i * 2 + q + 3)
                    copy(z[:, bass.ds(i * 2 + q, 1), :].rearrange("p a (h n) -> p (a h) n", h=2),
                         psum[:, 2 * q:2 * q + 2, 0:NH]).then_inc(s["z_ready"], 1)
            act.wait_ge(s["side_turned"], SIDE_PARAMS)
            copy(prm, bank(7, PR_N)).then_inc(s["side_ready"], 1)
            act.wait_ge(s["side_turned"], SIDE_SHIFT)
            copy(shb[0:9, :], bank(0, C_SHIFT)[0:9, :])
            copy(sstT, bank(4, SF, B)).then_inc(s["side_ready"], 1)
            copy(vtok[:, 1:, :], bank(5, NT, P))
            copy(vss[0:B, :], bank(6, P)[0:B, :]).then_inc(s["v_ready"], 1)
            act.wait_ge(s["kout_turned"], 1)
            copy(ktl, bank(2, P))
            copy(kss[0:B, :], bank(3, P)[0:B, :]).then_inc(s["kout_ready"], 1)

            def gate_take(k, q, n, b):
                act.wait_ge(s["gate_made"], k + 1)
                act.wait_ge(s[f"gate_spill{q}"], n * 16 + 16)
                copy(gout[q].rearrange("p (h n) -> p h n", h=2), psum[:, b:b + 2, 0:NH]).then_inc(s["gate_out"], 1)

            act.wait_ge(s["kT_ready"], 1)
            for q in range(2):
                act.sem_inc(s[f"gate_spill{q}"], 16)
            act.sem_inc(s["blk_out"], 1)
            with act.Fori(0, NT) as i:
                gate_take(i * 2, 0, i, 6)
                act.wait_ge(s["blk_max"], i + 1)
                for h in range(8):
                    act.activation(S[:, h, :], S[:, h, :], ACT.Exp, bias=nmx[:, h:h + 1], accum_out=den[:, h:h + 1])
                for h in range(8, 12):
                    act.activation(S[:, h, :], bank(0, 12, 256)[:, h, :], ACT.Exp, bias=nmx[:, h:h + 1], scale=0.125,
                                   accum_out=den[:, h:h + 1])
                act.activation(ske, ske, ACT.Exp).then_inc(s["blk_exp"], 1)
                gate_take(i * 2 + 1, 1, i, 6)
                act.wait_ge(s["blk_turned"], i + 1)
                copy(PT[:, 0:12, :], bank(0, 12, P)).then_inc(s["blk_pT_act"], 1)
                act.wait_ge(s["blk_mixed"], i + 1)
                cols = bass.ds(i * P, P)
                copy(z[:, FQ:FQ + NJ, cols], bank(6, NJ, P))
                copy(z[:, FM:FM + 2, cols], bank(7, 2, P)).then_inc(s["blk_out"], 1)

            for k in range(G_CACHE, G_BONUS):
                gate_take(k, k % 2, k // 2, 2 * (k % 2))

            for b in range(B):
                act.wait_ge(s["sk_turned"], b + 1)
                if b >= 2:
                    act.wait_ge(s["sk_scored"], b - 1)
                copy(kTb[b % 2], bank(2 * (b % 2), 5, P)).then_inc(s["sk_ready"], 1)
            act.wait_ge(s["sk_scored"], B)
            for kv in range(2):
                copy(sST[:, kv * 32:kv * 32 + 32], bank(4 + kv, 32))
                last = copy(sST[:, 64:128].rearrange("p (t k c) -> p t k c", t=2, k=2)[:, :, kv, :], bank(6 + kv, 2, 16))
            last.then_inc(s["sk_cols"], 1)
            act.wait_ge(s["sk_max"], 1)
            act.activation(sW[0:64, :], bank(0, P)[0:64, :], ACT.Exp, bias=snmx[0:64, 0:1], scale=0.125, accum_out=sden[0:64, 0:1])
            act.activation(sM[0:32, :, :], bank(1, 2, P)[0:32, :, :], ACT.Exp, bias=snmx[0:32, 1:2], scale=0.125,
                           accum_out=sden[0:32, 1:2])
            act.activation(sske[0:64, 0:1], sske[0:64, 0:1], ACT.Exp).then_inc(s["sk_exp"], 1)
            act.wait_ge(s["sk_pT_made"], 1)
            copy(sWT, bank(2, 64))
            copy(sMT, bank(3, 2, 32)).then_inc(s["sk_pT_ready"], 1)
            act.wait_ge(s["sk_mixed"], 1)
            copy(z[:, FQ:FQ + NJ, T:N], bank(4, B, NJ).rearrange("p b j -> p j b"))
            copy(z[:, FM:FM + 2, T:N], bank(5, B, 2).rearrange("p b j -> p j b")).then_inc(s["sk_done"], 1)

            act.wait_ge(s["zs_ready"], 1)
            act.activation(th[0:64, :], xwa[0:64, :], ACT.Tanh)
            act.activation(xg_, xg_, ACT.Sigmoid).then_inc(s["lora_act"], 1)
            n = 0
            for what in range(3):
                for j in range(NJ):
                    act.wait_ge(s["lora_mm"], n + 1)
                    src = psum[:, 2 * (n % 2):2 * (n % 2) + 2, 0:NH]
                    dst = (sg, ah, gT)[what][:, j, :].rearrange("p (h n) -> p h n", h=2)
                    if what < 2:
                        r0 = (PR_W0, PR_A0)[what] + j
                        last = act.activation(dst, src, ACT.Sigmoid, bias=prm[:, r0:r0 + 1])
                    else:
                        last = copy(dst, src)
                    last.then_inc(s["lora_sig"], 1)
                    n += 1
            for j in range(NJ):
                last = act.activation(sqb[:, j, :], kTr[:, j, :], ACT.Square, scale=prm[:, PR_KK + j:PR_KK + j + 1])
            last.then_inc(s["kk_sq"], 1)
            act.wait_ge(s["head_sum"], 1)
            act.activation(rn[0:HA, :].rearrange("p (h n) -> p h n", h=2), psum[0:HA, 4:6, 0:NH], ACT.Sqrt).then_inc(s["head_root"], 1)
            act.drain()
            act.activation(wS, sg[:, :, T:N], ACT.Exp, scale=-DECAY).then_inc(s["samp_stack"], 1)
            gate_take(G_BONUS, G_BONUS % 2, G_BONUS // 2, 0)
            act.wait_ge(s["side_turned"], SIDE_SAMP)
            copy(srow[0:B, :, :], bank(0, 6, C_A)[0:B, :, :]).then_inc(s["side_ready"], 1)
            for k in range(G_SAMP, G_TILE):
                gate_take(k, k % 2, k // 2, 2 * (k % 2))
            act.wait_ge(s["side_turned"], SIDE_YSAMP)
            copy(YT[:, :, T:N], bank(6, NJ, B)).then_inc(s["side_ready"], 1)

            act.wait_ge(s["prep_done"], 2 * NJ + 1)
            with act.Fori(0, NT) as i:
                cols = bass.ds(i * P, P)
                act.wait_ge(s["y_ready"], i + 1)
                act.wait_ge(s["gn_bcast"], i + 1)
                act.activation(Pinc, Lc[:, :, cols], ACT.Exp, scale=-DECAY)
                act.activation(Pinv, Lc[:, :, cols], ACT.Exp, scale=DECAY)
                act.activation(Pexc, Pexc, ACT.Exp, scale=-DECAY).then_inc(s["exps_made"], 1)
                gate_take(i * 2 + G_TILE, 0, i + G_TILE // 2, 4)
                act.wait_ge(s["tm_turned"], i + 1)
                copy(ANV[:, :, 0, :].rearrange("p (e j) k -> p e j k", e=2),
                     bank(0, NJ, 2, 64).rearrange("p j e k -> p e j k"))
                copy(Btok, bank(1, 512))
                copy(Ktok, bank(2, 512))
                copy(Vtok, bank(3, 512)).then_inc(s["tm_ready"], 1)
                gate_take(i * 2 + (G_TILE + 1), 1, i + G_TILE // 2, 6)
                act.wait_ge(s["nv_made"], i + 1)
                copy(ANV[:, :, 1, :], bank(6, HA, 64)).then_inc(s["nv_ready"], 1)
                act.wait_ge(s["xav_made"], i + 1)
                copy(XAV, bank(0, HA, 2, 64)).then_inc(s["xav_ready"], 1)
                act.wait_ge(s["ry_made"], i + 1)
                copy(Yl, bank(3, NJ, P)).then_inc(s["ry_ready"], 1)
            act.wait_ge(s["side_turned"], SIDE_STATE)
            copy(fst[0:64, :, :], bank(2, HA, 64)[0:64, :, :]).then_inc(s["fstate_ready"], 1)
            act.wait_ge(s["gn_sq"], 1)
            act.wait_ge(s["head_sum"], 2)
            act.activation(rn[0:HA, :].rearrange("p (h n) -> p h n", h=2), psum[0:HA, 0:2, 0:NH], ACT.Sqrt,
                           scale=1.0 / 64, bias=eps[0:HA, 1:2]).then_inc(s["head_root"], 1)

            with act.Fori(0, KD // 2) as i:
                for q in range(2):
                    act.wait_ge(s[f"mgw{q}_in"], i * 80 + 80)
                    act.activation(mgg[q], mgg[q], ACT.Sigmoid).then_inc(s["gate_sig"], 1)

            def x1_turned(t):
                n = rows(t)
                act.wait_ge(s["x1_turned"], t + 1)
                copy(x1T[:, :, t * P:t * P + n], bank(4, KD, P)[:, :, 0:n]).then_inc(s["x1T_ready"], 1)

            layer_norm(x1, 1, x1_turned)
            act.wait_ge(s["gexp_in"], 1)
            act.activation(t4, t4, ACT.Exp).then_inc(s["gexp"], 1)
            act.wait_ge(s["e2_in"], 1)
            act.activation(e2, e2, ACT.Exp).then_inc(s["e2_out"], 1)

            act.wait_ge(s["table_ready"], 1)
            def turned_rows(e):
                act.wait_ge(s["xg_turned"], e + 1)
                copy(xgT, bank(0, KD, P)).then_inc(s["xgT_ready"], 1)

            def gate_sigmoid(e):
                act.wait_ge(s["gate_mm"], e + 3)
                act.activation(esig, bank(2, FF), ACT.Sigmoid).then_inc(s["gate_act"], 1)

            turned_rows(0)
            with act.Fori(0, NE - 1) as e:
                gate_sigmoid(e)
                act.wait_ge(s["up_mm"], e + 3)
                turned_rows(e + 1)
            gate_sigmoid(NE - 1)

            def extra_act(i):
                turned_rows(i + NE)
                gate_sigmoid(i + NE)

            extra_blocks(act, extra_act)
            layer_norm(x1, 2)

        @block.vector
        def _(v):
            tab, ix = tabi.bitcast(U32), idx.bitcast(U32)

            def tt(out, a, b, op):
                return v.tensor_tensor(out, a, b, op)

            def stt(out, a, sc, b, op0, op1):
                return v.scalar_tensor_tensor(out, a, sc, b, op0, op1)

            def ts(out, a, s1, op0, s2=None, op1=None):
                if op1 is None:
                    return v.tensor_scalar(out, a, s1, None, op0)
                return v.tensor_scalar(out, a, s1, s2, op0, op1)

            def layer_norm(x, pas, before):
                for t in range(Q + 2):
                    if t < Q:
                        n = rows(t)
                        before(t)
                        for h in range(2):
                            v.bn_stats(st6[0:n, t, h, :], x[0:n, t, h * 512:(h + 1) * 512])
                        v.drain()
                        v.bn_aggr(mv[0:n, t, :], st6[0:n, t, :, :]).then_inc(s["ln_stats"], 1)
                    if 1 <= t <= Q:
                        u, n = t - 1, rows(t - 1)
                        v.wait_ge(s["ln_std"], pas * Q + u + 1)
                        v.reciprocal(rstd[0:n, u, :], rstd[0:n, u, :])
                        v.drain()
                        stt(nmr[0:n, u, :], mv[0:n, u, 0:1], -1.0, rstd[0:n, u, :], ALU.mult, ALU.mult).then_inc(s["ln_rs"], 1)
                    if t >= 2:
                        u, n = t - 2, rows(t - 2)
                        v.wait_ge(s["ln_scaled"], pas * Q + u + 1)
                        tt(x[0:n, u, :], x[0:n, u, :], gb[0:n, 0, :], ALU.mult).then_inc(s["ln_gained"], 1)

            v.wait_ge(s["x_in"], 64)
            layer_norm(xtok, 0, lambda t: None)

            v.wait_ge(s["mkT_ready"], 1)
            v.memset(kT[:, 0:P], 0.0)
            v.memset(vtok[:, 0, :], 0.0)
            v.wait_ge(s["z_ready"], NF + 2)
            cos, sin = const("cos"), const("sin")
            v.wait_ge(s["rot_made"], 1)
            v.wait_ge(s["spilled"], 16 * Q)
            tt(kT[:, P:], z[:, FK, 0:T], cos[:, 0:T], ALU.mult)
            tt(view(Fo, T), bank(7, T), sin[:, 0:T], ALU.mult)
            tt(kTs, z[:, FK, T:N], cos[:, T:N], ALU.mult)
            tt(view(Fo + 512, B), bank(0, B), sin[:, T:N], ALU.mult)
            tt(qsS[:, 0:4, :], z[:, FQ:FQ + NJ, T:N], bc(cos[:, T:N], 1, NJ), ALU.mult)
            tt(view(Fo + 520, NJ, B), bank(1, NJ, B), bc(sin[:, T:N], 1, NJ), ALU.mult)
            v.tensor_copy(qsS[:, 4:6, :], z[:, FM:FM + 2, T:N])
            v.drain()
            tt(kT[:, P:], kT[:, P:], view(Fo, T), ALU.add)
            tt(qsS[:, 0:4, :], qsS[:, 0:4, :], view(Fo + 520, NJ, B), ALU.add)
            tt(kTs, kTs, view(Fo + 512, B), ALU.add).then_inc(s["kT_ready"], 1)

            v.wait_ge(s["side_ready"], SIDE_SHIFT)
            tt(zs[:, :, 1:T], z[:, 0:SF, 0:T - 1], z[:, 0:SF, 1:T], ALU.subtract)
            ts(zs[:, :, 0:1], z[:, 0:SF, 0:1], -1.0, ALU.mult)
            tt(zs[:, :, T:N], sstT, z[:, 0:SF, T:N], ALU.subtract)
            v.drain()
            for f in range(SF):
                last = stt(zs[:, f, :], zs[:, f, :], prm[:, PR_MU + f:PR_MU + f + 1], z[:, f, :], ALU.mult, ALU.add)
            last.then_inc(s["zs_ready"], 1)

            v.wait_ge(s["params_in"], 80)
            v.wait_ge(s["mkv_made"], 2)
            with v.Fori(0, NT) as i:
                cols = bass.ds(i * P, P)
                v.wait_ge(s["blk_rot"], i + 1)
                tt(qs[:, 0:4, :], z[:, FQ:FQ + NJ, cols], bc(cos[:, cols], 1, NJ), ALU.mult)
                tt(tmpq, bank(6, NJ, P), bc(sin[:, cols], 1, NJ), ALU.mult)
                v.tensor_copy(qs[:, 4:6, :], z[:, FM:FM + 2, cols])
                v.drain()
                tt(qs[:, 0:4, :], qs[:, 0:4, :], tmpq, ALU.add).then_inc(s["blk_q"], 1)
                v.wait_ge(s["blk_scores"], i + 1)
                v.wait_ge(s["blk_kv"], i + 1)
                stt(S[:, 0:8, :], bank(0, 8, 256), 0.125, bc(mst, 1, 8), ALU.mult, ALU.add)
                v.tensor_reduce(mx[:, 8:12], bank(4, 4, 256), AX.X, ALU.max)
                v.drain()
                v.tensor_reduce(mx[:, 0:8], S[:, 0:8, :], AX.X, ALU.max)
                ts(nmx[:, 8:12], mx[:, 8:12], -0.125, ALU.mult)
                v.drain()
                tt(mx[:, 0:8], mx[:, 0:8], sink_bc, ALU.max)
                v.drain()
                ts(nmx[:, 0:8], mx[:, 0:8], -1.0, ALU.mult)
                v.drain()
                tt(ske, sink_bc, nmx[:, 0:8], ALU.add).then_inc(s["blk_max"], 1)
                v.wait_ge(s["blk_exp"], i + 1)
                tt(den[:, 0:8], den[:, 0:8], ske, ALU.add)
                v.drain()
                v.reciprocal(rden, den)
                v.drain()
                tt(S, S, bc(rden, 2, 256), ALU.mult).then_inc(s["blk_prob"], 1)
                v.wait_ge(s["blk_turned"], i + 1)
                v.tensor_copy(PT[:, 12:24, :], bank(3, 12, P)).then_inc(s["blk_pT_dve"], 1)

            v.wait_ge(s["sk_rows"], 1)
            v.tensor_reduce(smx[0:64, 0:1], bank(0, P)[0:64, :], AX.X, ALU.max)
            v.tensor_reduce(smx[0:32, 1:2], bank(1, 2 * P)[0:32, :], AX.X, ALU.max)
            v.drain()
            ts(smx[0:64, 0:1], smx[0:64, 0:1], 0.125, ALU.mult)
            ts(snmx[0:32, 1:2], smx[0:32, 1:2], -0.125, ALU.mult)
            v.drain()
            tt(smx[0:64, 0:1], smx[0:64, 0:1], sink_row[0:64, :], ALU.max)
            v.drain()
            ts(snmx[0:64, 0:1], smx[0:64, 0:1], -1.0, ALU.mult)
            v.drain()
            tt(sske[0:64, 0:1], sink_row[0:64, :], snmx[0:64, 0:1], ALU.add).then_inc(s["sk_max"], 1)
            v.wait_ge(s["sk_exp"], 1)
            tt(sden[0:64, 0:1], sden[0:64, 0:1], sske[0:64, 0:1], ALU.add)
            v.drain()
            v.reciprocal(srd[0:64, 0:1], sden[0:64, 0:1])
            v.reciprocal(srd[0:32, 1:2], sden[0:32, 1:2])
            v.drain()
            ts(sW[0:64, :], sW[0:64, :], srd[0:64, 0:1], ALU.mult)
            ts(sM[0:32, :, :], sM[0:32, :, :], srd[0:32, 1:2], ALU.mult).then_inc(s["sk_prob"], 1)

            def pcol(r0, j):
                return prm[:, r0 + j:r0 + j + 1]

            def halves(ap):
                return ap.rearrange("p (h n) -> p h n", h=2)

            v.wait_ge(s["head_root"], 1)
            ts(rn[0:HA, :], rn[0:HA, :], 1e-12, ALU.max)
            v.drain()
            v.reciprocal(rn[0:HA, :], rn[0:HA, :]).then_inc(s["head_recip"], 1)
            for j in range(NJ):
                v.wait_ge(s["kk_bcast"], j + 1)
                stt(halves(kk[:, j, :]), halves(kTr[:, j, :]), pcol(PR_KK, j), psum[:, 4:6, 0:NH], ALU.mult, ALU.mult).then_inc(s["prep_done"], 1)
            v.wait_ge(s["lora_sig"], 8)
            for j in range(NJ):
                ts(sqb[:, j, :], ah[:, j, :], 1.0, ALU.subtract, pcol(PR_KA, j), ALU.mult)
            v.drain()
            tt(ah, kk, ah, ALU.mult)
            stt(kTr, sqb, 1.0, kTr, ALU.add, ALU.mult)
            v.drain()
            for j in range(NJ):
                last = stt(sqb[:, j, :], rT[:, j, :], pcol(PR_RK, j), kTr[:, j, :], ALU.mult, ALU.mult)
            last.then_inc(s["bonus_in"], 1)
            for j in range(NJ):
                v.wait_ge(s["bonus_mm"], j + 1)
                tt(halves(BV[:, j, :]), halves(vT[:, j, :]), psum[:, 6:8, 0:NH], ALU.mult).then_inc(s["prep_done"], 1)
            v.wait_ge(s["samp_stack"], 1)
            ts(sstk[:, 0, :, :], kk[:, :, T:N], -1.0, ALU.mult)
            v.tensor_copy(sstk[:, 1, :, :], wS)
            v.tensor_copy(sstk[:, 2, :, :], kTr[:, :, T:N])
            v.tensor_copy(sstk[:, 3, :, :], vT[:, :, T:N])
            v.tensor_copy(sstk[:, 4, :, :], ah[:, :, T:N])
            v.tensor_copy(sstk[:, 5, :, :], rT[:, :, T:N]).then_inc(s["samp_stack"], 1)
            for j in range(NJ):
                v.tensor_tensor_scan(Lc[:, j, :], const("reset"), sg[:, j, 0:T], 0.0, ALU.mult, ALU.add)
            v.memset(SR[:, 0, :, :], 0.0)
            v.drain()
            v.sem_inc(s["prep_done"], 1)
            v.wait_ge(s["samp_in"], 64)
            v.wait_ge(s["state_in"], 32)

            def key(q):
                return bc(vec[:, q, :], 1, 32)

            tt(sTmp, sS, key(0), ALU.mult)
            v.drain()
            v.tensor_reduce(sa, sTmp, AX.X, ALU.add)
            tt(sS, sS, key(1), ALU.mult)
            v.drain()
            tt(sTmp, key(4), bc(sa, 2, 64), ALU.mult)
            v.drain()
            tt(sS, sS, sTmp, ALU.add)
            v.drain()
            tt(sTmp, key(2), bc(vvh, 2, 64), ALU.mult)
            v.drain()
            tt(sS, sS, sTmp, ALU.add)
            v.drain()
            tt(sTmp, sS, key(5), ALU.mult)
            v.drain()
            v.tensor_reduce(sy, sTmp, AX.X, ALU.add).then_inc(s["samp_state"], 1)
            v.wait_ge(s["side_turned"], SIDE_YSAMP)
            v.wait_ge(s["out_done"], 16 * 12)

            v.sem_inc(s["y_ready"], 1)
            v.sem_inc(s["chain_done"], 1)
            up2, lows = const("upper2", 2, P), [const(f"level{k}") for k in range(1, 6)]
            with v.Fori(0, NT) as i:
                cols = bass.ds(i * P, P)
                tt(Pexc, Lc[:, :, cols], sg[:, :, cols], ALU.subtract).then_inc(s["gn_bcast"], 1)
                v.wait_ge(s["exps_made"], i + 1)
                stt(AR[:, :, 0, :], kk[:, :, cols], -1.0, Pexc, ALU.mult, ALU.mult)
                tt(AR[:, :, 1, :], rT[:, :, cols], Pinc, ALU.mult)
                tt(Bt, ah[:, :, cols], Pinv, ALU.mult)
                tt(Kt, kTr[:, :, cols], Pinv, ALU.mult)
                v.tensor_copy(pc2, Pinc.rearrange("p j (c n) -> p c j n", c=2)[:, :, :, CH - 1])
                v.tensor_copy(Vt, vT[:, :, cols]).then_inc(s["tile_ready"], 1)
                v.wait_ge(s["tri_made"], i * 3 + 1)
                tt(MR, bank(4, HA, 2, P), bc(up2, 1, HA), ALU.mult).then_inc(s["tri_ready"], 1)
                v.wait_ge(s["tri_made"], i * 3 + 2)
                tt(NR, bank(0, HA, 2, P), bc(up2, 1, HA), ALU.mult).then_inc(s["nk_ready"], 1)
                v.wait_ge(s["tri_made"], i * 3 + 3)
                for par in range(2):
                    tt(XX[:, par * 4:par * 4 + 4, 0, :], bank(4 + par, NJ, P), bc(const("low1"), 1, NJ), ALU.mult)
                tt(XX[:, :, 1, :], MR[:, :, 0, :], bc(const("up1"), 1, HA), ALU.mult)
                v.drain()
                tt(XX, XX, bc(bc(ident, 1, 2), 1, HA), ALU.add).then_inc(s["tri_ready"], 1)
                for k in range(5):
                    for g in range(2):
                        v.wait_ge(s["lvl_t1"], i * 10 + 2 * k + g + 1)
                        tt(T1[:, g * 4:g * 4 + 4, :], bank(g, NJ, P), bc(lows[k], 1, NJ), ALU.mult).then_inc(s["lvl_t1_ready"], 1)
                    for g in range(2):
                        v.wait_ge(s["lvl_x"], i * 10 + 2 * k + g + 1)
                        h = slice(g * 4, g * 4 + 4)
                        if k < 4:
                            tt(XX[:, h, 0, :], XX[:, h, 0, :], bank(2 + g, NJ, P), ALU.add)
                        tt(XX[:, h, 1, :], XX[:, h, 1, :], bank(4 + g, NJ, P), ALU.add).then_inc(s["lvl_x_ready"], 1)
                v.wait_ge(s["gh_made"], i + 1)
                for c in range(2):
                    for r in (slice(0, 64), slice(64, 128)):
                        tt(GT[r, c, :, :], bank(4 + c, NJ, 2, 64)[r, :, 0, :], bc(ident[r, r], 1, NJ), ALU.add)
                    last = v.tensor_copy(Hm[:, c, :, :], bank(4 + c, NJ, 2, 64)[:, :, 1, :])
                last.then_inc(s["gh_ready"], 1)
                v.wait_ge(s["ry_made"], i + 1)
                tt(Rh, bank(2, NJ, P), AR[:, :, 1, :], ALU.add)
                for c in range(2):
                    v.wait_ge(s["chain_mm"], i * 2 + c + 1)
                    for par in range(2):
                        r = slice(par * 64, par * 64 + 64)
                        tt(SR[r, c + 1, :, :], bank(6 + par, NJ, 64)[r, :, :], Hm[r, c, :, :], ALU.add)
                    v.drain()
                    last = tt(SR[:, c + 1, :, :], SR[:, c + 1, :, :], bc(pc2[:, c, :], 2, 64), ALU.mult)
                    if c == 0:
                        last.then_inc(s["chain_done"], 1)
                v.wait_ge(s["y_made"], i + 1)
                v.wait_ge(s["ry_ready"], i + 1)
                for par in range(2):
                    r = slice(par * 64, par * 64 + 64)
                    tt(YT[r, :, cols], bank(par, NJ, P)[r, :, :], Yl[r, :, :], ALU.add)
                v.drain()
                v.sem_inc(s["y_ready"], 1)
                v.tensor_copy(SR[:, 0, :, :], SR[:, 2, :, :]).then_inc(s["chain_done"], 1)

            v.drain()
            v.sem_inc(s["merged"], 2)

            v.wait_ge(s["side_ready"], SIDE_YSAMP)
            v.wait_ge(s["side_turned"], SIDE_STATE)
            v.drain()
            for j in range(NJ):
                v.wait_ge(s["gn_mean"], j + 1)
                stt(halves(YT[:, j, :]), psum[:, 4 + 2 * (j % 2):6 + 2 * (j % 2), 0:NH], -1.0 / 64, halves(YT[:, j, :]),
                    ALU.mult, ALU.add).then_inc(s["gn_center"], 1)
            v.drain()
            tt(sqb, YT, YT, ALU.mult).then_inc(s["gn_sq"], 1)
            v.wait_ge(s["head_root"], 2)
            v.reciprocal(rn[0:HA, :], rn[0:HA, :]).then_inc(s["head_recip"], 1)
            for j in range(NJ):
                v.wait_ge(s["gn_mean"], NJ + j + 1)
                tt(halves(YT[:, j, :]), halves(YT[:, j, :]), psum[:, 4:6, 0:NH], ALU.mult).then_inc(s["gn_bcast"], 1)
                v.drain()
                ts(YT[:, j, :], YT[:, j, :], pcol(PR_LG, j), ALU.mult, pcol(PR_LB, j), ALU.add)
            v.drain()
            tt(YT, YT, BV, ALU.add)
            v.drain()
            tt(YT, YT, gT, ALU.mult).then_inc(s["oa_ready"], 1)

            v.drain()
            v.sem_inc(s["proj_used"], 2)
            with v.Fori(0, KD // 2) as i:
                for q in range(2):
                    dst = MG[:, bass.ds(i * 2 + q, 1), :].rearrange("p a (h n) -> p (a h) n", h=2)
                    v.wait_ge(s["gate_sig"], i * 2 + q + 1)
                    for g in range(3):
                        step = q * 3 + g
                        v.wait_ge(s["proj_made"], i * 6 + step + 1)
                        pj = psum[:, 4 + 2 * (step % 2):6 + 2 * (step % 2), 0:NH]
                        if g == 0:
                            tt(dst, halves(mgg[q][:, g, :]), pj, ALU.mult).then_inc(s["proj_used"], 1)
                        else:
                            tt(halves(ptmp), halves(mgg[q][:, g, :]), pj, ALU.mult).then_inc(s["proj_used"], 1)
                            v.drain()
                            last = tt(dst, dst, halves(ptmp), ALU.add)
                            v.drain()
                    v.sem_inc(s["merged"], 1)

            v.wait_ge(s["xback_in"], 32)
            v.wait_ge(s["out_in"], 80)

            def residual(t):
                n = rows(t)
                v.wait_ge(s["h_made"], t + 1)
                stt(x1[0:n, t, :], x1[0:n, t, :], ALPHA, bank(2 * (t % 2), D)[0:n, :], ALU.mult, ALU.add).then_inc(s["h_used"], 1)
                v.drain()

            layer_norm(x1, 1, residual)

            v.memset(LG, 0.0)
            v.drain()
            v.wait_ge(s["logits_made"], 1)
            lgp = bank(6, Q, NG + NE)
            tt(LG[:, 0:NT, :], lgp[:, 0:NT, :], bc(rb, 1, NT), ALU.add)
            tt(LG[0:B, NT, :], lgp[0:B, NT, :], rb[0:B, :], ALU.add)
            v.drain()
            iota = const("iota")

            def last1(ap, n):
                return ap.to_broadcast(list(ap.shape[:-1]) + [n])

            def first_max(vals, top, eq, cand, pos, onehot, n):
                v.tensor_reduce(top, vals, AX.X, ALU.max)
                v.drain()
                tt(eq, vals, last1(top, n), ALU.is_equal)
                v.drain()
                stt(cand, eq, -1000.0, bc(iota[:, 0:n], 1, Q), ALU.mult, ALU.add)
                v.drain()
                v.tensor_reduce(pos, cand, AX.X, ALU.min)
                v.drain()
                tt(onehot, cand, last1(pos, n), ALU.is_equal)
                v.drain()

            gl, er = LG[:, :, 0:NG], LG[:, :, NG:]
            first_max(gl, g1, eq4, c4, i1, oh4, NG)
            tt(t4, gl, last1(g1, NG), ALU.subtract).then_inc(s["gexp_in"], 1)
            ts(c4, oh4, 1.0, ALU.subtract, BIG, ALU.mult)
            tt(el.rearrange("p t (g e) -> p t g e", g=NG), er.rearrange("p t (g e) -> p t g e", g=NG), bc(oh4, 3, EPG), ALU.mult)
            v.drain()
            tt(el.rearrange("p t (g e) -> p t g e", g=NG), el.rearrange("p t (g e) -> p t g e", g=NG), bc(c4, 3, EPG), ALU.add)
            v.drain()
            first_max(el, v1, eqx, cx, i1, OH[:, 0, :, :], NE)
            stt(el, OH[:, 0, :, :], -2.0 * BIG, el, ALU.mult, ALU.add)
            v.drain()
            first_max(el, v2, eqx, cx, i1, OH[:, 1, :, :], NE)
            tt(e2, v2, v1, ALU.subtract).then_inc(s["e2_in"], 1)
            tt(OH, OH, bc(last1(const("valid", Q, 1), NE), 1, 2), ALU.mult)
            v.drain()
            tt(Osum, OH[:, 0, :, :], OH[:, 1, :, :], ALU.add).then_inc(s["onehot_ready"], 1)
            v.wait_ge(s["gexp"], 1)
            v.tensor_reduce(gd, t4, AX.X, ALU.add)
            v.wait_ge(s["e2_out"], 1)
            ts(rden2, e2, 1.0, ALU.add)
            v.drain()
            tt(gd, gd, rden2, ALU.mult)
            v.drain()
            v.reciprocal(pgate[:, 0, :, :], gd)
            v.drain()
            tt(pgate[:, 1, :, :], pgate[:, 0, :, :], e2, ALU.mult)
            v.wait_ge(s["rank_made"], 1)
            v.tensor_copy(rank, bank(1, Q, NE))
            v.tensor_copy(cnt, bank(2, NE))
            v.drain()
            ts(qb, rank, float(P), ALU.is_ge)
            ts(nx, cnt, float(P), ALU.is_gt)
            v.drain()
            for q in range(2, 5):
                stt(qb, rank, float(P * q), qb, ALU.is_ge, ALU.add)
                stt(nx, cnt, float(P * q), nx, ALU.is_gt, ALU.add)
                v.drain()
            v.tensor_tensor_scan(incl, const("ones")[:, 0:NE], nx, 0.0, ALU.mult, ALU.add)
            stt(rank, qb, -float(P), rank, ALU.mult, ALU.add)
            ts(blk, qb, 0.0, ALU.is_gt)
            v.drain()
            tt(osx, incl, nx, ALU.subtract)
            v.drain()
            stt(dov, osx, float(NE - 1), iota[:, 0:NE], ALU.add, ALU.subtract)
            v.drain()
            tt(blk, blk, bc(dov, 1, Q), ALU.mult)
            v.drain()
            tt(blk, blk, qb, ALU.add)
            v.drain()
            tt(blk, blk, bc(iota[:, 0:NE], 1, Q), ALU.add)
            v.drain()
            for k in range(2):
                tt(el, OH[:, k, :, :], blk, ALU.mult)
                tt(cx, OH[:, k, :, :], rank, ALU.mult)
                v.drain()
                v.tensor_reduce(bk[:, k, :, :], el, AX.X, ALU.add)
                v.tensor_reduce(sk[:, k, :, :], cx, AX.X, ALU.add)
                v.drain()
            asg = const("asg1", Q, 2)
            for k in range(2):
                tt(SK[:, k, :, :], bc(iota, 1, Q), last1(sk[:, k, :, :], P), ALU.is_equal)
                tt(VB[:, :, k, 1, :], bc(iota[:, 0:NB], 1, Q), last1(bk[:, k, :, :], NB), ALU.is_equal)
                v.drain()
                tt(VB[:, :, k, 1, :], VB[:, :, k, 1, :], last1(const("valid", Q, 1), NB), ALU.mult)
                v.drain()
                tt(VB[:, :, k, 0, :], VB[:, :, k, 1, :], last1(asg[:, :, k:k + 1], NB), ALU.mult)
                v.drain()
                tt(VB[:, :, k, 1, :], VB[:, :, k, 1, :], last1(const("tok1", Q, 1), NB), ALU.mult)
                v.drain()
            v.sem_inc(s["route_ready"], 1)
            tt(xe, bc(iota[:, 0:XB], 2, NE), bc(osx, 1, XB), ALU.is_ge)
            tt(xe2, bc(iota[:, 0:XB], 2, NE), bc(incl, 1, XB), ALU.is_lt)
            v.drain()
            tt(xe, xe, xe2, ALU.mult)
            v.drain()
            tt(xe, xe, bc(iota[:, 0:NE], 1, XB), ALU.mult)
            v.drain()
            v.tensor_reduce(ovf[:, 0:XB], xe, AX.X, ALU.add)
            v.tensor_copy(ovf[:, XB:XB + 1], incl[:, NE - 1:NE])
            v.drain()
            v.tensor_copy(ovfi.bitcast(I32), ovf)
            v.wait_ge(s["table_made"], 1)
            ts(tadd, bank(3, 2, NB), 0.0, ALU.is_equal, PAD_ROW, ALU.mult)
            v.drain()
            stt(tabf, bank(3, 2, NB), -1.0, tadd, ALU.add, ALU.add)
            v.drain()
            v.tensor_copy(tab[:, :, 0:NB], tabf)
            v.tensor_copy(tab[:, :, NB:NB + 1], tabf[:, :, 0:1])
            v.memset(xg[0], 0.0)
            v.memset(xg[1], 0.0)
            v.drain()
            v.tensor_copy(ix[:, 0, :], tab[:, 1, 0:1]).then_inc(s["gidx_ready"], 1)
            v.tensor_copy(ix[:, 1, :], tab[:, 1, 1:2]).then_inc(s["gidx_ready"], 1)
            v.sem_inc(s["table_ready"], 1)

            v.wait_ge(s["x1_spilled"], 16 * Q)
            v.wait_ge(s["x1T_ready"], Q)
            ts(x1[:, 0:NT, :], x1[:, 0:NT, :], ALPHA, ALU.mult)
            ts(x1[0:B, NT, :], x1[0:B, NT, :], ALPHA, ALU.mult)
            v.sem_inc(s["yb_ready"], 1)
            def silu_step(e):
                v.wait_ge(s["gate_act"], e + 1)
                tt(esig, esig, bank(2, FF), ALU.mult)

            def h_step(e):
                v.drain()
                v.wait_ge(s["up_mm"], e + 3)
                tt(hb, esig, bank(3, FF), ALU.mult).then_inc(s["h_ready"], 1)

            def row_index_step(e, q):
                v.tensor_copy(ix[:, q, :], tab[:, 1, bass.ds(e, 1)]).then_inc(s["gidx_ready"], 1)

            def hT_step(e):
                v.wait_ge(s["hT_turned"], e + 1)
                v.tensor_copy(hT, bank(4, 4, P)).then_inc(s["hT_ready"], 1)

            def y_step(e, q, n):
                v.wait_ge(s["y_mm"], e + 3)
                v.wait_ge(s[f"scat_{'ab'[q]}"], n * 16 + 16)
                v.tensor_copy(ix[:, 2 + q, :], tab[:, 0, bass.ds(e, 1)])
                v.tensor_copy(yb[q], bank(5, D)).then_inc(s["yb_ready"], 1)

            silu_step(0)
            h_step(0)
            row_index_step(2, 0)
            with v.Fori(0, NE // 2 - 1) as i:
                for q in range(2):
                    e = i * 2 + q + 1
                    silu_step(e)
                    hT_step(i * 2 + q)
                    h_step(e)
                    row_index_step(i * 2 + q + 3, 1 - q)
                    y_step(i * 2 + q, q, i)
            silu_step(NE - 1)
            hT_step(NE - 2)
            h_step(NE - 1)
            y_step(NE - 2, 0, NE // 2 - 1)
            hT_step(NE - 1)
            y_step(NE - 1, 1, NE // 2 - 1)

            def extra_vec(i):
                silu_step(i + NE)
                h_step(i + NE)
                row_index_step(i + NE + 1, 0)
                hT_step(i + NE)
                y_step(i + NE, 0, i + NE // 2)

            extra_blocks(v, extra_vec)


            def expert_sum(t):
                n = rows(t)
                xt = x1[0:n, t, :]
                if t == 0:
                    v.wait_ge(s["ln2_in"], 32)
                v.wait_ge(s[f"yk{t}_in"], 16)
                for k in range(2):
                    stt(xt, yk[0:n, t, k, :], pgate[0:n, k, t, :], xt, ALU.mult, ALU.add)
                    v.drain()

            layer_norm(x1, 2, expert_sum)

        @block.gpsimd
        def _(g):
            ix = idx.bitcast(U32)

            def offset(x, pas):
                for t in range(Q):
                    n = rows(t)
                    g.wait_ge(s["ln_gained"], pas * Q + t + 1)
                    g.tensor_tensor(x[0:n, t, :], x[0:n, t, :], gb[0:n, 1, :], ALU.add).then_inc(s["x_normed"], 1)

            offset(xtok, 0)
            g.wait_ge(s["kT_ready"], 1)
            g.wait_ge(s["v_ready"], 1)
            g.wait_ge(s["consts_in"], 16)
            g.wait_ge(s["mkv_made"], 2)
            g.wait_ge(s["spilled"], 16 * Q)
            g.tensor_copy(mst, const("mask0"))
            with g.Fori(0, NT) as i:
                g.wait_ge(s["blk_out"], i + 1)
                g.sem_inc(s["pace"], 1)
                g.tensor_copy(kst, kT[:, bass.ds(i * P, 2 * P)])
                g.tensor_copy(vst, vtok[:, bass.ds(i, 2), :])
                g.drain()
                g.sem_inc(s["blk_kv"], 1)
                g.wait_ge(s["blk_max"], i + 1)
                g.sem_inc(s["pace"], 1)
                g.tensor_copy(mst, const("mask"))
            g.drain()
            g.sem_inc(s["blk_kv"], 1)

            offset(x1, 1)
            g.wait_ge(s["table_ready"], 1)
            g.wait_ge(s["x1_spilled"], 16 * Q)
            def gather(e, q):
                g.wait_ge(s["gidx_ready"], e + 1)
                g.sem_inc(s["pace"], 1)
                g.indirect_dma_start(xg[q], None, X["x1"], bass.IndirectOffsetOnAxis(ap=ix[:, q, :], axis=0),
                                     bounds_check=N - 1, oob_is_err=False).then_inc(s[f"xg_in_{'ab'[q]}"], 16)

            def scatter(e, q):
                g.wait_ge(s["yb_ready"], e + 2)
                g.sem_inc(s["pace"], 1)
                g.indirect_dma_start(X["ya"], bass.IndirectOffsetOnAxis(ap=ix[:, 2 + q, :], axis=0), yb[q], None,
                                     bounds_check=2 * N - 1, oob_is_err=False).then_inc(s[f"scat_{'ab'[q]}"], 16)

            g.dma_start(X["prime"][0:1, :], const("iota")[0:1, 0:16]).then_inc(s["scat_a"], 16)
            g.dma_start(X["prime"][1:2, :], const("iota")[0:1, 0:16]).then_inc(s["scat_b"], 16)
            gather(0, 0)
            gather(1, 1)
            gather(2, 0)
            with g.Fori(0, NE // 2 - 2) as i:
                for q in range(2):
                    gather(i * 2 + q + 3, 1 - q)
                    scatter(i * 2 + q, q)
            gather(NE - 1, 1)
            scatter(NE - 4, 0)
            scatter(NE - 3, 1)
            scatter(NE - 2, 0)
            scatter(NE - 1, 1)
            g.wait_ge(s["scat_a"], 16 * (NE // 2 + 1))
            g.wait_ge(s["scat_b"], 16 * (NE // 2 + 1))

            def extra_rows(i):
                gather(i + NE, 0)
                scatter(i + NE, 0)
                g.wait_ge(s["scat_a"], i * 16 + 16 * (NE // 2 + 2))
                g.sem_inc(s["pace"], 1)

            extra_blocks(g, extra_rows)
            g.sem_inc(s["ovf_step"], 1)
            offset(x1, 2)


OUTS = [("y_prompt", (T, D), (1, T, D)), ("y_sample", (B, D), (B, 1, D)),
        ("wkv_prompt", (HA, 64, 64), (1, 1, HA, 64, 64)), ("wkv_sample", (B * HA, 64, 64), (1, B, HA, 64, 64)),
        ("shift_prompt", (1, C_SHIFT), (1, 1, C_SHIFT)), ("shift_sample", (B, C_SHIFT), (1, B, C_SHIFT)),
        ("win_k_prompt", (P, P), (1, 1, P, 2, 64)), ("win_v_prompt", (P, P), (1, 1, P, 2, 64)),
        ("win_k_sample", (B, P, P), (1, B, P, 2, 64)), ("win_v_sample", (B, P, P), (1, B, P, 2, 64)),
        ("mem_k_prompt", (NMEM, 256), (1, 1, NMEM, 4, 64)), ("mem_v_prompt", (NMEM, 256), (1, 1, NMEM, 4, 64))]


def kernel(**a):
    import concourse.bacc as bacc
    from concourse.bass_utils import run_bass_kernel_spmd

    nc = bacc.Bacc("TRN2", target_bir_lowering=False, num_devices=1)
    arrays, I, O, X = {}, {}, {}, {}

    def give(name, x):
        x = np.ascontiguousarray(x)
        arrays["in_" + name] = x
        I[name] = nc.dram_tensor("in_" + name, x.shape, F32, kind="ExternalInput").ap()

    give("consts", CONST)
    give("x_prompt", np.reshape(a["x_prompt"], (T, D)))
    give("x_sample", np.reshape(a["x_sample"], (B, D)))
    give("mem_prompt", np.reshape(a["mem_prompt"], (NMEM, D)))
    give("state_wkv", np.reshape(a["state_wkv"], (B * HA, 64, 64)))
    give("state_shift", np.reshape(a["state_shift"], (B, C_SHIFT)))
    for n in ("cache_win_k", "cache_win_v"):
        give(n, np.reshape(a[n], (B, WIN, P)))
    for n in ("cache_mem_k", "cache_mem_v"):
        give(n, np.reshape(a[n], (B, NMEM, 256)))
    for n in ("ln_in_g", "ln_in_b"):
        give(n, a[n])
    for n in ("ln1_g", "ln1_b", "ln2_g", "ln2_b", "w_in", "w_up", "a_up", "g_up", "w_mem_kv", "p_a", "p_b", "p_m", "w_o",
              "e_gate", "e_up", "e_down"):
        give(n, a[n][0])
    vecs = ("mu", "w0", "a0", "k_k", "k_a", "r_k", "lnx_g", "lnx_b")
    give("params", np.concatenate([np.reshape(a[n], (-1, P)) for n in vecs]))
    give("sinks_bc", np.tile(np.reshape(a["sinks"], (1, HA)), (P, 1)))
    give("sinks_row", np.reshape(np.tile(np.reshape(a["sinks"], (2, 1, 4)), (1, B, 1)), (64, 1)))
    give("router_b", np.tile(np.concatenate([a["b_group"], a["b_router"]], 1), (P, 1)))
    give("router_w", np.concatenate([a["w_group"][0], a["w_router"][0]], 1))
    for n, shape in (("x0", (N, D)), ("x1", (N, D)), ("ya", (2 * N, D)), ("gates", (N_GATE, P, N)), ("sv", (6, B, C_A)), ("sy", (B * HA, 64)), ("prime", (2, 16))):
        X[n] = nc.dram_tensor("scratch_" + n, shape, F32).ap()
    for n, shape, _ in OUTS:
        O[n] = nc.dram_tensor("out_" + n, shape, F32, kind="ExternalOutput").ap()
    build(nc, I, O, X)
    got = run_bass_kernel_spmd(nc, [arrays], core_ids=[0]).results[0]
    return tuple(np.reshape(got["out_" + n], shape) for n, _, shape in OUTS)
```

```python
import math
from contextlib import ExitStack

import numpy as np
import concourse.bass as bass
import concourse.mybir as mybir

F32 = mybir.dt.float32
I32 = mybir.dt.int32
U32 = mybir.dt.uint32
ALU = mybir.AluOpType
ACT = mybir.ActivationFunctionType
AX = mybir.AxisListType

P = 128
D = 1024
KD = D // P
T, B = 512, 8
N = T + B
NH = N // 2
NT = T // P
HA, C_A = 8, 512
NJ = C_A // P
CH = 64
C_SHIFT = 1792
SF = C_SHIFT // P
FQ, FK, FV, FM, NF = 14, 18, 19, 20, 22
GATE0 = NF * P
N_GATE = 3 * KD
G_CACHE, G_BONUS, G_SAMP, G_TILE = 8, 10, 11, 16
WIN, NMEM = 128, 256
ALPHA = 2.0 ** 0.25
LN_EPS, LNX_EPS = 1e-5, 64e-5
DECAY = math.exp(-0.5)
NE, FF, NG, EPG = 32, 512, 4, 8
XB = 8
NB = NE + XB
BIG = 1e30
PAD_ROW = 5000.0


def const_table():
    parts, at, off = [], {}, 0

    def put(name, a):
        nonlocal off
        a = np.asarray(a, np.float32)
        full = np.zeros((P, a.shape[1]), np.float32)
        full[:a.shape[0]] = a
        parts.append(full)
        at[name] = (off, a.shape[1])
        off += a.shape[1]

    r = np.arange(P)[:, None]
    c = np.arange(P)[None, :]
    same = (r // CH) == (c // CH)
    put("ident", np.eye(P))
    put("eps", np.tile(np.array([[LN_EPS, LNX_EPS]]), (P, 1)))
    put("upper2", np.concatenate([same & (r < c), same & (r <= c)], 1))
    put("low1", (r // 2 == c // 2) & (r > c))
    put("up1", (r // 2 == c // 2) & (r < c))
    for k in range(1, 6):
        b = 2 ** k
        put(f"level{k}", (r // (2 * b) == c // (2 * b)) & (r // b == c // b + 1))
    kj = np.arange(2 * P)[None, :]
    band = (kj <= r + P) & (r + P - kj < WIN)
    put("mask0", np.where(band & (kj >= P), 0.0, -BIG))
    put("mask", np.where(band, 0.0, -BIG))
    half = 8
    inv = 500000.0 ** (-np.arange(half, dtype=np.float32) / half)
    pos = np.concatenate([np.arange(T), np.full(B, 2048)]).astype(np.float32)
    ang = (pos[:, None] * inv[None, :].astype(np.float32)).astype(np.float32)
    cos, sin = np.ones((P, N)), np.zeros((P, N))
    rot = np.zeros((P, P))
    for h in range(2):
        for i in range(half):
            for base, sign, other in ((0, -1.0, half), (half, 1.0, 0)):
                f = h * 64 + base + i
                cos[f] = np.cos(ang[:, i])
                sin[f] = np.sin(ang[:, i])
                rot[h * 64 + other + i, f] = sign
    put("cos", cos)
    put("sin", sin)
    put("rot", rot)
    s8 = np.zeros((P, NJ, HA))
    for j in range(NJ):
        for p in range(P):
            s8[p, j, 2 * j + p // 64] = 1
    put("sel8", s8.reshape(P, -1))
    put("sel8t", np.transpose(s8, (2, 1, 0)).reshape(HA, -1))
    put("bones", (r // 64 == c // 64))
    put("before", r < c)
    put("ones", np.ones((P, P)))
    put("reset", np.tile((np.arange(T) % CH != 0)[None, :], (P, 1)))
    put("iota", np.tile(np.arange(P)[None, :], (P, 1)))
    tok = np.arange(NT + 1)[None, :] * P + r
    put("valid", tok < N)
    real = (tok < N)[:, :, None]
    put("tok1", (tok + 1) * (tok < N))
    put("asg1", (real * np.stack([2 * tok + 1, 2 * tok + 2], 2)).reshape(P, -1))
    return np.concatenate(parts, 1), at


CONST, CAT = const_table()
NCONST = CONST.shape[1]
PR_MU, PR_W0, PR_A0, PR_KK, PR_KA, PR_RK, PR_LG, PR_LB, PR_N = 0, 14, 18, 22, 26, 30, 34, 38, 42


SEMS = """
ident_in consts_in params_in x_in mem_in wmem_in cache_in 
lora_in state_in samp_in out_in xback_in 
p1w0_in p1w1_in mgw0_in mgw1_in spilled x1_spilled out_done
ln_stats ln_std ln_rs ln_scaled ln_gained x_normed x_turned xT_ready mem_turned memT_ready mkv_made mkv_ready mkT_ready
z_made z_ready side_turned side_ready
v_ready rot_made kT_ready kout_turned kout_ready
blk_kv decay_arg blk_q blk_scores blk_max blk_exp blk_prob blk_turned blk_pT_act blk_pT_dve blk_mixed blk_out
sk_turned sk_ready sk_scored sk_cols sk_rows sk_max sk_exp sk_prob sk_pT_made sk_pT_ready sk_mixed sk_done
zs_ready lora_act lora_mm lora_sig kk_sq head_sum head_root head_recip kk_bcast bonus_in bonus_mm prep_done
samp_stack samp_state
exps_made tile_ready tm_turned tm_ready tri_made tri_ready nk_ready lvl_t1 lvl_t1_ready lvl_x lvl_x_ready
nv_made nv_ready xav_made xav_ready gh_made gh_ready ry_made ry_ready chain_mm chain_done y_made y_ready
fstate_ready
gn_mean gn_center gn_sq gn_bcast oa_ready
gate_made gate_out gate_spill0 gate_spill1 gate_sig proj_made proj_used merged
h_made h_used x1_turned x1T_ready logits_made onehot_ready rank_made exp_asked exp_made
route_ready table_made table_ready
xg_in_a xg_in_b xg_turned xgT_ready gate_mm up_mm gate_act h_ready hT_turned hT_ready y_mm yb_ready
ew0g_in ew0u_in ew0d_in ew1g_in ew1u_in ew1d_in scat_a scat_b
ovf_step pace gidx_ready ln2_in tile0_in tile1_in tile2_in tile3_in tile4_in 
""".split()


SIDE_PARAMS, SIDE_SHIFT, SIDE_SAMP, SIDE_YSAMP, SIDE_STATE = 1, 2, 3, 4, 5


def build(nc, I, O, X):
    with ExitStack() as ctx:
        arena = ctx.enter_context(nc.sbuf_tensor("arena", [P, 53200], F32))
        psum = ctx.enter_context(nc.psum_tensor("psum", [P, 8, 512], F32))
        s = {n: ctx.enter_context(nc.semaphore(n)) for n in SEMS}

        def view(off, *dims):
            n = int(np.prod(dims))
            a = arena[:, off:off + n]
            if len(dims) == 1:
                return a
            names = "abcd"[:len(dims)]
            return a.rearrange("p (%s) -> p %s" % (" ".join(names), " ".join(names)),
                               **dict(zip(names[1:], dims[1:])))

        def bank(b, *dims, off=0):
            n = int(np.prod(dims))
            a = psum[:, :, :].rearrange("p a b -> p (a b)")[:, b * 512 + off:b * 512 + off + n]
            if len(dims) == 1:
                return a
            names = "abcd"[:len(dims)]
            return a.rearrange("p (%s) -> p %s" % (" ".join(names), " ".join(names)),
                               **dict(zip(names[1:], dims[1:])))

        def bc(ap, axis, n):
            a = ap.unsqueeze(axis)
            sh = list(a.shape)
            sh[axis] = n
            return a.to_broadcast(sh)

        off = [0]

        def take(n):
            o = off[0]
            off[0] += n
            return o

        C0 = take(NCONST)
        PRM = take(PR_N + 6)
        GBo = take(2 * D)
        SMo = take(800)
        XTo = take(KD * N)
        Zo = take(NF * N)
        ZSo = take(SF * N)
        KKo = take(NJ * N)
        BVo = take(NJ * N)
        LCo = take(NJ * T)
        YTo = take(NJ * N)
        Fo = off[0]
        FREE = 53200 - Fo
        assert FREE >= 14336, FREE

        def const(name, *dims):
            o, w = CAT[name]
            return view(C0 + o, *(dims or (w,)))

        ident = const("ident")
        prm = view(PRM, PR_N)
        gb = view(GBo, 2, D)
        sm = [SMo]

        def small(*dims):
            o = sm[0]
            sm[0] += int(np.prod(dims))
            assert sm[0] <= SMo + 800
            return view(o, *dims)

        sink_bc = small(HA)
        sink_row = small(1)
        rb = small(NG + NE)
        st6 = small(NT + 1, 2, 6)
        mv = small(NT + 1, 2)
        rstd, nmr = small(NT + 1, 1), small(NT + 1, 1)
        sstT = small(SF, B)
        mx, nmx, den, ske, rden = small(12), small(12), small(12), small(8), small(12)
        smx, snmx, sden, sske, srd = small(2), small(2), small(2), small(2), small(2)
        kTs = small(B)
        qsS = small(6, B)
        qbd = small(B, 12)
        pc2 = small(2, NJ)
        wS = small(NJ, B)

        xT = view(XTo, KD, N)
        z = view(Zo, NF, N)
        zs = view(ZSo, SF, N)

        xtok = view(Fo, NT + 1, D)
        memtok = view(Fo + 5120, 2, D)
        memT = view(Fo + 7168, KD, NMEM)
        wmem = view(Fo + 9216, KD, 512)
        p1w = [view(YTo + q * 1024, KD, P) for q in range(2)]
        kT = view(BVo, P + T)
        vtok = view(BVo + 640, NT + 1, P)
        mkT = view(BVo + 1280, 2, NMEM)
        mkv = view(LCo, 2, 512)
        ktl = view(LCo + 1024, P)
        kss = view(LCo + 1152, P)
        vss = view(LCo + 1280, P)
        shb = view(KKo, C_SHIFT)
        prow = view(LCo + 1408, P)
        ssraw = view(ZSo, C_SHIFT)

        S = view(Fo, 12, 256)
        PT = view(Fo + 3072, 24, P)
        qs = view(Fo + 6144, 6, P)
        kst = view(Fo + 6912, 256)
        vst = view(Fo + 7168, 2, P)
        mst = view(Fo + 7424, 256)
        tmpq = view(Fo + 7680, NJ, T)
        kwin = view(Fo, B, P)
        vwin = view(Fo + 1024, B, P)
        kmem = view(Fo + 2048, B, 2, 256)
        vmem = view(Fo + 6144, B, 2, 256)
        kTb = [view(Fo + 10240 + q * 640, 5, P) for q in range(2)]
        sST = view(Fo + 11520, P)
        sW = view(Fo + 11648, P)
        sM = view(Fo + 11776, 2, P)
        sWT = view(Fo + 12032, 64)
        sMT = view(Fo + 12096, 2, 32)

        sg = view(Zo, NJ, N)
        ah = view(Zo + 2080, NJ, N)
        gT = view(Zo + 4160, NJ, N)
        th = view(Zo + 6240, N)
        kk = view(KKo, NJ, N)
        BV = view(BVo, NJ, N)
        Lc = view(LCo, NJ, T)
        YT = view(YTo, NJ, N)
        rT, kTr, vT = zs[:, 0:4, :], zs[:, 4:8, :], zs[:, 8:12, :]
        xwa, xg_ = zs[:, 12, :], zs[:, 13, :]
        wup = view(BVo, C_A)
        gup = view(BVo + 512, C_A)
        sqb = view(Fo + 12160, NJ, N)
        gsq = view(Fo + 1024, NJ, N)
        rnk = view(YTo, N)
        rn = view(Fo + 3104, N)
        sS = view(Fo + 3640, 32, 64)
        sTmp = view(Fo + 5688, 32, 64)
        vec = view(Fo + 7736, 6, 64)
        vvh = view(Fo + 8120, 32)
        sa = view(Fo + 8152, 32)
        sy = view(Fo + 8184, 32)
        sstk = view(Fo + 8216, 6, NJ, B)
        srow = view(Fo + 8408, 6, C_A)
        yrow = view(Fo + 11480, C_A)
        o = [Fo]

        def F(*dims):
            v = view(o[0], *dims)
            o[0] += int(np.prod(dims))
            assert o[0] <= 53200
            return v

        Pexc, Pinc, Pinv = F(NJ, P), F(NJ, P), F(NJ, P)
        AR = F(NJ, 2, P)
        Bt, Kt, Vt = F(NJ, P), F(NJ, P), F(NJ, P)
        Btok, Ktok, Vtok = F(C_A), F(C_A), F(C_A)
        ANV = F(HA, 2, 64)
        MR, NR = F(HA, 2, P), F(HA, 2, P)
        XX = F(HA, 2, P)
        GT, Hm = F(2, NJ, 64), F(2, NJ, 64)
        T1 = view(Fo, HA, P)
        Rh = view(Fo + 1024, NJ, P)
        XAV = view(Fo + 2560, HA, 2, 64)
        Yl = view(Fo + 3584, NJ, P)
        SR = view(ZSo + 12 * N, 3, NJ, 64)
        fst = view(Fo, HA, 64)

        MGo = Fo + 3640
        MGW = 10 * P + 3 * N
        mgw = [view(MGo + q * MGW, 10, P) for q in range(2)]
        mgg = [view(MGo + q * MGW + 10 * P, 3, N) for q in range(2)]
        ptmp = view(ZSo + 4160, N)
        MG = view(ZSo, KD, N)
        wo = [view(MGo + 2 * MGW, KD, 512), view(KKo, KD, 512)]
        wr = view(MGo + 2 * MGW + 4096, KD, NG + NE)
        assert MGo + 2 * MGW + 4096 + KD * (NG + NE) <= 53200
        gcol = [view(GBo + q * 1024, KD, P) for q in range(2)]
        gout = [z[:, FK + q, :] for q in range(2)]
        x1 = view(Zo, NT + 1, D)
        x1T = xT
        R0 = [ZSo]

        def R(*dims):
            v = view(R0[0], *dims)
            R0[0] += int(np.prod(dims))
            assert R0[0] <= ZSo + SF * N
            return v

        T5 = NT + 1
        LG = R(T5, NG + NE)
        g1 = R(T5, 1)
        eq4, c4, oh4, t4 = R(T5, NG), R(T5, NG), R(T5, NG), R(T5, NG)
        i1 = R(T5, 1)
        gd = R(T5, 1)
        el = R(T5, NE)
        eqx, cx = R(T5, NE), R(T5, NE)
        v1, v2 = R(T5, 1), R(T5, 1)
        OH = R(2, T5, NE)
        earlier = R(T5 + 1, NE)
        Osum, rank, qb, blk = R(T5, NE), R(T5, NE), R(T5, NE), R(T5, NE)
        cnt, nx, incl, osx, dov = R(NE), R(NE), R(NE), R(NE), R(NE)
        bk, sk = R(2, T5, 1), R(2, T5, 1)
        SK = R(2, T5, P)
        VB = R(T5, 2, 2, NB)
        tabf = R(2, NB)
        tadd = R(2, NB)
        xe = R(XB, NE)
        xe2 = R(XB, NE)
        pgate = small(2, T5, 1)
        tabi = small(2, NB + 1)
        ovf, ovfi = small(XB + 1), small(XB + 1)
        e2, rden2 = small(T5, 1), small(T5, 1)
        idx = small(4, 1)

        EW = KD * FF
        eg = [view(Fo, KD, FF), view(Fo + EW, KD, FF)]
        eu = [view(Zo + 5120, KD, FF), view(KKo, KD, FF)]
        ed = [view(LCo, FF // P, D), view(Fo + 2 * EW, FF // P, D)]
        yb = [view(Fo + 3 * EW + q * D, D) for q in range(2)]
        esig = view(Zo + 5120 + EW, FF)
        yk = view(Fo, T5, 2, D)
        assert MGo + 2 * MGW >= Fo + 2 * EW and Fo + 3 * EW + 2 * D <= 53200
        m0 = [XTo]

        def M1(*dims):
            v = view(m0[0], *dims)
            m0[0] += int(np.prod(dims))
            assert m0[0] <= XTo + KD * N
            return v

        xg = [M1(D), M1(D)]
        xgT = M1(KD, P)
        hb, hT = M1(FF), M1(FF // P, P)

        block = ctx.enter_context(nc.Block())
        Q = NT + 1

        def rows(t):
            return P if t < NT else B

        def tile_at(pas, t):
            return (t - 1) % Q if pas == 2 else t

        def extra_blocks(eng, body):
            n = eng.value_load(ovfi.bitcast(I32)[0:1, XB:XB + 1], min_val=0, max_val=XB)
            with eng.If(n > 0):
                with eng.Fori(0, n) as i:
                    body(i)

        @block.sync
        def _(sp):
            def x_load(t):
                src = I["x_prompt"][t * P:(t + 1) * P, :] if t < NT else I["x_sample"]
                sp.dma_start(xtok[0:rows(t), t, :], src).then_inc(s[f"tile{t}_in"], 16)

            first = C0 + P + 2
            x_load(0)
            sp.dma_start(view(C0, P + 2), I["consts"][:, 0:P + 2]).then_inc(s["ident_in"], 16)
            sp.dma_start(gb[:, 0, :], I["ln_in_g"].partition_broadcast(P)).then_inc(s["x_in"], 16)
            sp.dma_start(gb[:, 1, :], I["ln_in_b"].partition_broadcast(P)).then_inc(s["x_in"], 16)
            x_load(1)
            sp.dma_start(memtok, I["mem_prompt"].rearrange("(t p) d -> p t d", p=P)).then_inc(s["mem_in"], 16)
            for t in range(2, Q):
                x_load(t)
            sp.dma_start(wmem, I["w_mem_kv"].rearrange("(p c) n -> p c n", c=KD)).then_inc(s["wmem_in"], 16)
            sp.dma_start(view(first, NCONST - P - 2), I["consts"][:, P + 2:]).then_inc(s["consts_in"], 16)
            sp.dma_start(prow[0:PR_N, :], I["params"]).then_inc(s["params_in"], 16)
            sp.dma_start(ssraw[0:B, :], I["state_shift"]).then_inc(s["params_in"], 16)
            sp.dma_start(sink_bc, I["sinks_bc"]).then_inc(s["params_in"], 16)
            sp.dma_start(sink_row[0:64, :], I["sinks_row"]).then_inc(s["params_in"], 16)
            sp.dma_start(rb, I["router_b"]).then_inc(s["params_in"], 16)

            w_in = I["w_in"].rearrange("(p c) n -> p c n", c=KD)

            def p1_load(q, need, src_a, src_b, dst_a, dst_b):
                sp.wait_ge(s["z_made"], need)
                sp.dma_start(dst_a, src_a).then_inc(s[f"p1w{q}_in"], 16)
                sp.dma_start(dst_b, src_b).then_inc(s[f"p1w{q}_in"], 16)

            def p1_tile(f, q, need):
                cols = bass.ds(f * P, P)
                p1_load(q, need, w_in[:, 0:4, cols], w_in[:, 4:8, cols], p1w[q][:, 0:4, :], p1w[q][:, 4:8, :])

            with sp.Fori(0, FQ // 2) as i:
                for q in range(2):
                    p1_tile(i * 2 + q, q, i * 2 + q + 1)
            for j in range(4):
                c0 = FQ * P + j * 64
                p1_load(j % 2, FQ + j + 1, w_in[:, :, c0:c0 + 64], w_in[:, :, c0 + 256:c0 + 320],
                        p1w[j % 2][:, :, 0:64], p1w[j % 2][:, :, 64:128])
            for f in range(FK, NF):
                p1_tile(f, f % 2, f + 1)

            for t in range(Q):
                sp.wait_ge(s["x_normed"], t + 1)
                sp.dma_start(X["x0"][t * P:t * P + rows(t), :], xtok[0:rows(t), t, :]).then_inc(s["spilled"], 16)

            def gate_load(k, q):
                sp.dma_start(gcol[q], w_in[:, :, bass.ds(k * P + GATE0, P)]).then_inc(s[f"p1w{q}_in"], 16)

            def gate_step(k, q, ahead=True):
                if ahead:
                    sp.wait_ge(s["gate_made"], k + 1)
                    gate_load(k + 2, q)
                sp.wait_ge(s["gate_out"], k + 1)
                sp.dma_start(X["gates"][bass.ds(k, 1)].rearrange("a p n -> (a p) n"), gout[q]).then_inc(s[f"gate_spill{q}"], 16)

            sp.wait_ge(s["z_ready"], NF + 2)
            for q in range(2):
                gate_load(q, q)
            for t in range(2):
                sp.wait_ge(s["mkv_ready"], t + 1)
                sp.dma_start(O["mem_k_prompt"][t * P:(t + 1) * P, :], mkv[:, t, 0:256]).then_inc(s["out_done"], 16)
                sp.dma_start(O["mem_v_prompt"][t * P:(t + 1) * P, :], mkv[:, t, 256:512]).then_inc(s["out_done"], 16)
            sp.wait_ge(s["side_ready"], SIDE_SHIFT)
            sp.dma_start(O["shift_prompt"], shb[0:1, :]).then_inc(s["out_done"], 16)
            sp.dma_start(O["shift_sample"], shb[1:1 + B, :]).then_inc(s["out_done"], 16)
            sp.wait_ge(s["kout_ready"], 1)
            sp.wait_ge(s["v_ready"], 1)
            sp.dma_start(O["win_k_prompt"], ktl).then_inc(s["out_done"], 16)
            sp.dma_start(O["win_v_prompt"], vtok[:, NT, :]).then_inc(s["out_done"], 16)

            with sp.Fori(0, NT) as i:
                for q in range(2):
                    gate_step(i * 2 + q, q)

            sp.wait_ge(s["blk_out"], NT + 1)
            sp.wait_ge(s["blk_kv"], 2 * NT)
            sp.dma_start(kwin[0:P - 1, :, :], I["cache_win_k"][:, 1:, :].rearrange("b w f -> w b f")).then_inc(s["cache_in"], 16)
            sp.dma_start(vwin[0:P - 1, :, :], I["cache_win_v"][:, 1:, :].rearrange("b w f -> w b f")).then_inc(s["cache_in"], 16)
            sp.dma_start(kwin[P - 1:P, :, :], kss[0:B, :]).then_inc(s["cache_in"], 16)
            sp.dma_start(vwin[P - 1:P, :, :], vss[0:B, :]).then_inc(s["cache_in"], 16)
            sp.dma_start(kmem, I["cache_mem_k"].rearrange("b (t p) f -> p b t f", p=P)).then_inc(s["cache_in"], 16)
            sp.dma_start(vmem, I["cache_mem_v"].rearrange("b (t p) f -> p b t f", p=P)).then_inc(s["cache_in"], 16)
            sp.dma_start(wup[0:64, :], I["w_up"]).then_inc(s["lora_in"], 16)
            sp.dma_start(wup[64:128, :], I["a_up"]).then_inc(s["lora_in"], 16)
            sp.dma_start(gup, I["g_up"]).then_inc(s["lora_in"], 16)
            for k in range(G_CACHE, G_BONUS):
                gate_step(k, k % 2)
            sp.wait_ge(s["cache_in"], 96)
            sp.dma_start(O["win_k_sample"].rearrange("b w f -> w b f"), kwin).then_inc(s["out_done"], 16)
            sp.dma_start(O["win_v_sample"].rearrange("b w f -> w b f"), vwin).then_inc(s["out_done"], 16)

            sp.wait_ge(s["sk_done"], 1)
            sp.wait_ge(s["out_done"], 16 * 10)
            for h in range(2):
                sp.dma_start(sS[h * 64:h * 64 + 64, :, :],
                             I["state_wkv"][:, h * 32:h * 32 + 32, :]).then_inc(s["state_in"], 16)
            gate_step(G_BONUS, G_BONUS % 2)
            sp.wait_ge(s["side_ready"], SIDE_SAMP)
            sp.dma_start(X["sv"].rearrange("q b f -> b q f"), srow[0:B, :, :]).then_inc(s["spilled"], 16)
            sp.wait_ge(s["spilled"], 16 * (Q + 1))
            svv = X["sv"].rearrange("q b (h k) -> (b h) q k", k=64)
            for h in range(2):
                sp.dma_start(vec[h * 64:h * 64 + 64, :, :], svv).then_inc(s["samp_in"], 16)
                sp.dma_start(vvh[h * 64:h * 64 + 64, :], svv[:, 3, h * 32:h * 32 + 32]).then_inc(s["samp_in"], 16)
            for k in range(G_SAMP, G_TILE - 1):
                gate_step(k, k % 2)
            sp.wait_ge(s["samp_state"], 1)
            for h in range(2):
                sp.dma_start(O["wkv_sample"][:, h * 32:h * 32 + 32, :], sS[h * 64:h * 64 + 64, :, :]).then_inc(s["out_done"], 16)
                sp.dma_start(X["sy"][:, h * 32:h * 32 + 32], sy[h * 64:h * 64 + 64, :]).then_inc(s["spilled"], 16)
            sp.wait_ge(s["spilled"], 16 * (Q + 3))
            sp.dma_start(yrow[0:B, :], X["sy"].rearrange("(b h) v -> b (h v)", b=B)).then_inc(s["samp_in"], 16)
            gate_step(G_TILE - 1, (G_TILE - 1) % 2)
            with sp.Fori(0, NT - 1) as i:
                for q in range(2):
                    gate_step(i * 2 + (G_TILE + q), q)
            for k in range(N_GATE - 2, N_GATE):
                gate_step(k, k % 2, ahead=False)
            sp.wait_ge(s["fstate_ready"], 1)
            sp.dma_start(O["wkv_prompt"].rearrange("h v k -> v h k"), fst[0:64, :, :]).then_inc(s["out_done"], 16)

            for q in range(2):
                sp.wait_ge(s[f"gate_spill{q}"], 16 * (N_GATE // 2 + 1))
            gates = X["gates"].rearrange("(g c) p n -> c p g n", g=3)
            pa = I["p_a"].rearrange("(c p) n -> p c n", p=P)
            pm = I["p_m"].rearrange("(c p) n -> p c n", p=P)
            pbv = I["p_b"].rearrange("(e j p) n -> e p j n", e=2, p=64)
            def merge_load(o, q):
                sp.wait_ge(s["merged"], o + 1)
                sp.dma_start(mgg[q], gates[bass.ds(o, 1)].rearrange("c p g n -> (c p) g n")).then_inc(s[f"mgw{q}_in"], 16)
                cols = bass.ds(o * P, P)
                sp.dma_start(mgw[q][:, 0:4, :], pa[:, :, cols]).then_inc(s[f"mgw{q}_in"], 16)
                for e in range(2):
                    sp.dma_start(mgw[q][e * 64:e * 64 + 64, 4:8, :], pbv[e, :, :, cols]).then_inc(s[f"mgw{q}_in"], 16)
                sp.dma_start(mgw[q][:, 8:10, :], pm[:, :, cols]).then_inc(s[f"mgw{q}_in"], 16)

            for q in range(2):
                merge_load(q, q)
            wov = I["w_o"].rearrange("(c p) n -> p c n", p=P)
            sp.dma_start(wo[0], wov[:, :, 0:512]).then_inc(s["out_in"], 16)
            sp.dma_start(wr, I["router_w"].rearrange("(p c) n -> p c n", c=KD)).then_inc(s["out_in"], 16)
            sp.dma_start(gb[:, 0, :], I["ln1_g"].partition_broadcast(P)).then_inc(s["out_in"], 16)
            sp.dma_start(gb[:, 1, :], I["ln1_b"].partition_broadcast(P)).then_inc(s["out_in"], 16)
            for q in range(2):
                merge_load(q + 2, q)
            sp.wait_ge(s["oa_ready"], 1)
            sp.dma_start(wo[1], wov[:, :, 512:1024]).then_inc(s["out_in"], 16)
            with sp.Fori(2, KD // 2) as i:
                for q in range(2):
                    merge_load(i * 2 + q, q)
            sp.wait_ge(s["merged"], KD + 2)
            sp.wait_ge(s["spilled"], 16 * Q)
            sp.dma_start(x1[:, 0:NT, :], X["x0"][0:T, :].rearrange("(t p) d -> p t d", p=P)).then_inc(s["xback_in"], 16)
            sp.dma_start(x1[0:B, NT, :], X["x0"][T:N, :]).then_inc(s["xback_in"], 16)
            wg = I["e_gate"].rearrange("e (p c) n -> e p c n", c=KD)
            wu = I["e_up"].rearrange("e (p c) n -> e p c n", c=KD)
            wd = I["e_down"].rearrange("e (p c) n -> e p c n", c=FF // P)
            sp.dma_start(eg[0], wg[0]).then_inc(s["ew0g_in"], 16)
            sp.dma_start(eu[0], wu[0]).then_inc(s["ew0u_in"], 16)
            sp.dma_start(ed[0], wd[0]).then_inc(s["ew0d_in"], 16)
            sp.dma_start(eg[1], wg[1]).then_inc(s["ew1g_in"], 16)
            for t in range(Q):
                sp.wait_ge(s["x_normed"], Q + t + 1)
                sp.dma_start(X["x1"][t * P:t * P + rows(t), :], x1[0:rows(t), t, :]).then_inc(s["x1_spilled"], 16)
            sp.wait_ge(s["x_normed"], 2 * Q)
            sp.dma_start(gb[:, 0, :], I["ln2_g"].partition_broadcast(P)).then_inc(s["ln2_in"], 16)
            sp.dma_start(gb[:, 1, :], I["ln2_b"].partition_broadcast(P)).then_inc(s["ln2_in"], 16)

            sp.wait_ge(s["h_made"], Q)
            sp.dma_start(eu[1], wu[1]).then_inc(s["ew1u_in"], 16)
            sp.dma_start(ed[1], wd[1]).then_inc(s["ew1d_in"], 16)

            def expert_load(e):
                return [w[bass.ds(e, 1)].rearrange("e p c n -> (e p) c n") for w in (wg, wu, wd)]

            def extra_load(i):
                e = sp.value_load(ovfi.bitcast(I32)[0:1, bass.ds(i, 1)], min_val=0, max_val=NE - 1)
                sp.wait_ge(s["y_mm"], i + (NE + 2))
                for w, dst, what in zip(expert_load(e), (eg[0], eu[0], ed[0]), "gud"):
                    sp.dma_start(dst, w).then_inc(s[f"ew0{what}_in"], 16)

            with sp.Fori(0, NE // 2 - 1) as i:
                for q in range(2):
                    e = i * 2 + (q + 2)
                    sp.wait_ge(s["gate_mm"], e + 1)
                    sp.dma_start(eg[q], wg[bass.ds(e, 1)].rearrange("e p c n -> (e p) c n")).then_inc(s[f"ew{q}g_in"], 16)
                    sp.wait_ge(s["up_mm"], e + 1)
                    sp.dma_start(eu[q], wu[bass.ds(e, 1)].rearrange("e p c n -> (e p) c n")).then_inc(s[f"ew{q}u_in"], 16)
                    sp.wait_ge(s["y_mm"], e + 1)
                    sp.dma_start(ed[q], wd[bass.ds(e, 1)].rearrange("e p c n -> (e p) c n")).then_inc(s[f"ew{q}d_in"], 16)
            extra_blocks(sp, extra_load)
            sp.wait_ge(s["ovf_step"], 1)
            ya = X["ya"].rearrange("(t k) d -> t k d", k=2)
            for t in [tile_at(2, u) for u in range(Q)]:
                sp.dma_start(yk[0:rows(t), t, :, :], ya[t * P:t * P + rows(t), :, :]).then_inc(s[f"tile{t}_in"], 16)
            for u in range(Q):
                t = tile_at(2, u)
                sp.wait_ge(s["x_normed"], 2 * Q + u + 1)
                dst = O["y_prompt"][t * P:(t + 1) * P, :] if t < NT else O["y_sample"]
                sp.dma_start(dst, x1[0:rows(t), t, :]).then_inc(s["out_done"], 16)
            sp.wait_ge(s["out_done"], 16 * (13 + Q))
            sp.wait_ge(s["x1_spilled"], 16 * Q)

        @block.tensor
        def _(pe):
            def mm(out, a, b, start=True, stop=True):
                return pe.matmul(out, a, b, start=start, stop=stop)

            def turn(out, a):
                n = a.shape[0]
                b = a.start_partition() if n < P else 0
                return pe.transpose(out, a, ident[b:b + n, b:b + n])

            def gate_tile(k, q, n, b):
                pe.wait_ge(s[f"p1w{q}_in"], n * 16 + (16 * NF + 16))
                for h in range(2):
                    for c in range(KD):
                        last = mm(bank(b + h, NH), gcol[q][:, c, :], xT[:, c, h * NH:(h + 1) * NH], c == 0, c == KD - 1)
                last.then_inc(s["gate_made"], 1)

            pe.sem_inc(s["z_made"], 2)
            pe.wait_ge(s["ident_in"], 16)
            def turn_x(t):
                n = rows(t)
                pe.wait_ge(s["x_normed"], t + 1)
                if t >= 2:
                    pe.wait_ge(s["xT_ready"], t - 1)
                for c in range(KD):
                    last = turn(bank(2 * (t % 2), KD, P)[:, c, 0:n], xtok[0:n, t, c::KD])
                last.then_inc(s["x_turned"], 1)

            pe.wait_ge(s["mem_in"], 16)
            for t in range(2):
                for c in range(KD):
                    last = turn(bank(4 + 2 * t, KD, P)[:, c, :], memtok[:, t, c::KD])
                last.then_inc(s["mem_turned"], 1)
            pe.wait_ge(s["memT_ready"], 2)
            pe.wait_ge(s["wmem_in"], 16)
            for t in range(2):
                for c in range(KD):
                    last = mm(bank(4 + t, 512), memT[:, c, t * P:(t + 1) * P], wmem[:, c, :], c == 0, c == KD - 1)
                last.then_inc(s["mkv_made"], 1)
                for u in ((0, 1), (2, 3, 4))[t]:
                    turn_x(u)
            pe.wait_ge(s["mkv_ready"], 2)
            for f in range(2):
                for t in range(2):
                    last = turn(bank(6, 2, NMEM)[:, f, t * P:(t + 1) * P], mkv[:, t, f * P:(f + 1) * P])
            last.then_inc(s["mkv_made"], 1)
            pe.wait_ge(s["xT_ready"], Q)
            with pe.Fori(0, NF // 2) as i:
                for q in range(2):
                    pe.wait_ge(s[f"p1w{q}_in"], i * 32 + 32)
                    pe.wait_ge(s["z_ready"], i * 2 + q + 1)
                    for h in range(2):
                        for c in range(KD):
                            last = mm(bank(2 * q + h, NH), p1w[q][:, c, :], xT[:, c, h * NH:(h + 1) * NH], c == 0, c == KD - 1)
                    last.then_inc(s["z_made"], 1)
            pe.wait_ge(s["z_ready"], NF + 2)
            pe.wait_ge(s["mkT_ready"], 1)
            pe.wait_ge(s["params_in"], 80)
            turn(bank(7, PR_N), prow[0:PR_N, :]).then_inc(s["side_turned"], 1)
            for f in range(SF):
                last = turn(bank(0, C_SHIFT)[0:9, f * P:(f + 1) * P], z[:, f, T - 1:N])
            for f in range(SF):
                last = turn(bank(4, SF, B)[:, f, :], ssraw[0:B, f * P:(f + 1) * P])
            for t in range(NT):
                last = turn(bank(5, NT, P)[:, t, :], z[:, FV, t * P:(t + 1) * P])
            last = turn(bank(6, P)[0:B, :], z[:, FV, T:N])
            last.then_inc(s["side_turned"], 1)
            pe.wait_ge(s["side_ready"], SIDE_PARAMS)
            pe.wait_ge(s["side_ready"], SIDE_SHIFT)
            pe.wait_ge(s["consts_in"], 16)
            mm(bank(7, T), const("rot"), z[:, FK, 0:T])
            mm(bank(0, B), const("rot"), z[:, FK, T:N])
            mm(bank(1, NJ, B), const("rot"), z[:, FQ:FQ + NJ, T:N]).then_inc(s["rot_made"], 1)
            pe.wait_ge(s["kT_ready"], 1)
            turn(bank(2, P), kT[:, T:T + P])
            turn(bank(3, P)[0:B, :], kTs).then_inc(s["kout_turned"], 1)
            pe.wait_ge(s["kout_ready"], 1)
            pe.wait_ge(s["v_ready"], 1)

            for j in range(NJ):
                mm(bank(j, T), const("rot"), z[:, FQ + j, 0:T]).then_inc(s["rot_made"], 1)

            with pe.Fori(0, NT) as i:
                pe.wait_ge(s["blk_q"], i + 1)
                pe.wait_ge(s["blk_kv"], i * 2 + 1)
                for kv in range(2):
                    r = slice(kv * 64, kv * 64 + 64)
                    for j in range(NJ):
                        last = mm(bank(0, 12, 256)[:, kv * 4 + j, :], qs[r, j, :], kst[r, :])
                last.then_inc(s["blk_scores"], 1)
                for kv in range(2):
                    r = slice(kv * 64, kv * 64 + 64)
                    for m in range(2):
                        last = mm(bank(0, 12, 256)[:, 8 + kv * 2 + m, :], qs[r, 4 + m, :], mkT[r, m, :])
                last.then_inc(s["blk_scores"], 1)
                pe.wait_ge(s["blk_out"], i + 1)
                gate_tile(i * 2, 0, i, 6)
                pe.wait_ge(s["gate_out"], i * 2 + 1)
                gate_tile(i * 2 + 1, 1, i, 6)
                for half in range(2):
                    pe.wait_ge(s["blk_prob"], i * 2 + (half + 1))
                    for g in range(half * 12, half * 12 + 12):
                        last = turn(bank(0, 24, P)[:, g, :], S[:, g // 2, (g % 2) * P:(g % 2) * P + P])
                    last.then_inc(s["blk_turned"], 1)
                pe.wait_ge(s["blk_pT_act"], i * 2 + 2)
                pe.wait_ge(s["blk_pT_dve"], i + 1)
                pe.wait_ge(s["blk_kv"], i * 2 + 2)
                pe.wait_ge(s["gate_out"], i * 2 + 2)
                for kv in range(2):
                    r = slice(kv * 64, kv * 64 + 64)
                    for j in range(NJ):
                        for k in range(2):
                            mm(bank(6, NJ, P)[r, j, :], vst[:, k, r], PT[:, (kv * 4 + j) * 2 + k, :], k == 0, k == 1)
                    for m in range(2):
                        for k in range(2):
                            last = mm(bank(7, 2, P)[r, m, :], mkv[:, k, 256 + (2 * m + kv) * 64:320 + (2 * m + kv) * 64],
                                      PT[:, (8 + kv * 2 + m) * 2 + k, :], k == 0, k == 1)
                last.then_inc(s["blk_mixed"], 1)
            pe.wait_ge(s["blk_out"], NT + 1)

            for k in range(G_CACHE, G_BONUS):
                gate_tile(k, k % 2, k // 2, 2 * (k % 2))
            pe.wait_ge(s["gate_out"], G_BONUS)
            pe.wait_ge(s["cache_in"], 96)
            def turn_keys(b):
                if b >= 2:
                    pe.wait_ge(s["sk_ready"], b - 1)
                kp = bank(2 * (b % 2), 5, P)
                turn(kp[:, 0, :], kwin[:, b, :])
                for f in range(2):
                    for t in range(2):
                        last = turn(kp[:, 1 + 2 * f + t, :], kmem[:, b, t, f * P:(f + 1) * P])
                last.then_inc(s["sk_turned"], 1)

            turn_keys(0)
            for b in range(B):
                if b + 1 < B:
                    turn_keys(b + 1)
                pe.wait_ge(s["sk_ready"], b + 1)
                kt = kTb[b % 2]
                mm(bank(4, B, 8)[:, b, :], kt[:, 0, :], qbd[:, b, 0:8])
                for f in range(2):
                    for t in range(2):
                        last = mm(bank(6, 2, B, 2, 2)[:, t, b, f, :], kt[:, 1 + 2 * f + t, :], qbd[:, b, 8 + 2 * f:10 + 2 * f])
                last.then_inc(s["sk_scored"], 1)
            pe.wait_ge(s["sk_cols"], 1)
            turn(bank(0, P)[0:64, :], sST[:, 0:64])
            for t in range(2):
                last = turn(bank(1, 2, P)[0:32, t, :], sST[:, 64 + 32 * t:96 + 32 * t])
            last.then_inc(s["sk_rows"], 1)
            pe.wait_ge(s["sk_prob"], 1)
            turn(bank(2, 64), sW[0:64, :])
            for t in range(2):
                last = turn(bank(3, 2, 32)[:, t, :], sM[0:32, t, :])
            last.then_inc(s["sk_pT_made"], 1)
            pe.wait_ge(s["sk_pT_ready"], 1)
            for b in range(B):
                for kv in range(2):
                    r = slice(kv * 64, kv * 64 + 64)
                    mm(bank(4, B, NJ)[r, b, :], vwin[:, b, r], sWT[:, kv * 32 + b * 4:kv * 32 + b * 4 + 4])
                    for f in range(2):
                        for t in range(2):
                            last = mm(bank(5, B, 2)[r, b, f:f + 1], vmem[:, b, t, (2 * f + kv) * 64:(2 * f + kv) * 64 + 64],
                                      sMT[:, t, kv * 16 + b * 2 + f:kv * 16 + b * 2 + f + 1], t == 0, t == 1)
            last.then_inc(s["sk_mixed"], 1)

            pe.wait_ge(s["kk_sq"], 1)
            for h in range(2):
                for j in range(NJ):
                    last = mm(bank(6 + h, NH)[0:HA, :], const("sel8", NJ, HA)[:, j, :], sqb[:, j, h * NH:(h + 1) * NH], j == 0, j == 3)
            last.then_inc(s["head_sum"], 1)
            pe.wait_ge(s["sk_done"], 1)
            pe.wait_ge(s["lora_in"], 48)
            pe.wait_ge(s["lora_act"], 1)
            n = 0
            for what in range(3):
                for j in range(NJ):
                    if n >= 2:
                        pe.wait_ge(s["lora_sig"], n - 1)
                    for h in range(2):
                        cols = slice(h * NH, (h + 1) * NH)
                        a, b_ = [(wup[0:64, j * P:(j + 1) * P], th[0:64, cols]),
                                 (wup[64:128, j * P:(j + 1) * P], xwa[64:128, cols]),
                                 (gup[:, j * P:(j + 1) * P], xg_[:, cols])][what]
                        last = mm(bank(2 * (n % 2) + h, NH), a, b_)
                    last.then_inc(s["lora_mm"], 1)
                    n += 1
                    if what == 1:
                        if j == 0:
                            pe.wait_ge(s["head_recip"], 1)
                        else:
                            pe.wait_ge(s["prep_done"], j)
                        for h in range(2):
                            last = mm(bank(4 + h, NH), const("sel8t", NJ, P)[0:HA, j, :], rnk[0:HA, h * NH:(h + 1) * NH])
                        last.then_inc(s["kk_bcast"], 1)
            pe.wait_ge(s["lora_sig"], 12)
            gate_tile(G_BONUS, G_BONUS % 2, G_BONUS // 2, 0)
            pe.wait_ge(s["bonus_in"], 1)
            for j in range(NJ):
                if j >= 2:
                    pe.wait_ge(s["prep_done"], NJ + j - 1)
                for h in range(2):
                    last = mm(bank(4 + 2 * (j % 2) + h, NH), const("bones"), sqb[:, j, h * NH:(h + 1) * NH])
                last.then_inc(s["bonus_mm"], 1)
            pe.wait_ge(s["samp_stack"], 2)
            pe.wait_ge(s["prep_done"], 2 * NJ)
            pe.wait_ge(s["gate_out"], G_SAMP)
            for q in range(6):
                for j in range(NJ):
                    last = turn(bank(0, 6, C_A)[0:B, q, j * P:(j + 1) * P], sstk[:, q, j, :])
            last.then_inc(s["side_turned"], 1)
            for k in range(G_SAMP, G_TILE):
                if k == G_SAMP + 1:
                    pe.wait_ge(s["side_ready"], SIDE_SAMP)
                if k >= G_SAMP + 2:
                    pe.wait_ge(s["gate_out"], k - 1)
                gate_tile(k, k % 2, k // 2, 6 * (k % 2))
            pe.wait_ge(s["gate_out"], G_TILE)
            pe.wait_ge(s["samp_in"], 80)
            for j in range(NJ):
                last = turn(bank(6, NJ, B)[:, j, :], yrow[0:B, j * P:(j + 1) * P])
            last.then_inc(s["side_turned"], 1)
            pe.wait_ge(s["side_ready"], SIDE_YSAMP)

            with pe.Fori(0, NT) as i:
                gate_tile(i * 2 + G_TILE, 0, i + G_TILE // 2, 4)
                pe.wait_ge(s["tile_ready"], i + 1)
                pe.wait_ge(s["y_ready"], i + 1)
                for q, src in enumerate((AR[:, :, 0, :], Bt, Kt, Vt)):
                    for j in range(NJ):
                        last = turn(bank(q, NJ, P)[:, j, :], src[:, j, :])
                last.then_inc(s["tm_turned"], 1)
                pe.wait_ge(s["gate_out"], i * 2 + (G_TILE + 1))
                pe.sem_inc(s["pace"], 1)
                for par in range(2):
                    r = slice(par * 64, par * 64 + 64)
                    for j in range(NJ):
                        last = mm(bank(4 + 2 * par, NJ, 2, P)[:, j, :, :], Bt[r, j, :], AR[r, j, :, :])
                last.then_inc(s["tri_made"], 1)
                pe.wait_ge(s["tm_ready"], i + 1)
                for par in range(2):
                    r = slice(par * 64, par * 64 + 64)
                    for j in range(NJ):
                        last = mm(bank(2 * par, NJ, 2, P)[:, j, :, :], Kt[r, j, :], AR[r, j, :, :])
                last.then_inc(s["tri_made"], 1)
                pe.wait_ge(s["tri_ready"], i * 2 + 1)
                for par in range(2):
                    r = slice(par * 64, par * 64 + 64)
                    for j in range(NJ):
                        last = mm(bank(4 + par, NJ, P)[:, j, :], AR[r, j, 0, :], Bt[r, j, :])
                last.then_inc(s["tri_made"], 1)
                gate_tile(i * 2 + (G_TILE + 1), 1, i + G_TILE // 2, 6)
                pe.wait_ge(s["nk_ready"], i + 1)
                pe.wait_ge(s["tri_ready"], i * 2 + 2)
                for k in range(5):
                    for g in range(2):
                        if k:
                            pe.wait_ge(s["lvl_x_ready"], i * 10 + 2 * (k - 1) + g + 1)
                        for j in range(NJ):
                            last = mm(bank(g, NJ, P)[:, j, :], MR[:, g * 4 + j, 0, :], XX[:, g * 4 + j, 0, :])
                        last.then_inc(s["lvl_t1"], 1)
                    for g in range(2):
                        pe.wait_ge(s["lvl_t1_ready"], i * 10 + 2 * k + g + 1)
                        for j in range(NJ):
                            h = g * 4 + j
                            if k < 4:
                                mm(bank(2 + g, NJ, P)[:, j, :], XX[:, h, 1, :], T1[:, h, :])
                            last = mm(bank(4 + g, NJ, P)[:, j, :], T1[:, h, :], XX[:, h, 1, :])
                        last.then_inc(s["lvl_x"], 1)
                pe.wait_ge(s["lvl_x_ready"], i * 10 + 10)
                pe.wait_ge(s["gate_out"], i * 2 + (G_TILE + 2))
                for h in range(HA):
                    hd = (h % 4) * 2 + h // 4
                    last = mm(bank(6, HA, 64)[:, h, :], NR[:, h, 0, :], Vtok[:, hd * 64:hd * 64 + 64])
                last.then_inc(s["nv_made"], 1)
                pe.wait_ge(s["nv_ready"], i + 1)
                for h in range(HA):
                    last = mm(bank(0, HA, P)[:, h, :], XX[:, h, 1, :], ANV[:, h, :, :])
                last.then_inc(s["xav_made"], 1)
                pe.wait_ge(s["xav_ready"], i + 1)
                pe.sem_inc(s["pace"], 1)
                for c in range(2):
                    t_ = slice(c * 64, c * 64 + 64)
                    for h in range(HA):
                        j, par = h % 4, h // 4
                        hd = j * 2 + par
                        r = slice(par * 64, par * 64 + 64)
                        f = slice(hd * 64, hd * 64 + 64)
                        o_ = bank(4 + c, NJ, 2, 64)
                        mm(o_[r, j, 0, :], XAV[t_, h, 0, :], Btok[t_, f])
                        mm(o_[r, j, 1, :], Btok[t_, f], XAV[t_, h, 1, :], True, False)
                        last = mm(o_[r, j, 1, :], Ktok[t_, f], Vtok[t_, f], False, True)
                last.then_inc(s["gh_made"], 1)
                for h in range(HA):
                    j, par = h % 4, h // 4
                    hd = j * 2 + par
                    r = slice(par * 64, par * 64 + 64)
                    mm(bank(2, NJ, P)[r, j, :], XAV[:, h, 0, :], MR[:, h, 1, :])
                    mm(bank(3, NJ, P)[r, j, :], XAV[:, h, 1, :], MR[:, h, 1, :], True, False)
                    last = mm(bank(3, NJ, P)[r, j, :], Vtok[:, hd * 64:hd * 64 + 64], NR[:, h, 1, :], False, True)
                last.then_inc(s["ry_made"], 1)
                pe.wait_ge(s["gh_ready"], i + 1)
                for c in range(2):
                    pe.wait_ge(s["chain_done"], i * 2 + c + 1)
                    pe.sem_inc(s["pace"], 1)
                    for par in range(2):
                        r = slice(par * 64, par * 64 + 64)
                        for j in range(NJ):
                            last = mm(bank(6 + par, NJ, 64)[r, j, :], GT[r, c, j, :], SR[r, c, j, :])
                    last.then_inc(s["chain_mm"], 1)
                pe.wait_ge(s["ry_ready"], i + 1)
                pe.sem_inc(s["pace"], 1)
                for par in range(2):
                    r = slice(par * 64, par * 64 + 64)
                    for j in range(NJ):
                        for c in range(2):
                            last = mm(bank(par, NJ, P)[r, j, c * 64:c * 64 + 64], SR[r, c, j, :], Rh[r, j, c * 64:c * 64 + 64])
                last.then_inc(s["y_made"], 1)
            pe.wait_ge(s["y_ready"], NT + 1)
            pe.wait_ge(s["chain_done"], 2 * NT + 1)
            for j in range(NJ):
                last = turn(bank(2, NJ, P)[0:64, j, :], SR[:, 0, j, :])
            last.then_inc(s["side_turned"], 1)
            for j in range(NJ):
                if j >= 2:
                    pe.wait_ge(s["gn_center"], j - 1)
                for h in range(2):
                    last = mm(bank(4 + 2 * (j % 2) + h, NH), const("bones"), YT[:, j, h * NH:(h + 1) * NH])
                last.then_inc(s["gn_mean"], 1)
            branch = [(0, 4, lambda c: YT[:, c, :]), (4, 4, lambda c: z[:, FQ + c, :]), (8, 2, lambda c: z[:, FM + c, :])]

            def project(q, g, b):
                w0, nk, act = branch[g]
                for h in range(2):
                    for c in range(nk):
                        last = mm(bank(b + h, NH), mgw[q][:, w0 + c, :], act(c)[:, h * NH:(h + 1) * NH], c == 0, c == nk - 1)
                last.then_inc(s["proj_made"], 1)

            pe.wait_ge(s["fstate_ready"], 1)
            pe.wait_ge(s["mgw0_in"], 80)
            project(0, 1, 0)
            project(0, 2, 2)
            pe.wait_ge(s["gn_sq"], 1)
            for h in range(2):
                for j in range(NJ):
                    last = mm(bank(4 + h, NH)[0:HA, :], const("sel8", NJ, HA)[:, j, :], gsq[:, j, h * NH:(h + 1) * NH], j == 0, j == 3)
            last.then_inc(s["head_sum"], 1)
            pe.wait_ge(s["mgw1_in"], 80)
            for g in (1, 2):
                pe.wait_ge(s["proj_used"], g)
                project(1, g, 2 * (g - 1))
            pe.wait_ge(s["head_recip"], 2)
            for j in range(NJ):
                if j >= 2:
                    pe.wait_ge(s["gn_bcast"], j - 1)
                for h in range(2):
                    last = mm(bank(4 + 2 * (j % 2) + h, NH), const("sel8t", NJ, P)[0:HA, j, :], rn[0:HA, h * NH:(h + 1) * NH])
                last.then_inc(s["gn_mean"], 1)
            pe.wait_ge(s["oa_ready"], 1)
            for q in range(2):
                project(q, 0, 4 + 2 * q)
            with pe.Fori(1, KD // 2) as i:
                for q in range(2):
                    pe.wait_ge(s[f"mgw{q}_in"], i * 80 + 80)
                    for g in range(3):
                        step = q * 3 + g
                        pe.wait_ge(s["proj_used"], i * 6 + (step - 1))
                        project(q, g, 4 + 2 * (step % 2))
            pe.wait_ge(s["merged"], KD + 2)
            pe.wait_ge(s["out_in"], 80)
            def logits(u):
                pe.wait_ge(s["x1T_ready"], u + 1)
                for c in range(KD):
                    last = mm(bank(6, Q, NG + NE)[0:rows(u), u, :], x1T[:, c, u * P:u * P + rows(u)], wr[:, c, :], c == 0, c == KD - 1)
                return last

            for t in range(Q + 1):
                if t < Q:
                    n = rows(t)
                    if t >= 2:
                        pe.wait_ge(s["h_used"], t - 1)
                    for h in range(2):
                        for c in range(KD):
                            last = mm(bank(2 * (t % 2) + h, 512)[0:n, :], MG[:, c, t * P:t * P + n], wo[h][:, c, :], c == 0, c == KD - 1)
                    last.then_inc(s["h_made"], 1)
                if t >= 1:
                    u = t - 1
                    n = rows(u)
                    pe.wait_ge(s["x_normed"], Q + u + 1)
                    if u >= 1:
                        pe.wait_ge(s["x1T_ready"], u)
                    for c in range(KD):
                        last = turn(bank(4, KD, P)[:, c, 0:n], x1[0:n, u, c::KD])
                    last.then_inc(s["x1_turned"], 1)
                if t >= 2:
                    logits(t - 2)
            logits(Q - 1).then_inc(s["logits_made"], 1)
            pe.wait_ge(s["onehot_ready"], 1)
            mm(bank(1, Q, NE), const("ones"), earlier[:, 0:Q, :], True, False)
            mm(bank(1, Q, NE), const("before"), Osum, False, True)
            last = mm(bank(2, NE), const("ones"), earlier[:, Q, :])
            last.then_inc(s["rank_made"], 1)
            pe.wait_ge(s["route_ready"], 1)
            for t in range(Q):
                for k in range(2):
                    last = mm(bank(3, 2, NB), SK[:, k, t, :], VB[:, t, k, :, :], t == 0 and k == 0, t == Q - 1 and k == 1)
            last.then_inc(s["table_made"], 1)
            pe.wait_ge(s["table_ready"], 1)
            pe.sem_inc(s["gate_mm"], 2)
            pe.sem_inc(s["up_mm"], 2)
            pe.sem_inc(s["y_mm"], 2)

            def turn_rows(q):
                for c in range(KD):
                    last = turn(bank(0, KD, P)[:, c, :], xg[q][:, c::KD])
                last.then_inc(s["xg_turned"], 1)

            def gate(q):
                for c in range(KD):
                    last = mm(bank(2, FF), xgT[:, c, :], eg[q][:, c, :], c == 0, c == KD - 1)
                last.then_inc(s["gate_mm"], 1)

            def up(q):
                for c in range(KD):
                    last = mm(bank(3, FF), xgT[:, c, :], eu[q][:, c, :], c == 0, c == KD - 1)
                last.then_inc(s["up_mm"], 1)

            def turn_h():
                for c in range(FF // P):
                    last = turn(bank(4, 4, P)[:, c, :], hb[:, c::4])
                last.then_inc(s["hT_turned"], 1)

            def down(q):
                for h in range(2):
                    for c in range(FF // P):
                        last = mm(bank(5 + h, 512), hT[:, c, :], ed[q][:, c, h * 512:h * 512 + 512], c == 0, c == 3)
                last.then_inc(s["y_mm"], 1)

            def rows_step(e, q, n):
                pe.wait_ge(s[f"xg_in_{'ab'[q]}"], n * 16 + 16)
                turn_rows(q)

            def gate_step(e, q, n, first=False):
                pe.wait_ge(s["xgT_ready"], e + 1)
                if not first:
                    pe.wait_ge(s["h_ready"], e)
                pe.wait_ge(s[f"ew{q}g_in"], n * 16 + 16)
                gate(q)

            def up_step(e, q, n):
                pe.wait_ge(s[f"ew{q}u_in"], n * 16 + 16)
                up(q)

            def turn_h_step(e, q, n):
                pe.wait_ge(s["h_ready"], e + 1)
                turn_h()

            def down_step(e, q, n):
                pe.wait_ge(s["hT_ready"], e + 1)
                pe.wait_ge(s[f"ew{q}d_in"], n * 16 + 16)
                pe.wait_ge(s["yb_ready"], e + 1)
                down(q)

            def steady(e, q, n, before, after):
                gate_step(e, q, n)
                turn_h_step(*before)
                up_step(e, q, n)
                if after:
                    rows_step(*after)
                down_step(*before)

            rows_step(0, 0, 0)
            gate_step(0, 0, 0, first=True)
            up_step(0, 0, 0)
            rows_step(1, 1, 0)
            with pe.Fori(0, NE // 2 - 1) as i:
                e = i * 2
                steady(e + 1, 1, i, (e, 0, i), (e + 2, 0, i + 1))
                steady(e + 2, 0, i + 1, (e + 1, 1, i), (e + 3, 1, i + 1))
            last_n = NE // 2 - 1
            steady(NE - 1, 1, last_n, (NE - 2, 0, last_n), None)
            turn_h_step(NE - 1, 1, last_n)
            down_step(NE - 1, 1, last_n)

            def extra(i):
                b = (i + NE, 0, i + NE // 2)
                rows_step(*b)
                gate_step(*b)
                up_step(*b)
                turn_h_step(*b)
                down_step(*b)

            extra_blocks(pe, extra)

        @block.scalar
        def _(act):
            def copy(out, a):
                return act.activation(out, a, ACT.Copy)

            eps = const("eps")

            def layer_norm(x, pas, lag, before=None, after=None):
                for t in range(Q + lag):
                    if before:
                        before(t)
                    if t < Q:
                        i, n = tile_at(pas, t), rows(tile_at(pas, t))
                        act.wait_ge(s["ln_stats"], pas * Q + t + 1)
                        act.activation(rstd[0:n, i, :], mv[0:n, i, 1:2], ACT.Sqrt, bias=eps[0:n, 0:1]).then_inc(s["ln_std"], 1)
                    u = t - lag
                    if u >= 0:
                        i, n = tile_at(pas, u), rows(tile_at(pas, u))
                        act.wait_ge(s["ln_rs"], pas * Q + u + 1)
                        act.activation(x[0:n, i, :], x[0:n, i, :], ACT.Identity, bias=nmr[0:n, i, :],
                                       scale=rstd[0:n, i, :]).then_inc(s["ln_scaled"], 1)
                    if after:
                        after(t)

            act.wait_ge(s["ident_in"], 16)

            def x_turned(t):
                n = rows(t)
                act.wait_ge(s["x_turned"], t + 1)
                copy(xT[:, :, t * P:t * P + n], bank(2 * (t % 2), KD, P)[:, :, 0:n]).then_inc(s["xT_ready"], 1)

            def mem_turned(t):
                if t < 2:
                    act.wait_ge(s["mem_turned"], t + 1)
                    copy(memT[:, :, t * P:(t + 1) * P], bank(4 + 2 * t, KD, P)).then_inc(s["memT_ready"], 1)

            layer_norm(xtok, 0, 1, after=lambda t: mem_turned(t - 1) if t >= 1 else None)
            for t in range(2):
                act.wait_ge(s["mkv_made"], t + 1)
                copy(mkv[:, t, :], bank(4 + t, 512)).then_inc(s["mkv_ready"], 1)
                for u in ((0, 1), (2, 3, 4))[t]:
                    x_turned(u)
            act.wait_ge(s["mkv_made"], 3)
            copy(mkT, bank(6, 2, NMEM)).then_inc(s["mkT_ready"], 1)
            act.sem_inc(s["z_ready"], 2)
            with act.Fori(0, NF // 2) as i:
                for q in range(2):
                    act.wait_ge(s["z_made"], i * 2 + q + 3)
                    copy(z[:, bass.ds(i * 2 + q, 1), :].rearrange("p a (h n) -> p (a h) n", h=2),
                         psum[:, 2 * q:2 * q + 2, 0:NH]).then_inc(s["z_ready"], 1)
            act.wait_ge(s["side_turned"], SIDE_PARAMS)
            copy(prm, bank(7, PR_N)).then_inc(s["side_ready"], 1)
            act.wait_ge(s["side_turned"], SIDE_SHIFT)
            copy(shb[0:9, :], bank(0, C_SHIFT)[0:9, :])
            copy(sstT, bank(4, SF, B)).then_inc(s["side_ready"], 1)
            copy(vtok[:, 1:, :], bank(5, NT, P))
            copy(vss[0:B, :], bank(6, P)[0:B, :]).then_inc(s["v_ready"], 1)
            act.wait_ge(s["kout_turned"], 1)
            copy(ktl, bank(2, P))
            copy(kss[0:B, :], bank(3, P)[0:B, :]).then_inc(s["kout_ready"], 1)

            def gate_take(k, q, n, b):
                act.wait_ge(s["gate_made"], k + 1)
                act.wait_ge(s[f"gate_spill{q}"], n * 16 + 16)
                copy(gout[q].rearrange("p (h n) -> p h n", h=2), psum[:, b:b + 2, 0:NH]).then_inc(s["gate_out"], 1)

            act.wait_ge(s["kT_ready"], 1)
            for q in range(2):
                act.sem_inc(s[f"gate_spill{q}"], 16)
            act.sem_inc(s["blk_out"], 1)
            with act.Fori(0, NT) as i:
                act.wait_ge(s["blk_max"], i + 1)
                for h in range(8):
                    act.activation(S[:, h, :], S[:, h, :], ACT.Exp, bias=nmx[:, h:h + 1], accum_out=den[:, h:h + 1])
                for h in range(8, 12):
                    act.activation(S[:, h, :], bank(0, 12, 256)[:, h, :], ACT.Exp, bias=nmx[:, h:h + 1], scale=0.125,
                                   accum_out=den[:, h:h + 1])
                act.activation(ske, ske, ACT.Exp).then_inc(s["blk_exp"], 1)
                gate_take(i * 2 + 1, 1, i, 6)
                act.wait_ge(s["blk_turned"], i * 2 + 1)
                copy(PT[:, 0:12, :], bank(0, 12, P)).then_inc(s["blk_pT_act"], 1)
                act.wait_ge(s["blk_turned"], i * 2 + 2)
                copy(PT[:, 20:24, :], bank(5, 4, P)).then_inc(s["blk_pT_act"], 1)
                act.wait_ge(s["blk_mixed"], i + 1)
                cols = bass.ds(i * P, P)
                copy(z[:, FQ:FQ + NJ, cols], bank(6, NJ, P))
                copy(z[:, FM:FM + 2, cols], bank(7, 2, P)).then_inc(s["blk_out"], 1)

            for k in range(G_CACHE, G_BONUS):
                gate_take(k, k % 2, k // 2, 2 * (k % 2))

            act.wait_ge(s["zs_ready"], 1)
            for j in range(NJ):
                last = act.activation(sqb[:, j, :], kTr[:, j, :], ACT.Square, scale=prm[:, PR_KK + j:PR_KK + j + 1])
            last.then_inc(s["kk_sq"], 1)
            act.activation(th[0:64, :], xwa[0:64, :], ACT.Tanh)
            act.activation(xg_, xg_, ACT.Sigmoid).then_inc(s["lora_act"], 1)

            for b in range(B):
                act.wait_ge(s["sk_turned"], b + 1)
                if b >= 2:
                    act.wait_ge(s["sk_scored"], b - 1)
                copy(kTb[b % 2], bank(2 * (b % 2), 5, P)).then_inc(s["sk_ready"], 1)
            act.wait_ge(s["sk_scored"], B)
            copy(sST[:, 0:64].rearrange("p (k b j) -> p k b j", k=2, b=B), bank(4, B, 2, NJ).rearrange("p b k j -> p k b j"))
            for t in range(2):
                last = copy(sST[:, 64 + 32 * t:96 + 32 * t].rearrange("p (k b f) -> p k b f", k=2, b=B),
                            bank(6, 2, B, 2, 2)[:, t].rearrange("p b f k -> p k b f"))
            last.then_inc(s["sk_cols"], 1)
            act.wait_ge(s["sk_max"], 1)
            act.activation(sW[0:64, :], bank(0, P)[0:64, :], ACT.Exp, bias=snmx[0:64, 0:1], scale=0.125, accum_out=sden[0:64, 0:1])
            act.activation(sM[0:32, :, :], bank(1, 2, P)[0:32, :, :], ACT.Exp, bias=snmx[0:32, 1:2], scale=0.125,
                           accum_out=sden[0:32, 1:2])
            act.activation(sske[0:64, 0:1], sske[0:64, 0:1], ACT.Exp).then_inc(s["sk_exp"], 1)
            act.wait_ge(s["sk_pT_made"], 1)
            copy(sWT, bank(2, 64))
            copy(sMT, bank(3, 2, 32)).then_inc(s["sk_pT_ready"], 1)
            act.wait_ge(s["sk_mixed"], 1)
            copy(z[:, FQ:FQ + NJ, T:N], bank(4, B, NJ).rearrange("p b j -> p j b"))
            copy(z[:, FM:FM + 2, T:N], bank(5, B, 2).rearrange("p b j -> p j b")).then_inc(s["sk_done"], 1)

            act.wait_ge(s["head_sum"], 1)
            act.activation(rnk[0:HA, :].rearrange("p (h n) -> p h n", h=2), psum[0:HA, 6:8, 0:NH], ACT.Sqrt).then_inc(s["head_root"], 1)
            n = 0
            for what in range(3):
                for j in range(NJ):
                    act.wait_ge(s["lora_mm"], n + 1)
                    src = psum[:, 2 * (n % 2):2 * (n % 2) + 2, 0:NH]
                    dst = (sg, ah, gT)[what][:, j, :].rearrange("p (h n) -> p h n", h=2)
                    if what < 2:
                        r0 = (PR_W0, PR_A0)[what] + j
                        last = act.activation(dst, src, ACT.Sigmoid, bias=prm[:, r0:r0 + 1])
                    else:
                        last = copy(dst, src)
                    last.then_inc(s["lora_sig"], 1)
                    n += 1
            act.drain()
            act.activation(wS, sg[:, :, T:N], ACT.Exp, scale=-DECAY).then_inc(s["samp_stack"], 1)
            gate_take(G_BONUS, G_BONUS % 2, G_BONUS // 2, 0)
            act.wait_ge(s["side_turned"], SIDE_SAMP)
            copy(srow[0:B, :, :], bank(0, 6, C_A)[0:B, :, :]).then_inc(s["side_ready"], 1)
            for k in range(G_SAMP, G_TILE):
                gate_take(k, k % 2, k // 2, 6 * (k % 2))
            act.wait_ge(s["side_turned"], SIDE_YSAMP)
            copy(YT[:, :, T:N], bank(6, NJ, B)).then_inc(s["side_ready"], 1)

            act.wait_ge(s["prep_done"], 2 * NJ + 1)
            with act.Fori(0, NT) as i:
                cols = bass.ds(i * P, P)
                act.wait_ge(s["y_ready"], i + 1)
                act.wait_ge(s["decay_arg"], i + 1)
                act.activation(Pinc, Lc[:, :, cols], ACT.Exp, scale=-DECAY)
                act.activation(Pinv, Lc[:, :, cols], ACT.Exp, scale=DECAY)
                act.activation(Pexc, Pexc, ACT.Exp, scale=-DECAY).then_inc(s["exps_made"], 1)
                gate_take(i * 2 + G_TILE, 0, i + G_TILE // 2, 4)
                act.wait_ge(s["tm_turned"], i + 1)
                copy(ANV[:, :, 0, :].rearrange("p (e j) k -> p e j k", e=2),
                     bank(0, NJ, 2, 64).rearrange("p j e k -> p e j k"))
                copy(Btok, bank(1, 512))
                copy(Ktok, bank(2, 512))
                copy(Vtok, bank(3, 512)).then_inc(s["tm_ready"], 1)
                gate_take(i * 2 + (G_TILE + 1), 1, i + G_TILE // 2, 6)
                act.wait_ge(s["nv_made"], i + 1)
                copy(ANV[:, :, 1, :], bank(6, HA, 64)).then_inc(s["nv_ready"], 1)
                act.wait_ge(s["xav_made"], i + 1)
                copy(XAV, bank(0, HA, 2, 64)).then_inc(s["xav_ready"], 1)
                act.wait_ge(s["ry_made"], i + 1)
                copy(Yl, bank(3, NJ, P)).then_inc(s["ry_ready"], 1)
            act.wait_ge(s["side_turned"], SIDE_STATE)
            copy(fst[0:64, :, :], bank(2, HA, 64)[0:64, :, :]).then_inc(s["fstate_ready"], 1)
            def gate_sigmoids(q, n):
                act.wait_ge(s[f"mgw{q}_in"], n * 80 + 80)
                act.activation(mgg[q], mgg[q], ACT.Sigmoid).then_inc(s["gate_sig"], 1)

            gate_sigmoids(0, 0)
            act.wait_ge(s["gn_sq"], 1)
            act.wait_ge(s["head_sum"], 2)
            act.activation(rn[0:HA, :].rearrange("p (h n) -> p h n", h=2), psum[0:HA, 4:6, 0:NH], ACT.Sqrt,
                           scale=1.0 / 64, bias=eps[0:HA, 1:2]).then_inc(s["head_root"], 1)

            gate_sigmoids(1, 0)
            with act.Fori(1, KD // 2) as i:
                for q in range(2):
                    gate_sigmoids(q, i)

            def x1_turned(t):
                n = rows(t)
                act.wait_ge(s["x1_turned"], t + 1)
                copy(x1T[:, :, t * P:t * P + n], bank(4, KD, P)[:, :, 0:n]).then_inc(s["x1T_ready"], 1)

            layer_norm(x1, 1, 0, before=lambda t: x1_turned(t - 1) if t >= 1 else None)
            x1_turned(Q - 1)
            act.wait_ge(s["exp_asked"], 1)
            act.activation(t4, t4, ACT.Exp).then_inc(s["exp_made"], 1)
            act.wait_ge(s["exp_asked"], 2)
            act.activation(e2, e2, ACT.Exp).then_inc(s["exp_made"], 1)

            act.wait_ge(s["table_ready"], 1)
            def turned_rows(e):
                act.wait_ge(s["xg_turned"], e + 1)
                copy(xgT, bank(0, KD, P)).then_inc(s["xgT_ready"], 1)

            def gate_sigmoid(e):
                act.wait_ge(s["gate_mm"], e + 3)
                act.activation(esig, bank(2, FF), ACT.Sigmoid).then_inc(s["gate_act"], 1)

            turned_rows(0)
            with act.Fori(0, NE - 1) as e:
                gate_sigmoid(e)
                act.wait_ge(s["up_mm"], e + 3)
                turned_rows(e + 1)
            gate_sigmoid(NE - 1)

            def extra_act(i):
                turned_rows(i + NE)
                gate_sigmoid(i + NE)

            extra_blocks(act, extra_act)
            layer_norm(x1, 2, 1)

        @block.vector
        def _(v):
            tab, ix = tabi.bitcast(U32), idx.bitcast(U32)

            def tt(out, a, b, op):
                return v.tensor_tensor(out, a, b, op)

            def stt(out, a, sc, b, op0, op1):
                return v.scalar_tensor_tensor(out, a, sc, b, op0, op1)

            def ts(out, a, s1, op0, s2=None, op1=None):
                if op1 is None:
                    return v.tensor_scalar(out, a, s1, None, op0)
                return v.tensor_scalar(out, a, s1, s2, op0, op1)

            def layer_norm(x, pas, before, lag):
                for t in range(Q + 2 * lag):
                    if t < Q:
                        i, n = tile_at(pas, t), rows(tile_at(pas, t))
                        before(i, t)
                        for h in range(2):
                            v.bn_stats(st6[0:n, i, h, :], x[0:n, i, h * 512:(h + 1) * 512])
                        v.drain()
                        v.bn_aggr(mv[0:n, i, :], st6[0:n, i, :, :]).then_inc(s["ln_stats"], 1)
                    u = t - lag
                    if 0 <= u < Q:
                        i, n = tile_at(pas, u), rows(tile_at(pas, u))
                        v.wait_ge(s["ln_std"], pas * Q + u + 1)
                        v.reciprocal(rstd[0:n, i, :], rstd[0:n, i, :])
                        v.drain()
                        stt(nmr[0:n, i, :], mv[0:n, i, 0:1], -1.0, rstd[0:n, i, :], ALU.mult, ALU.mult).then_inc(s["ln_rs"], 1)
                    u = t - 2 * lag
                    if u >= 0:
                        i, n = tile_at(pas, u), rows(tile_at(pas, u))
                        v.wait_ge(s["ln_scaled"], pas * Q + u + 1)
                        tt(x[0:n, i, :], x[0:n, i, :], gb[0:n, 0, :], ALU.mult).then_inc(s["ln_gained"], 1)

            def rows_in(t, at):
                v.wait_ge(s[f"tile{t}_in"], 16)
                if t == 2:
                    v.wait_ge(s["x_in"], 32)

            layer_norm(xtok, 0, rows_in, 1)

            v.wait_ge(s["mkT_ready"], 1)
            v.memset(kT[:, 0:P], 0.0)
            v.memset(vtok[:, 0, :], 0.0)
            v.wait_ge(s["z_ready"], NF + 2)
            cos, sin = const("cos"), const("sin")
            v.wait_ge(s["consts_in"], 16)
            v.wait_ge(s["rot_made"], 1)
            v.wait_ge(s["spilled"], 16 * Q)
            tt(kT[:, P:], z[:, FK, 0:T], cos[:, 0:T], ALU.mult)
            tt(view(Fo, T), bank(7, T), sin[:, 0:T], ALU.mult)
            tt(kTs, z[:, FK, T:N], cos[:, T:N], ALU.mult)
            tt(view(Fo + 512, B), bank(0, B), sin[:, T:N], ALU.mult)
            tt(qsS[:, 0:4, :], z[:, FQ:FQ + NJ, T:N], bc(cos[:, T:N], 1, NJ), ALU.mult)
            tt(view(Fo + 520, NJ, B), bank(1, NJ, B), bc(sin[:, T:N], 1, NJ), ALU.mult)
            v.tensor_copy(qsS[:, 4:6, :], z[:, FM:FM + 2, T:N])
            v.drain()
            tt(kT[:, P:], kT[:, P:], view(Fo, T), ALU.add)
            tt(qsS[:, 0:4, :], qsS[:, 0:4, :], view(Fo + 520, NJ, B), ALU.add)
            tt(kTs, kTs, view(Fo + 512, B), ALU.add).then_inc(s["kT_ready"], 1)
            v.memset(qbd, 0.0)
            v.drain()
            for kv in range(2):
                r = slice(kv * 64, kv * 64 + 64)
                v.tensor_copy(qbd[r, :, kv * 4:kv * 4 + 4].rearrange("p b j -> p j b"), qsS[r, 0:4, :])
                v.tensor_copy(qbd[r, :, 8 + kv::2].rearrange("p b f -> p f b"), qsS[r, 4:6, :])

            v.wait_ge(s["params_in"], 80)
            v.wait_ge(s["mkv_made"], 2)
            for j in range(NJ):
                v.wait_ge(s["rot_made"], j + 2)
                tt(z[:, FQ + j, 0:T], z[:, FQ + j, 0:T], cos[:, 0:T], ALU.mult)
                tt(tmpq[:, j, :], bank(j, T), sin[:, 0:T], ALU.mult)
            v.drain()
            tt(z[:, FQ:FQ + NJ, 0:T], z[:, FQ:FQ + NJ, 0:T], tmpq, ALU.add)
            v.drain()

            def block_queries(cols):
                v.tensor_copy(qs[:, 4:6, :], z[:, FM:FM + 2, cols])
                v.tensor_copy(qs[:, 0:4, :], z[:, FQ:FQ + NJ, cols]).then_inc(s["blk_q"], 1)

            block_queries(slice(0, P))

            def block_softmax(i, ahead):
                v.wait_ge(s["blk_scores"], i * 2 + 1)
                v.wait_ge(s["blk_kv"], i * 2 + 1)
                stt(S[:, 0:8, :], bank(0, 8, 256), 0.125, bc(mst, 1, 8), ALU.mult, ALU.add)
                v.wait_ge(s["blk_scores"], i * 2 + 2)
                v.tensor_reduce(mx[:, 8:12], bank(4, 4, 256), AX.X, ALU.max)
                v.drain()
                v.tensor_reduce(mx[:, 0:8], S[:, 0:8, :], AX.X, ALU.max)
                ts(nmx[:, 8:12], mx[:, 8:12], -0.125, ALU.mult)
                v.drain()
                tt(mx[:, 0:8], mx[:, 0:8], sink_bc, ALU.max)
                v.drain()
                ts(nmx[:, 0:8], mx[:, 0:8], -1.0, ALU.mult)
                v.drain()
                tt(ske, sink_bc, nmx[:, 0:8], ALU.add).then_inc(s["blk_max"], 1)
                v.wait_ge(s["gate_made"], i * 2 + 1)
                v.wait_ge(s["gate_spill0"], i * 16 + 16)
                v.tensor_copy(gout[0].rearrange("p (h n) -> p h n", h=2), psum[:, 6:8, 0:NH]).then_inc(s["gate_out"], 1)
                if ahead:
                    block_queries(bass.ds(i * P + P, P))
                v.wait_ge(s["blk_exp"], i + 1)
                tt(den[:, 0:8], den[:, 0:8], ske, ALU.add)
                v.drain()
                v.reciprocal(rden, den)
                v.drain()
                for h in (slice(0, 6), slice(6, 12)):
                    tt(S[:, h, :], S[:, h, :], bc(rden[:, h], 2, 256), ALU.mult).then_inc(s["blk_prob"], 1)
                v.wait_ge(s["blk_turned"], i * 2 + 2)
                v.tensor_copy(PT[:, 12:20, :], bank(3, 8, P)).then_inc(s["blk_pT_dve"], 1)

            with v.Fori(0, NT - 1) as i:
                block_softmax(i, True)
            block_softmax(NT - 1, False)

            v.wait_ge(s["side_ready"], SIDE_SHIFT)
            tt(zs[:, :, 1:T], z[:, 0:SF, 0:T - 1], z[:, 0:SF, 1:T], ALU.subtract)
            ts(zs[:, :, 0:1], z[:, 0:SF, 0:1], -1.0, ALU.mult)
            tt(zs[:, :, T:N], sstT, z[:, 0:SF, T:N], ALU.subtract)
            v.drain()
            for f in range(SF):
                last = stt(zs[:, f, :], zs[:, f, :], prm[:, PR_MU + f:PR_MU + f + 1], z[:, f, :], ALU.mult, ALU.add)
            last.then_inc(s["zs_ready"], 1)

            v.wait_ge(s["sk_rows"], 1)
            v.tensor_reduce(smx[0:64, 0:1], bank(0, P)[0:64, :], AX.X, ALU.max)
            v.tensor_reduce(smx[0:32, 1:2], bank(1, 2 * P)[0:32, :], AX.X, ALU.max)
            v.drain()
            ts(smx[0:64, 0:1], smx[0:64, 0:1], 0.125, ALU.mult)
            ts(snmx[0:32, 1:2], smx[0:32, 1:2], -0.125, ALU.mult)
            v.drain()
            tt(smx[0:64, 0:1], smx[0:64, 0:1], sink_row[0:64, :], ALU.max)
            v.drain()
            ts(snmx[0:64, 0:1], smx[0:64, 0:1], -1.0, ALU.mult)
            v.drain()
            tt(sske[0:64, 0:1], sink_row[0:64, :], snmx[0:64, 0:1], ALU.add).then_inc(s["sk_max"], 1)
            v.wait_ge(s["sk_exp"], 1)
            tt(sden[0:64, 0:1], sden[0:64, 0:1], sske[0:64, 0:1], ALU.add)
            v.drain()
            v.reciprocal(srd[0:64, 0:1], sden[0:64, 0:1])
            v.reciprocal(srd[0:32, 1:2], sden[0:32, 1:2])
            v.drain()
            ts(sW[0:64, :], sW[0:64, :], srd[0:64, 0:1], ALU.mult)
            ts(sM[0:32, :, :], sM[0:32, :, :], srd[0:32, 1:2], ALU.mult).then_inc(s["sk_prob"], 1)

            def pcol(r0, j):
                return prm[:, r0 + j:r0 + j + 1]

            def halves(ap):
                return ap.rearrange("p (h n) -> p h n", h=2)

            v.wait_ge(s["head_root"], 1)
            ts(rnk[0:HA, :], rnk[0:HA, :], 1e-12, ALU.max)
            v.drain()
            v.reciprocal(rnk[0:HA, :], rnk[0:HA, :]).then_inc(s["head_recip"], 1)
            for j in range(NJ):
                v.wait_ge(s["kk_bcast"], j + 1)
                stt(halves(kk[:, j, :]), halves(kTr[:, j, :]), pcol(PR_KK, j), psum[:, 4:6, 0:NH], ALU.mult, ALU.mult).then_inc(s["prep_done"], 1)
            v.wait_ge(s["lora_sig"], 8)
            for j in range(NJ):
                ts(sqb[:, j, :], ah[:, j, :], 1.0, ALU.subtract, pcol(PR_KA, j), ALU.mult)
            v.drain()
            tt(ah, kk, ah, ALU.mult)
            stt(kTr, sqb, 1.0, kTr, ALU.add, ALU.mult)
            v.drain()
            for j in range(NJ):
                last = stt(sqb[:, j, :], rT[:, j, :], pcol(PR_RK, j), kTr[:, j, :], ALU.mult, ALU.mult)
            last.then_inc(s["bonus_in"], 1)
            for j in range(NJ):
                v.wait_ge(s["bonus_mm"], j + 1)
                tt(halves(BV[:, j, :]), halves(vT[:, j, :]), psum[:, 4 + 2 * (j % 2):6 + 2 * (j % 2), 0:NH], ALU.mult).then_inc(s["prep_done"], 1)
            v.wait_ge(s["samp_stack"], 1)
            ts(sstk[:, 0, :, :], kk[:, :, T:N], -1.0, ALU.mult)
            v.tensor_copy(sstk[:, 1, :, :], wS)
            v.tensor_copy(sstk[:, 2, :, :], kTr[:, :, T:N])
            v.tensor_copy(sstk[:, 3, :, :], vT[:, :, T:N])
            v.tensor_copy(sstk[:, 4, :, :], ah[:, :, T:N])
            v.tensor_copy(sstk[:, 5, :, :], rT[:, :, T:N]).then_inc(s["samp_stack"], 1)
            for j in range(NJ):
                v.tensor_tensor_scan(Lc[:, j, :], const("reset"), sg[:, j, 0:T], 0.0, ALU.mult, ALU.add)
            v.memset(SR[:, 0, :, :], 0.0)
            v.drain()
            for j in range(NJ):
                ts(BV[:, j, :], BV[:, j, :], pcol(PR_LB, j), ALU.add)
            v.drain()
            v.sem_inc(s["prep_done"], 1)
            v.wait_ge(s["samp_in"], 64)
            v.wait_ge(s["state_in"], 32)

            def key(q):
                return bc(vec[:, q, :], 1, 32)

            tt(sTmp, sS, key(0), ALU.mult)
            v.drain()
            v.tensor_reduce(sa, sTmp, AX.X, ALU.add)
            tt(sS, sS, key(1), ALU.mult)
            v.drain()
            tt(sTmp, key(4), bc(sa, 2, 64), ALU.mult)
            v.drain()
            tt(sS, sS, sTmp, ALU.add)
            v.drain()
            tt(sTmp, key(2), bc(vvh, 2, 64), ALU.mult)
            v.drain()
            tt(sS, sS, sTmp, ALU.add)
            v.drain()
            tt(sTmp, sS, key(5), ALU.mult)
            v.drain()
            v.tensor_reduce(sy, sTmp, AX.X, ALU.add).then_inc(s["samp_state"], 1)
            v.wait_ge(s["side_turned"], SIDE_YSAMP)
            v.wait_ge(s["out_done"], 16 * 12)

            v.sem_inc(s["y_ready"], 1)
            v.sem_inc(s["chain_done"], 1)
            up2, lows = const("upper2", 2, P), [const(f"level{k}") for k in range(1, 6)]
            with v.Fori(0, NT) as i:
                cols = bass.ds(i * P, P)
                tt(Pexc, Lc[:, :, cols], sg[:, :, cols], ALU.subtract).then_inc(s["decay_arg"], 1)
                v.wait_ge(s["exps_made"], i + 1)
                stt(AR[:, :, 0, :], kk[:, :, cols], -1.0, Pexc, ALU.mult, ALU.mult)
                tt(AR[:, :, 1, :], rT[:, :, cols], Pinc, ALU.mult)
                tt(Bt, ah[:, :, cols], Pinv, ALU.mult)
                tt(Kt, kTr[:, :, cols], Pinv, ALU.mult)
                v.tensor_copy(pc2, Pinc.rearrange("p j (c n) -> p c j n", c=2)[:, :, :, CH - 1])
                v.tensor_copy(Vt, vT[:, :, cols]).then_inc(s["tile_ready"], 1)
                v.wait_ge(s["tri_made"], i * 3 + 1)
                tt(MR, bank(4, HA, 2, P), bc(up2, 1, HA), ALU.mult).then_inc(s["tri_ready"], 1)
                v.wait_ge(s["tri_made"], i * 3 + 2)
                tt(NR, bank(0, HA, 2, P), bc(up2, 1, HA), ALU.mult).then_inc(s["nk_ready"], 1)
                v.wait_ge(s["tri_made"], i * 3 + 3)
                for par in range(2):
                    tt(XX[:, par * 4:par * 4 + 4, 0, :], bank(4 + par, NJ, P), bc(const("low1"), 1, NJ), ALU.mult)
                tt(XX[:, :, 1, :], MR[:, :, 0, :], bc(const("up1"), 1, HA), ALU.mult)
                v.drain()
                tt(XX, XX, bc(bc(ident, 1, 2), 1, HA), ALU.add).then_inc(s["tri_ready"], 1)
                for k in range(5):
                    for g in range(2):
                        v.wait_ge(s["lvl_t1"], i * 10 + 2 * k + g + 1)
                        tt(T1[:, g * 4:g * 4 + 4, :], bank(g, NJ, P), bc(lows[k], 1, NJ), ALU.mult).then_inc(s["lvl_t1_ready"], 1)
                    for g in range(2):
                        v.wait_ge(s["lvl_x"], i * 10 + 2 * k + g + 1)
                        h = slice(g * 4, g * 4 + 4)
                        if k < 4:
                            tt(XX[:, h, 0, :], XX[:, h, 0, :], bank(2 + g, NJ, P), ALU.add).then_inc(s["lvl_x_ready"], 1)
                            tt(XX[:, h, 1, :], XX[:, h, 1, :], bank(4 + g, NJ, P), ALU.add)
                        else:
                            tt(XX[:, h, 1, :], XX[:, h, 1, :], bank(4 + g, NJ, P), ALU.add).then_inc(s["lvl_x_ready"], 1)
                v.wait_ge(s["gh_made"], i + 1)
                for c in range(2):
                    for r in (slice(0, 64), slice(64, 128)):
                        tt(GT[r, c, :, :], bank(4 + c, NJ, 2, 64)[r, :, 0, :], bc(ident[r, r], 1, NJ), ALU.add)
                    last = v.tensor_copy(Hm[:, c, :, :], bank(4 + c, NJ, 2, 64)[:, :, 1, :])
                last.then_inc(s["gh_ready"], 1)
                v.wait_ge(s["ry_made"], i + 1)
                tt(Rh, bank(2, NJ, P), AR[:, :, 1, :], ALU.add)
                for c in range(2):
                    v.wait_ge(s["chain_mm"], i * 2 + c + 1)
                    for par in range(2):
                        r = slice(par * 64, par * 64 + 64)
                        tt(SR[r, c + 1, :, :], bank(6 + par, NJ, 64)[r, :, :], Hm[r, c, :, :], ALU.add)
                    v.drain()
                    last = tt(SR[:, c + 1, :, :], SR[:, c + 1, :, :], bc(pc2[:, c, :], 2, 64), ALU.mult)
                    if c == 0:
                        last.then_inc(s["chain_done"], 1)
                v.wait_ge(s["y_made"], i + 1)
                v.wait_ge(s["ry_ready"], i + 1)
                for par in range(2):
                    r = slice(par * 64, par * 64 + 64)
                    tt(YT[r, :, cols], bank(par, NJ, P)[r, :, :], Yl[r, :, :], ALU.add)
                v.drain()
                v.sem_inc(s["y_ready"], 1)
                v.tensor_copy(SR[:, 0, :, :], SR[:, 2, :, :]).then_inc(s["chain_done"], 1)

            v.drain()
            v.sem_inc(s["merged"], 2)

            v.wait_ge(s["side_ready"], SIDE_YSAMP)
            v.wait_ge(s["side_turned"], SIDE_STATE)
            v.drain()
            for j in range(NJ):
                v.wait_ge(s["gn_mean"], j + 1)
                stt(halves(YT[:, j, :]), psum[:, 4 + 2 * (j % 2):6 + 2 * (j % 2), 0:NH], -1.0 / 64, halves(YT[:, j, :]),
                    ALU.mult, ALU.add).then_inc(s["gn_center"], 1)
            v.drain()
            tt(gsq, YT, YT, ALU.mult).then_inc(s["gn_sq"], 1)

            def gated(o, q, g, b, first):
                dst = MG[:, bass.ds(o, 1), :].rearrange("p a (h n) -> p (a h) n", h=2)
                pj = psum[:, b:b + 2, 0:NH]
                if first:
                    tt(dst, halves(mgg[q][:, g, :]), pj, ALU.mult).then_inc(s["proj_used"], 1)
                else:
                    tt(halves(ptmp), halves(mgg[q][:, g, :]), pj, ALU.mult).then_inc(s["proj_used"], 1)
                    v.drain()
                    tt(dst, dst, halves(ptmp), ALU.add)
                    v.drain()

            def attention_branches(o):
                v.wait_ge(s["gate_sig"], o + 1)
                for g in (1, 2):
                    v.wait_ge(s["proj_made"], 2 * o + g)
                    gated(o, o, g, 2 * (g - 1), g == 1)

            attention_branches(0)
            v.wait_ge(s["head_root"], 2)
            v.reciprocal(rn[0:HA, :], rn[0:HA, :]).then_inc(s["head_recip"], 1)
            attention_branches(1)
            for j in range(NJ):
                v.wait_ge(s["gn_mean"], NJ + j + 1)
                tt(halves(YT[:, j, :]), halves(YT[:, j, :]), psum[:, 4 + 2 * (j % 2):6 + 2 * (j % 2), 0:NH],
                   ALU.mult).then_inc(s["gn_bcast"], 1)
                v.drain()
                stt(YT[:, j, :], YT[:, j, :], pcol(PR_LG, j), BV[:, j, :], ALU.mult, ALU.add)
            v.drain()
            tt(YT, YT, gT, ALU.mult).then_inc(s["oa_ready"], 1)

            for o in range(2):
                v.wait_ge(s["proj_made"], 5 + o)
                gated(o, o, 0, 4 + 2 * o, False)
                v.sem_inc(s["merged"], 1)
            with v.Fori(1, KD // 2) as i:
                for q in range(2):
                    v.wait_ge(s["gate_sig"], i * 2 + q + 1)
                    for g in range(3):
                        step = q * 3 + g
                        v.wait_ge(s["proj_made"], i * 6 + step + 1)
                        gated(i * 2 + q, q, g, 4 + 2 * (step % 2), g == 0)
                    v.sem_inc(s["merged"], 1)

            v.wait_ge(s["xback_in"], 32)
            v.wait_ge(s["out_in"], 80)

            def residual(t, at):
                n = rows(t)
                v.wait_ge(s["h_made"], t + 1)
                stt(x1[0:n, t, :], x1[0:n, t, :], ALPHA, bank(2 * (t % 2), D)[0:n, :], ALU.mult, ALU.add).then_inc(s["h_used"], 1)
                v.drain()

            layer_norm(x1, 1, residual, 0)

            v.memset(LG, 0.0)
            v.drain()
            v.wait_ge(s["logits_made"], 1)
            lgp = bank(6, Q, NG + NE)
            tt(LG[:, 0:NT, :], lgp[:, 0:NT, :], bc(rb, 1, NT), ALU.add)
            tt(LG[0:B, NT, :], lgp[0:B, NT, :], rb[0:B, :], ALU.add)
            v.drain()
            iota = const("iota")

            def last1(ap, n):
                return ap.to_broadcast(list(ap.shape[:-1]) + [n])

            def first_max(vals, top, eq, cand, pos, onehot, n):
                v.tensor_reduce(top, vals, AX.X, ALU.max)
                v.drain()
                tt(eq, vals, last1(top, n), ALU.is_equal)
                v.drain()
                stt(cand, eq, -1000.0, bc(iota[:, 0:n], 1, Q), ALU.mult, ALU.add)
                v.drain()
                v.tensor_reduce(pos, cand, AX.X, ALU.min)
                v.drain()
                tt(onehot, cand, last1(pos, n), ALU.is_equal)
                v.drain()

            gl, er = LG[:, :, 0:NG], LG[:, :, NG:]
            first_max(gl, g1, eq4, c4, i1, oh4, NG)
            tt(t4, gl, last1(g1, NG), ALU.subtract).then_inc(s["exp_asked"], 1)
            ts(c4, oh4, 1.0, ALU.subtract, BIG, ALU.mult)
            tt(el.rearrange("p t (g e) -> p t g e", g=NG), er.rearrange("p t (g e) -> p t g e", g=NG), bc(oh4, 3, EPG), ALU.mult)
            v.drain()
            tt(el.rearrange("p t (g e) -> p t g e", g=NG), el.rearrange("p t (g e) -> p t g e", g=NG), bc(c4, 3, EPG), ALU.add)
            v.drain()
            first_max(el, v1, eqx, cx, i1, OH[:, 0, :, :], NE)
            stt(el, OH[:, 0, :, :], -2.0 * BIG, el, ALU.mult, ALU.add)
            v.drain()
            first_max(el, v2, eqx, cx, i1, OH[:, 1, :, :], NE)
            tt(e2, v2, v1, ALU.subtract).then_inc(s["exp_asked"], 1)
            tt(OH, OH, bc(last1(const("valid", Q, 1), NE), 1, 2), ALU.mult)
            v.drain()
            v.memset(earlier[:, 0, :], 0.0)
            tt(Osum, OH[:, 0, :, :], OH[:, 1, :, :], ALU.add)
            for t in range(Q):
                v.drain()
                last = tt(earlier[:, t + 1, :], earlier[:, t, :], Osum[:, t, :], ALU.add)
            last.then_inc(s["onehot_ready"], 1)
            v.wait_ge(s["exp_made"], 1)
            v.tensor_reduce(gd, t4, AX.X, ALU.add)
            v.wait_ge(s["exp_made"], 2)
            ts(rden2, e2, 1.0, ALU.add)
            v.drain()
            tt(gd, gd, rden2, ALU.mult)
            v.drain()
            v.reciprocal(pgate[:, 0, :, :], gd)
            v.drain()
            tt(pgate[:, 1, :, :], pgate[:, 0, :, :], e2, ALU.mult)
            v.memset(xg[0], 0.0)
            v.wait_ge(s["rank_made"], 1)
            v.tensor_copy(rank, bank(1, Q, NE))
            v.tensor_copy(cnt, bank(2, NE))
            v.drain()
            ts(qb, rank, float(P), ALU.is_ge)
            ts(nx, cnt, float(P), ALU.is_gt)
            v.drain()
            for q in range(2, 5):
                stt(qb, rank, float(P * q), qb, ALU.is_ge, ALU.add)
                stt(nx, cnt, float(P * q), nx, ALU.is_gt, ALU.add)
                v.drain()
            v.tensor_tensor_scan(incl, const("ones")[:, 0:NE], nx, 0.0, ALU.mult, ALU.add)
            stt(rank, qb, -float(P), rank, ALU.mult, ALU.add)
            ts(blk, qb, 0.0, ALU.is_gt)
            v.drain()
            tt(osx, incl, nx, ALU.subtract)
            v.drain()
            stt(dov, osx, float(NE - 1), iota[:, 0:NE], ALU.add, ALU.subtract)
            v.drain()
            tt(blk, blk, bc(dov, 1, Q), ALU.mult)
            v.drain()
            tt(blk, blk, qb, ALU.add)
            v.drain()
            tt(blk, blk, bc(iota[:, 0:NE], 1, Q), ALU.add)
            v.drain()
            for k in range(2):
                tt(el, OH[:, k, :, :], blk, ALU.mult)
                tt(cx, OH[:, k, :, :], rank, ALU.mult)
                v.drain()
                v.tensor_reduce(bk[:, k, :, :], el, AX.X, ALU.add)
                v.tensor_reduce(sk[:, k, :, :], cx, AX.X, ALU.add)
                v.drain()
            asg = const("asg1", Q, 2)
            for k in range(2):
                tt(SK[:, k, :, :], bc(iota, 1, Q), last1(sk[:, k, :, :], P), ALU.is_equal)
                tt(VB[:, :, k, 1, :], bc(iota[:, 0:NB], 1, Q), last1(bk[:, k, :, :], NB), ALU.is_equal)
            v.drain()
            for k in range(2):
                tt(VB[:, :, k, 0, :], VB[:, :, k, 1, :], last1(asg[:, :, k:k + 1], NB), ALU.mult)
            v.drain()
            for k in range(2):
                tt(VB[:, :, k, 1, :], VB[:, :, k, 1, :], last1(const("tok1", Q, 1), NB), ALU.mult)
            v.drain()
            v.sem_inc(s["route_ready"], 1)
            tt(xe, bc(iota[:, 0:XB], 2, NE), bc(osx, 1, XB), ALU.is_ge)
            tt(xe2, bc(iota[:, 0:XB], 2, NE), bc(incl, 1, XB), ALU.is_lt)
            v.drain()
            tt(xe, xe, xe2, ALU.mult)
            v.drain()
            tt(xe, xe, bc(iota[:, 0:NE], 1, XB), ALU.mult)
            v.drain()
            v.tensor_reduce(ovf[:, 0:XB], xe, AX.X, ALU.add)
            v.tensor_copy(ovf[:, XB:XB + 1], incl[:, NE - 1:NE])
            v.drain()
            v.tensor_copy(ovfi.bitcast(I32), ovf)
            v.memset(xg[1], 0.0)
            v.wait_ge(s["table_made"], 1)
            ts(tadd, bank(3, 2, NB), 0.0, ALU.is_equal, PAD_ROW, ALU.mult)
            v.drain()
            stt(tabf, bank(3, 2, NB), -1.0, tadd, ALU.add, ALU.add)
            v.drain()
            v.tensor_copy(tab[:, :, 0:NB], tabf)
            v.tensor_copy(tab[:, :, NB:NB + 1], tabf[:, :, 0:1])
            v.drain()
            v.tensor_copy(ix[:, 0, :], tab[:, 1, 0:1]).then_inc(s["gidx_ready"], 1)
            v.tensor_copy(ix[:, 1, :], tab[:, 1, 1:2]).then_inc(s["gidx_ready"], 1)
            v.sem_inc(s["table_ready"], 1)

            v.wait_ge(s["x1_spilled"], 16 * Q)
            v.wait_ge(s["x1T_ready"], Q)
            ts(x1[:, 0:NT, :], x1[:, 0:NT, :], ALPHA, ALU.mult)
            ts(x1[0:B, NT, :], x1[0:B, NT, :], ALPHA, ALU.mult)
            v.sem_inc(s["yb_ready"], 1)
            def silu_step(e):
                v.wait_ge(s["gate_act"], e + 1)
                tt(esig, esig, bank(2, FF), ALU.mult)

            def h_step(e):
                v.drain()
                v.wait_ge(s["up_mm"], e + 3)
                tt(hb, esig, bank(3, FF), ALU.mult).then_inc(s["h_ready"], 1)

            def row_index_step(e, q):
                v.tensor_copy(ix[:, q, :], tab[:, 1, bass.ds(e, 1)]).then_inc(s["gidx_ready"], 1)

            def hT_step(e):
                v.wait_ge(s["hT_turned"], e + 1)
                v.tensor_copy(hT, bank(4, 4, P)).then_inc(s["hT_ready"], 1)

            def y_step(e, q, n):
                v.wait_ge(s["y_mm"], e + 3)
                v.wait_ge(s[f"scat_{'ab'[q]}"], n * 16 + 16)
                v.tensor_copy(ix[:, 2 + q, :], tab[:, 0, bass.ds(e, 1)])
                v.tensor_copy(yb[q], bank(5, D)).then_inc(s["yb_ready"], 1)

            silu_step(0)
            h_step(0)
            row_index_step(2, 0)
            with v.Fori(0, NE // 2 - 1) as i:
                for q in range(2):
                    e = i * 2 + q + 1
                    silu_step(e)
                    hT_step(i * 2 + q)
                    h_step(e)
                    row_index_step(i * 2 + q + 3, 1 - q)
                    y_step(i * 2 + q, q, i)
            silu_step(NE - 1)
            hT_step(NE - 2)
            h_step(NE - 1)
            y_step(NE - 2, 0, NE // 2 - 1)
            hT_step(NE - 1)
            y_step(NE - 1, 1, NE // 2 - 1)

            def extra_vec(i):
                silu_step(i + NE)
                h_step(i + NE)
                row_index_step(i + NE + 1, 0)
                hT_step(i + NE)
                y_step(i + NE, 0, i + NE // 2)

            extra_blocks(v, extra_vec)


            def expert_sum(t, at):
                n = rows(t)
                xt = x1[0:n, t, :]
                if at == 0:
                    v.wait_ge(s["ln2_in"], 32)
                v.wait_ge(s[f"tile{t}_in"], 32)
                for k in range(2):
                    stt(xt, yk[0:n, t, k, :], pgate[0:n, k, t, :], xt, ALU.mult, ALU.add)
                    v.drain()

            layer_norm(x1, 2, expert_sum, 1)

        @block.gpsimd
        def _(g):
            ix = idx.bitcast(U32)

            def offset(x, pas):
                for t in range(Q):
                    i, n = tile_at(pas, t), rows(tile_at(pas, t))
                    g.wait_ge(s["ln_gained"], pas * Q + t + 1)
                    g.tensor_tensor(x[0:n, i, :], x[0:n, i, :], gb[0:n, 1, :], ALU.add).then_inc(s["x_normed"], 1)

            offset(xtok, 0)
            g.wait_ge(s["kT_ready"], 1)
            g.wait_ge(s["v_ready"], 1)
            g.wait_ge(s["consts_in"], 16)
            g.wait_ge(s["mkv_made"], 2)
            g.wait_ge(s["spilled"], 16 * Q)
            g.tensor_copy(mst, const("mask0"))
            g.tensor_copy(kst, kT[:, 0:2 * P])
            g.drain()
            g.sem_inc(s["blk_kv"], 1)

            def block_keys(i, ahead):
                g.wait_ge(s["blk_out"], i + 1)
                g.sem_inc(s["pace"], 1)
                g.tensor_copy(vst, vtok[:, bass.ds(i, 2), :])
                g.drain()
                g.sem_inc(s["blk_kv"], 1)
                if ahead:
                    g.wait_ge(s["blk_max"], i + 1)
                    g.sem_inc(s["pace"], 1)
                    g.tensor_copy(mst, const("mask"))
                    g.tensor_copy(kst, kT[:, bass.ds(i * P + P, 2 * P)])
                    g.drain()
                    g.sem_inc(s["blk_kv"], 1)

            with g.Fori(0, NT - 1) as i:
                block_keys(i, True)
            block_keys(NT - 1, False)

            offset(x1, 1)
            g.wait_ge(s["table_ready"], 1)
            g.wait_ge(s["x1_spilled"], 16 * Q)
            def gather(e, q):
                g.wait_ge(s["gidx_ready"], e + 1)
                g.sem_inc(s["pace"], 1)
                g.indirect_dma_start(xg[q], None, X["x1"], bass.IndirectOffsetOnAxis(ap=ix[:, q, :], axis=0),
                                     bounds_check=N - 1, oob_is_err=False).then_inc(s[f"xg_in_{'ab'[q]}"], 16)

            def scatter(e, q):
                g.wait_ge(s["yb_ready"], e + 2)
                g.sem_inc(s["pace"], 1)
                g.indirect_dma_start(X["ya"], bass.IndirectOffsetOnAxis(ap=ix[:, 2 + q, :], axis=0), yb[q], None,
                                     bounds_check=2 * N - 1, oob_is_err=False).then_inc(s[f"scat_{'ab'[q]}"], 16)

            g.dma_start(X["prime"][0:1, :], const("iota")[0:1, 0:16]).then_inc(s["scat_a"], 16)
            g.dma_start(X["prime"][1:2, :], const("iota")[0:1, 0:16]).then_inc(s["scat_b"], 16)
            gather(0, 0)
            gather(1, 1)
            gather(2, 0)
            with g.Fori(0, NE // 2 - 2) as i:
                for q in range(2):
                    gather(i * 2 + q + 3, 1 - q)
                    scatter(i * 2 + q, q)
            gather(NE - 1, 1)
            scatter(NE - 4, 0)
            scatter(NE - 3, 1)
            scatter(NE - 2, 0)
            scatter(NE - 1, 1)
            g.wait_ge(s["scat_a"], 16 * (NE // 2 + 1))
            g.wait_ge(s["scat_b"], 16 * (NE // 2 + 1))

            def extra_rows(i):
                gather(i + NE, 0)
                scatter(i + NE, 0)
                g.wait_ge(s["scat_a"], i * 16 + 16 * (NE // 2 + 2))
                g.sem_inc(s["pace"], 1)

            extra_blocks(g, extra_rows)
            g.sem_inc(s["ovf_step"], 1)
            offset(x1, 2)


OUTS = [("y_prompt", (T, D), (1, T, D)), ("y_sample", (B, D), (B, 1, D)),
        ("wkv_prompt", (HA, 64, 64), (1, 1, HA, 64, 64)), ("wkv_sample", (B * HA, 64, 64), (1, B, HA, 64, 64)),
        ("shift_prompt", (1, C_SHIFT), (1, 1, C_SHIFT)), ("shift_sample", (B, C_SHIFT), (1, B, C_SHIFT)),
        ("win_k_prompt", (P, P), (1, 1, P, 2, 64)), ("win_v_prompt", (P, P), (1, 1, P, 2, 64)),
        ("win_k_sample", (B, P, P), (1, B, P, 2, 64)), ("win_v_sample", (B, P, P), (1, B, P, 2, 64)),
        ("mem_k_prompt", (NMEM, 256), (1, 1, NMEM, 4, 64)), ("mem_v_prompt", (NMEM, 256), (1, 1, NMEM, 4, 64))]


def kernel(**a):
    import concourse.bacc as bacc
    from concourse.bass_utils import run_bass_kernel_spmd

    nc = bacc.Bacc("TRN2", target_bir_lowering=False, num_devices=1)
    arrays, I, O, X = {}, {}, {}, {}

    def give(name, x):
        x = np.ascontiguousarray(x)
        arrays["in_" + name] = x
        I[name] = nc.dram_tensor("in_" + name, x.shape, F32, kind="ExternalInput").ap()

    give("consts", CONST)
    give("x_prompt", np.reshape(a["x_prompt"], (T, D)))
    give("x_sample", np.reshape(a["x_sample"], (B, D)))
    give("mem_prompt", np.reshape(a["mem_prompt"], (NMEM, D)))
    give("state_wkv", np.reshape(a["state_wkv"], (B * HA, 64, 64)))
    give("state_shift", np.reshape(a["state_shift"], (B, C_SHIFT)))
    for n in ("cache_win_k", "cache_win_v"):
        give(n, np.reshape(a[n], (B, WIN, P)))
    for n in ("cache_mem_k", "cache_mem_v"):
        give(n, np.reshape(a[n], (B, NMEM, 256)))
    for n in ("ln_in_g", "ln_in_b"):
        give(n, a[n])
    for n in ("ln1_g", "ln1_b", "ln2_g", "ln2_b", "w_in", "w_up", "a_up", "g_up", "w_mem_kv", "p_a", "p_b", "p_m", "w_o",
              "e_gate", "e_up", "e_down"):
        give(n, a[n][0])
    vecs = ("mu", "w0", "a0", "k_k", "k_a", "r_k", "lnx_g", "lnx_b")
    give("params", np.concatenate([np.reshape(a[n], (-1, P)) for n in vecs]))
    give("sinks_bc", np.tile(np.reshape(a["sinks"], (1, HA)), (P, 1)))
    give("sinks_row", np.reshape(np.tile(np.reshape(a["sinks"], (2, 1, 4)), (1, B, 1)), (64, 1)))
    give("router_b", np.tile(np.concatenate([a["b_group"], a["b_router"]], 1), (P, 1)))
    give("router_w", np.concatenate([a["w_group"][0], a["w_router"][0]], 1))
    for n, shape in (("x0", (N, D)), ("x1", (N, D)), ("ya", (2 * N, D)), ("gates", (N_GATE, P, N)), ("sv", (6, B, C_A)), ("sy", (B * HA, 64)), ("prime", (2, 16))):
        X[n] = nc.dram_tensor("scratch_" + n, shape, F32).ap()
    for n, shape, _ in OUTS:
        O[n] = nc.dram_tensor("out_" + n, shape, F32, kind="ExternalOutput").ap()
    build(nc, I, O, X)
    got = run_bass_kernel_spmd(nc, [arrays], core_ids=[0]).results[0]
    return tuple(np.reshape(got["out_" + n], shape) for n, _, shape in OUTS)
```
